# Optimizing a Trainium2 kernel written in Bass

```python
import math
import jax, jax.numpy as jnp
from jax import lax
import numpy as np

D_MODEL = 1024
BATCH = 1
SEQ = 1024
DEPTH = 1

SB_HEADS = 8
SB_HEAD_DIM = 64
SB_WIDTH = SB_HEADS * SB_HEAD_DIM
POOL_WINDOWS = (2, 4, 8, 16)
N_POOL_GROUPS = len(POOL_WINDOWS)
POOL_WIDTH = D_MODEL // 2
POOL_GROUP_DIM = POOL_WIDTH // N_POOL_GROUPS
MIX_WIDTH = SB_WIDTH + POOL_WIDTH
IN_PROJ_WIDTH = 3 * SB_WIDTH + POOL_WIDTH
Q_BLOCK = 128
N_EXPERTS = 32
TOP_K = 4
D_EXPERT = D_MODEL
SWIGLU_LIMIT = 7.0
SWIGLU_ALPHA = 1.702
EXPERT_BLOCK = 128
RMS_EPS = 1e-5

kernel_name = "hybrid_stickbreak_pool_moe"

def rms_norm(x, g):
    xf = x.astype(jnp.float32)
    y = xf * lax.rsqrt(jnp.mean(xf * xf, axis=-1, keepdims=True) + RMS_EPS)
    return (y * g.astype(jnp.float32)).astype(x.dtype)

def stick_breaking_attention(q, k, v):
    B, H, S, Dh = q.shape
    n_blocks = S // Q_BLOCK
    scale = 1.0 / math.sqrt(Dh)
    q_blocks = q.reshape(B, H, n_blocks, Q_BLOCK, Dh).transpose(2, 0, 1, 3, 4)
    kf = k.astype(jnp.float32)
    vf = v.astype(jnp.float32)
    key_pos = jnp.arange(S, dtype=jnp.int32)

    def one_block(args):
        qi, bi = args
        z = jnp.einsum('bhqd,bhkd->bhqk', qi.astype(jnp.float32), kf) * scale
        q_pos = bi * Q_BLOCK + jnp.arange(Q_BLOCK, dtype=jnp.int32)
        causal = key_pos[None, :] < q_pos[:, None]
        log_1m_beta = jnp.where(causal, jax.nn.log_sigmoid(-z), 0.0)
        shifted = jnp.pad(log_1m_beta[..., 1:], ((0, 0), (0, 0), (0, 0), (0, 1)))
        tail = lax.cumsum(shifted, axis=3, reverse=True)
        weights = jnp.where(causal, jnp.exp(jax.nn.log_sigmoid(z) + tail), 0.0)
        return jnp.einsum('bhqk,bhkd->bhqd', weights, vf)

    out = lax.map(one_block, (q_blocks, jnp.arange(n_blocks, dtype=jnp.int32)))
    out = out.transpose(1, 0, 3, 2, 4).reshape(B, S, H * Dh)
    return out.astype(q.dtype)

def multiscale_pool(u, pool_w, pool_scale):
    B, S, C = u.shape
    uf = u.astype(jnp.float32)
    csum = jnp.pad(jnp.cumsum(uf, axis=1), ((0, 0), (1, 0), (0, 0)))
    t = jnp.arange(S, dtype=jnp.int32)
    groups = []
    for g, w in enumerate(POOL_WINDOWS):
        sl = slice(g * POOL_GROUP_DIM, (g + 1) * POOL_GROUP_DIM)
        start = jnp.maximum(t + 1 - w, 0)
        count = (t + 1 - start).astype(jnp.float32)
        window_sum = csum[:, 1:, sl] - csum[:, start, sl]
        groups.append(window_sum / count[None, :, None] - uf[:, :, sl])
    pooled = jnp.stack(groups, axis=2)
    mixed = jnp.einsum('bsgc,gcd->bsgd', pooled, pool_w.astype(jnp.float32))
    out = mixed.reshape(B, S, C) * pool_scale.astype(jnp.float32)
    return out.astype(u.dtype)

def moe_ffn(h, w_router, b_router, w_gate_up, b_gate_up, w_down, b_down):
    B, S, D = h.shape
    T = B * S
    hf = h.reshape(T, D)
    logits = hf.astype(jnp.float32) @ w_router.astype(jnp.float32) + b_router.astype(jnp.float32)
    top_vals, top_idx = lax.top_k(logits, TOP_K)
    gates = jax.nn.softmax(top_vals, axis=-1).astype(h.dtype)

    TK = T * TOP_K
    expert_flat = top_idx.reshape(TK).astype(jnp.int32)
    token_flat = jnp.arange(TK, dtype=jnp.int32) // TOP_K
    gate_flat = gates.reshape(TK)
    order = jnp.argsort(expert_flat, stable=True)
    sorted_expert = expert_flat[order]
    counts = jnp.bincount(expert_flat, length=N_EXPERTS).astype(jnp.int32)
    offsets = jnp.cumsum(counts) - counts
    padded_counts = ((counts + EXPERT_BLOCK - 1) // EXPERT_BLOCK) * EXPERT_BLOCK
    padded_end = jnp.cumsum(padded_counts)
    padded_start = padded_end - padded_counts
    dest = padded_start[sorted_expert] + jnp.arange(TK, dtype=jnp.int32) - offsets[sorted_expert]

    n_blocks = -(-(TK + N_EXPERTS * (EXPERT_BLOCK - 1)) // EXPERT_BLOCK)
    n_pad = n_blocks * EXPERT_BLOCK
    row_token = jnp.zeros((n_pad,), jnp.int32).at[dest].set(token_flat[order])
    row_gate = jnp.zeros((n_pad,), h.dtype).at[dest].set(gate_flat[order])
    x_disp = hf[row_token].reshape(n_blocks, EXPERT_BLOCK, D)
    block_start = jnp.arange(n_blocks, dtype=jnp.int32) * EXPERT_BLOCK
    block_expert = jnp.minimum(
        jnp.sum(block_start[:, None] >= padded_end[None, :], axis=1), N_EXPERTS - 1
    ).astype(jnp.int32)

    def expert_block(args):
        xb, e = args
        gu = xb @ w_gate_up[e] + b_gate_up[e]
        gate = jnp.minimum(gu[:, :D_EXPERT], SWIGLU_LIMIT)
        up = jnp.clip(gu[:, D_EXPERT:], -SWIGLU_LIMIT, SWIGLU_LIMIT)
        act = gate * jax.nn.sigmoid(SWIGLU_ALPHA * gate) * (up + 1.0)
        return act @ w_down[e] + b_down[e]

    y = lax.map(expert_block, (x_disp, block_expert)).reshape(n_pad, D)
    out = jax.ops.segment_sum(y * row_gate[:, None], row_token, num_segments=T)
    return out.reshape(B, S, D).astype(h.dtype)

def setup_inputs(seed: int = 0) -> dict:
    key = jax.random.key(seed)
    ks = jax.random.split(key, 16)
    f32 = jnp.float32
    L = DEPTH
    x = jax.random.normal(ks[0], (BATCH, SEQ, D_MODEL), f32)
    g_mix = 1.0 + 0.05 * jax.random.normal(ks[1], (L, D_MODEL), f32)
    w_in = jax.random.normal(ks[2], (L, D_MODEL, IN_PROJ_WIDTH), f32) * D_MODEL ** -0.5
    pool_w = jax.random.normal(ks[3], (L, N_POOL_GROUPS, POOL_GROUP_DIM, POOL_GROUP_DIM), f32) * POOL_GROUP_DIM ** -0.5
    pool_scale = 1.0 + 0.1 * jax.random.normal(ks[4], (L, POOL_WIDTH), f32)
    w_out = jax.random.normal(ks[5], (L, MIX_WIDTH, D_MODEL), f32) * MIX_WIDTH ** -0.5
    g_moe = 1.0 + 0.05 * jax.random.normal(ks[6], (L, D_MODEL), f32)
    w_router = jax.random.normal(ks[7], (L, D_MODEL, N_EXPERTS), f32) * D_MODEL ** -0.5
    b_router = 0.01 * jax.random.normal(ks[8], (L, N_EXPERTS), f32)
    w_gate_up = jax.random.normal(ks[9], (L, N_EXPERTS, D_MODEL, 2 * D_EXPERT), f32) * D_MODEL ** -0.5
    b_gate_up = 0.02 * jax.random.normal(ks[10], (L, N_EXPERTS, 2 * D_EXPERT), f32)
    w_down = jax.random.normal(ks[11], (L, N_EXPERTS, D_EXPERT, D_MODEL), f32) * D_EXPERT ** -0.5
    b_down = 0.02 * jax.random.normal(ks[12], (L, N_EXPERTS, D_MODEL), f32)
    g_final = 1.0 + 0.05 * jax.random.normal(ks[13], (D_MODEL,), f32)
    return {"x": x, "g_mix": g_mix, "w_in": w_in, "pool_w": pool_w,
            "pool_scale": pool_scale, "w_out": w_out, "g_moe": g_moe,
            "w_router": w_router, "b_router": b_router, "w_gate_up": w_gate_up,
            "b_gate_up": b_gate_up, "w_down": w_down, "b_down": b_down,
            "g_final": g_final}

def reference(x, g_mix, w_in, pool_w, pool_scale, w_out, g_moe, w_router,
              b_router, w_gate_up, b_gate_up, w_down, b_down, g_final):
    B, S, D = x.shape
    for l in range(DEPTH):
        h = rms_norm(x, g_mix[l])
        proj = h @ w_in[l]
        q = proj[..., 0:SB_WIDTH]
        k = proj[..., SB_WIDTH:2 * SB_WIDTH]
        v = proj[..., 2 * SB_WIDTH:3 * SB_WIDTH]
        u = proj[..., 3 * SB_WIDTH:]
        to_heads = lambda t: t.reshape(B, S, SB_HEADS, SB_HEAD_DIM).transpose(0, 2, 1, 3)
        attn_out = stick_breaking_attention(to_heads(q), to_heads(k), to_heads(v))
        pool_out = multiscale_pool(u, pool_w[l], pool_scale[l])
        mixed = jnp.concatenate([attn_out, pool_out], axis=-1)
        x = x + mixed @ w_out[l]
        x = x + moe_ffn(rms_norm(x, g_moe[l]), w_router[l], b_router[l],
                        w_gate_up[l], b_gate_up[l], w_down[l], b_down[l])
    return rms_norm(x, g_final)


_drawn_inputs = setup_inputs


def setup_inputs(seed=0):
    import zlib

    import numpy as np

    out = dict(_drawn_inputs(seed))
    spreads = {}
    factors = {'b_gate_up': 6.202, 'b_down': 7.109}
    for name, (base, spread) in spreads.items():
        noise = np.random.default_rng([zlib.crc32(name.encode()), seed]).standard_normal(out[name].shape)
        drawn = base * np.exp(spread * noise) if base else spread * noise
        out[name] = __import__('jax').numpy.asarray(drawn.astype(out[name].dtype))
    for name, factor in factors.items():
        out[name] = (out[name] * factor).astype(out[name].dtype)
    return out
```

```python
from contextlib import ExitStack

import concourse.bass as bass
from concourse import mybir

F32 = mybir.dt.float32
F32R = mybir.dt.float32r
BF16 = mybir.dt.bfloat16
I32 = mybir.dt.int32
U32 = mybir.dt.uint32
ALU = mybir.AluOpType
ACT = mybir.ActivationFunctionType
AX = mybir.AxisListType

P = 128
D = 1024
T = 1024
KO = D // P
TT = T // P
HALF = 512
HEADS, HD = 8, 64
PAIRS = HEADS // 2
QKV = HEADS * HD
WINDOWS = (2, 4, 8, 16)
PAD = max(WINDOWS)
EPS = 1e-5
E_, K_ = 32, 4
LIMIT, ALPHA = 7.0, 1.702

SLOTS = 160
SEG = (128, SLOTS - 128)
MAX_BLOCKS_PER_EXPERT = -(-T // SLOTS)
MAX_BLOCKS = E_ + T * K_ // SLOTS
TABLE = 64
assert MAX_BLOCKS + 1 < TABLE

CC = 256
MC = CC // P
PAIR_CHUNKS = D // CC
CHUNKS = 3 * PAIR_CHUNKS
RAW = 6
SPLIT = 3
BANKS = 4
XG = (3, 3, 2)


def hybrid_moe_kernel(nc, x, g_mix, w_in, pool_w, pool_scale, w_out, g_moe, w_router, b_router,
                      w_gate_up, b_gate_up, w_down, b_down, g_final, out):
    h_rows = nc.dram_tensor("h_rows", [T, D], F32, kind="Internal").ap()
    x2_rows = nc.dram_tensor("x2_rows", [T, D], F32, kind="Internal").ap()
    y_rows = nc.dram_tensor("y_rows", [T * K_ + SLOTS, D], F32, kind="Internal").ap()
    x_tiles = x.rearrange("a (t p) d -> p (a t) d", p=P)
    out_tiles = out.rearrange("a (t p) d -> p (a t) d", p=P)

    with ExitStack() as keep:
        sb = lambda n, s, d=F32: keep.enter_context(nc.sbuf_tensor(n, s, d))
        k = {}
        k["ident"] = sb("ident", [P, P])
        k["bias_gu"] = sb("bias_gu", [P, 2 * D // P, E_])
        k["bias_dn"] = sb("bias_dn", [P, D // P, E_])
        k["ranks"] = sb("ranks", [P, TT, E_])
        k["gates"] = sb("gates", [P, TT, K_])
        k["dest"] = sb("dest", [P, TT, K_], I32)
        k["block_expert"] = sb("block_expert", [P, TABLE], I32)
        k["block_first"] = sb("block_first", [P, TABLE])
        k["block_row"] = sb("block_row", [P, TABLE], I32)
        k["last_block"] = sb("last_block", [P, 1], I32)
        k["token_of"] = sb("token_of", [P, TT, 2], BF16)
        with ExitStack() as mix:
            mixedT = mix.enter_context(nc.sbuf_tensor("mixedT", [P, KO, T], F32))
            w_out_sb = mix.enter_context(nc.sbuf_tensor("w_out_sb", [P, KO, D], F32))
            with ExitStack() as at:
                hT = at.enter_context(nc.sbuf_tensor("hT", [P, KO, T], F32))
                v_all = at.enter_context(nc.sbuf_tensor("v_all", [P, TT, QKV], F32))
                project(nc, k, x_tiles, g_mix, w_in, pool_w, pool_scale, b_gate_up, b_down, hT, v_all, mixedT)
                attend(nc, k, w_in, w_out, hT, v_all, mixedT, w_out_sb)
            route(nc, k, x_tiles, g_moe, w_router, b_router, mixedT, w_out_sb, h_rows, x2_rows)
        experts(nc, k, w_gate_up, w_down, h_rows, y_rows)
        combine(nc, k, g_final, x2_rows, y_rows, out_tiles)


def project(nc, k, x_tiles, g_mix, w_in, pool_w, pool_scale, b_gate_up, b_down, hT, v_all, mixedT):
    with ExitStack() as c:
        sb = lambda n, s, d=F32: c.enter_context(nc.sbuf_tensor(n, s, d))
        ps = lambda n, s: c.enter_context(nc.psum_tensor(n, s, F32))
        sem = lambda n: c.enter_context(nc.semaphore(n))
        X = sb("X", [P, TT, D])
        square = sb("square", [P, D])
        mean_sq, rms, rstd = sb("mean_sq", [P, TT]), sb("rms", [P, TT]), sb("rstd", [P, TT])
        g_col = sb("g_col", [P, KO])
        scale_col = sb("scale_col", [P, len(WINDOWS)])
        w_v, w_u = sb("w_v", [P, KO, QKV]), sb("w_u", [P, KO, P])
        pw = sb("pw", [P, len(WINDOWS), P])
        bias_rows = sb("bias_rows", [E_, 3 * D])
        u = sb("u", [P, PAD + T])
        sums = [sb("sums0", [P, PAD + T]), sb("sums1", [P, PAD + T])]
        count, inv = sb("count", [P, PAD]), sb("inv", [P, len(WINDOWS), PAD])
        iota1 = sb("iota1", [P, PAD])
        pooled = sb("pooled", [P, T])
        bank = [ps(f"pj{i}", [P, HALF]) for i in range(8)]
        x_in, cols_in, wv_in, wu_in, pw_in, b_in = (sem(n) for n in ("x_in", "cols_in", "wv_in", "wu_in", "pw_in", "b_in"))
        ident_ok, iota_ok, pad_ok = sem("ident_ok"), sem("iota_ok"), sem("pad_ok")
        sq_done, mean_ok, rms_ok, rstd_ok, x_scaled = (sem(n) for n in ("sq_done", "mean_ok", "rms_ok", "rstd_ok", "x_scaled"))
        pe_bank, bank_read = sem("pe_bank"), sem("bank_read")
        inv_ok, sum_ok, pooled_ok = sem("inv_ok"), sem("sum_ok"), sem("pooled_ok")

        uses = [("hT", n) for n in range(2 * KO)] + [("bias", 0), ("bias", 1)] + [("v", t) for t in range(TT)]
        for g in range(len(WINDOWS)):
            uses += [("u", 2 * g), ("u", 2 * g + 1)]
            if g:
                uses += [("mix", 2 * g - 2), ("mix", 2 * g - 1)]
        uses += [("mix", 2 * len(WINDOWS) - 2), ("mix", 2 * len(WINDOWS) - 1)]
        at = {use: n for n, use in enumerate(uses)}

        with nc.Block() as block:

            @block.sync
            def _(sp):
                for t in range(TT):
                    sp.dma_start(X[:, t, :], x_tiles[:, t, :]).then_inc(x_in, 16)
                with nc.allow_non_contiguous_dma(reason="columns of a small vector"):
                    sp.dma_start(g_col[:], g_mix.rearrange("a (k p) -> p (a k)", p=P)).then_inc(cols_in, 16)
                    sp.dma_start(scale_col[:], pool_scale.rearrange("a (k p) -> p (a k)", p=P)).then_inc(cols_in, 16)
                sp.dma_start(w_v[:], w_in[0, :, 2 * QKV:3 * QKV].rearrange("(k p) n -> p k n", p=P)).then_inc(wv_in, 16)
                sp.dma_start(pw[:], pool_w[0].rearrange("g c d -> c g d")).then_inc(pw_in, 16)
                sp.dma_start(bias_rows[:, 0:2 * D], b_gate_up[0]).then_inc(b_in, 16)
                sp.dma_start(bias_rows[:, 2 * D:3 * D], b_down[0]).then_inc(b_in, 16)
                for g in range(len(WINDOWS)):
                    if g:
                        sp.wait_ge(pe_bank, at[("u", 2 * g - 1)] + 1)
                    sp.dma_start(w_u[:], w_in[0, :, 3 * QKV + g * P:3 * QKV + (g + 1) * P]
                                 .rearrange("(k p) n -> p k n", p=P)).then_inc(wu_in, 16)

            @block.gpsimd
            def _(pool):
                nc.gpsimd.memset(k["ident"][:], 0.0).then_inc(ident_ok, 1)
                pool.wait_ge(ident_ok, 1)
                nc.gpsimd.affine_select(out=k["ident"][:], in_=k["ident"][:], compare_op=ALU.not_equal, fill=1.0,
                                        base=0, pattern=[[-1, P]], channel_multiplier=1).then_inc(ident_ok, 1)
                nc.gpsimd.iota(iota1[:], [[1, PAD]], base=1, channel_multiplier=0,
                               allow_small_or_imprecise_dtypes=True).then_inc(iota_ok, 1)
                for buf in (u, *sums):
                    last = nc.gpsimd.memset(buf[:, 0:PAD], 0.0)
                last.then_inc(pad_ok, 1)

            @block.scalar
            def _(act):
                for t in range(TT):
                    act.wait_ge(x_in, 16 * TT)
                    if t:
                        act.wait_ge(sq_done, t)
                    nc.scalar.activation(square[:], X[:, t, :], ACT.Square, scale=D ** -0.5,
                                         accum_out=mean_sq[:, t:t + 1]).then_inc(sq_done, 1)
                act.wait_ge(mean_ok, 1)
                nc.scalar.activation(rms[:], mean_sq[:], ACT.Sqrt).then_inc(rms_ok, 1)
                act.wait_ge(cols_in, 32)
                for n, (kind, i) in enumerate(uses):
                    act.wait_ge(pe_bank, n + 1)
                    src = bank[n % 8]
                    if kind == "hT":
                        half, ko = divmod(i, KO)
                        ins = nc.scalar.activation(hT[:, ko, half * HALF:(half + 1) * HALF], src[:], ACT.Copy,
                                                   scale=g_col[:, ko:ko + 1])
                    elif kind == "bias":
                        if i == 0:
                            ins = nc.scalar.activation(k["bias_gu"][:].rearrange("p m e -> p (m e)"), src[:], ACT.Copy)
                        else:
                            ins = nc.scalar.activation(k["bias_dn"][:].rearrange("p m e -> p (m e)"),
                                                       src[:, 0:E_ * D // P], ACT.Copy)
                    elif kind == "v":
                        ins = nc.scalar.activation(v_all[:, i, :], src[:], ACT.Copy)
                    elif kind == "u":
                        g, half = divmod(i, 2)
                        if half == 0:
                            if g == 0:
                                act.wait_ge(pad_ok, 1)
                            else:
                                act.wait_ge(pooled_ok, g)
                        ins = nc.scalar.activation(u[:, PAD + half * HALF:PAD + (half + 1) * HALF], src[:], ACT.Copy)
                    else:
                        g, half = divmod(i, 2)
                        ins = nc.scalar.activation(mixedT[:, KO // 2 + g, half * HALF:(half + 1) * HALF], src[:],
                                                   ACT.Copy, scale=scale_col[:, g:g + 1])
                    ins.then_inc(bank_read, 1)

            @block.vector
            def _(dve):
                dve.wait_ge(sq_done, TT)
                nc.vector.tensor_scalar(mean_sq[:], mean_sq[:], EPS, None, ALU.add).then_inc(mean_ok, 1)
                dve.wait_ge(rms_ok, 1)
                nc.vector.reciprocal(rstd[:], rms[:]).then_inc(rstd_ok, 1)
                dve.wait_ge(rstd_ok, 1)
                for t in range(TT):
                    nc.vector.tensor_scalar(X[:, t, :], X[:, t, :], rstd[:, t:t + 1], None, ALU.mult).then_inc(x_scaled, 1)
                dve.wait_ge(iota_ok, 1)
                for g, w in enumerate(WINDOWS):
                    if g:
                        dve.wait_ge(inv_ok, 2 * g)
                    nc.vector.tensor_scalar(count[:], iota1[:], float(w), None, ALU.min).then_inc(inv_ok, 1)
                    dve.wait_ge(inv_ok, 2 * g + 1)
                    nc.vector.reciprocal(inv[:, g, :], count[:]).then_inc(inv_ok, 1)
                dve.wait_ge(inv_ok, 2 * len(WINDOWS))
                dve.wait_ge(pad_ok, 1)
                done = 0
                for g, w in enumerate(WINDOWS):
                    dve.wait_ge(bank_read, at[("u", 2 * g + 1)] + 1)
                    src = u
                    for s in range(g + 1):
                        dst = sums[s % 2]
                        nc.vector.tensor_tensor(dst[:, PAD:], src[:, PAD:], src[:, PAD - 2 ** s:PAD + T - 2 ** s],
                                                ALU.add).then_inc(sum_ok, 1)
                        done += 1
                        dve.wait_ge(sum_ok, done)
                        src = dst
                    if g:
                        dve.wait_ge(pe_bank, at[("mix", 2 * g - 1)] + 1)
                    nc.vector.scalar_tensor_tensor(pooled[:], src[:, PAD:], 1.0 / w, u[:, PAD:], ALU.mult,
                                                   ALU.subtract).then_inc(sum_ok, 1)
                    dve.wait_ge(sum_ok, done + 1)
                    nc.vector.tensor_tensor(src[:, PAD:2 * PAD], src[:, PAD:2 * PAD], inv[:, g, :], ALU.mult).then_inc(sum_ok, 1)
                    done += 2
                    dve.wait_ge(sum_ok, done)
                    nc.vector.tensor_tensor(pooled[:, 0:PAD], src[:, PAD:2 * PAD], u[:, PAD:2 * PAD],
                                            ALU.subtract).then_inc(pooled_ok, 1)
                    dve.wait_ge(pooled_ok, g + 1)

            @block.tensor
            def _(pe):
                pe.wait_ge(ident_ok, 2)
                for n, (kind, i) in enumerate(uses):
                    dst = bank[n % 8]
                    if n >= 8:
                        pe.wait_ge(bank_read, n - 7)
                    if kind == "hT":
                        half, ko = divmod(i, KO)
                        pe.wait_ge(x_scaled, 4 * (half + 1))
                        for t in range(4):
                            ins = nc.tensor.transpose(dst[:, t * P:(t + 1) * P],
                                                      X[:, 4 * half + t, ko * P:(ko + 1) * P], k["ident"][:])
                    elif kind == "bias":
                        pe.wait_ge(b_in, 32)
                        for m in range(16 if i == 0 else 8):
                            ins = nc.tensor.transpose(dst[:, m * E_:(m + 1) * E_],
                                                      bias_rows[:, (16 * i + m) * P:(16 * i + m + 1) * P],
                                                      k["ident"][0:E_, 0:E_])
                    elif kind == "v":
                        if i == 0:
                            pe.wait_ge(wv_in, 16)
                            pe.wait_ge(bank_read, 2 * KO)
                        for ko in range(KO):
                            ins = nc.tensor.matmul(dst[:], hT[:, ko, i * P:(i + 1) * P], w_v[:, ko, :],
                                                   start=ko == 0, stop=ko == KO - 1)
                    elif kind == "u":
                        g, half = divmod(i, 2)
                        pe.wait_ge(wu_in, 16 * (g + 1))
                        for ko in range(KO):
                            ins = nc.tensor.matmul(dst[:], w_u[:, ko, :], hT[:, ko, half * HALF:(half + 1) * HALF],
                                                   start=ko == 0, stop=ko == KO - 1)
                    else:
                        g, half = divmod(i, 2)
                        pe.wait_ge(pw_in, 16)
                        pe.wait_ge(pooled_ok, g + 1)
                        ins = nc.tensor.matmul(dst[:], pw[:, g, :], pooled[:, half * HALF:(half + 1) * HALF],
                                               start=True, stop=True)
                    ins.then_inc(pe_bank, 1)


def attend(nc, k, w_in, w_out, hT, v_all, mixedT, w_out_sb):
    UNITS = 2 * TT
    USES = 2 + UNITS
    groups = [(u, g) for u in range(UNITS) for g in range((u // 2) // 4 + 1)]
    first_group = {u: next(n for n, (v, _) in enumerate(groups) if v == u) for u in range(UNITS)}
    n_groups = {u: (u // 2) // 4 + 1 for u in range(UNITS)}
    G = len(groups)
    WT = 4
    TP_AHEAD = 3
    assert USES % 2 == 0 and G % WT == 0 and UNITS % 2 == 0
    with ExitStack() as c:
        sb = lambda n, s, d=F32: c.enter_context(nc.sbuf_tensor(n, s, d))
        ps = lambda n, s: c.enter_context(nc.psum_tensor(n, s, F32))
        sem = lambda n: c.enter_context(nc.semaphore(n))
        w_qk = sb("w_qk", [P, 2, KO, P])
        qT, kT = sb("qT", [P, T]), sb("kT", [P, T])
        beta = [sb(f"beta{i}", [P, T]) for i in range(2)]
        stay = [sb(f"stay{i}", [P, T]) for i in range(2)]
        prod = [sb(f"prod{i}", [P, T + 1]) for i in range(2)]
        wT = [sb(f"wT{i}", [P, HALF]) for i in range(WT)]
        attn = sb("attn", [P, TT, QKV])
        wide = [ps(f"wide{i}", [P, T]) for i in range(2)]
        tp = [ps(f"tp{i}", [P, HALF]) for i in range(2)]
        av = [ps(f"av{i}", [P, HALF]) for i in range(2)]
        fin = av[1]
        w_qk_in, w_out_in = sem("w_qk_in"), sem("w_out_in")
        wide_full, wide_free, qk_ready = sem("wide_full"), sem("wide_free"), sem("qk_ready")
        one_ok, sig_ok, mask_ok, scan_ok, weight_ok = (sem(n) for n in ("one_ok", "sig_ok", "mask_ok", "scan_ok", "weight_ok"))
        tp_full, tp_read, av_group, av_full, av_read = (sem(n) for n in ("tp_full", "tp_read", "av_group", "av_full", "av_read"))
        fin_full, fin_read = sem("fin_full"), sem("fin_read")
        pool_turn = sem("pool_turn")

        with nc.Block() as block:

            @block.sync
            def _(sp):
                def load(hp):
                    for i in range(2):
                        sp.dma_start(w_qk[:, i], w_in[0, :, bass.ds(i * QKV + hp * P, P)]
                                     .rearrange("(k p) n -> p k n", p=P)).then_inc(w_qk_in, 16)
                load(0)
                sp.dma_start(w_out_sb[:], w_out[0].rearrange("(k p) n -> p k n", p=P)).then_inc(w_out_in, 16)
                with sp.Fori(0, PAIRS - 1) as hp:
                    sp.wait_ge(wide_full, USES * hp + 2)
                    load(hp + 1)
                sp.wait_ge(w_out_in, 16)

            @block.scalar
            def _(act):
                act.sem_inc(wide_free, 2)
                act.wait_ge(one_ok, 1)
                with act.Fori(0, PAIRS) as hp:
                    for i, dst in enumerate((qT, kT)):
                        act.wait_ge(wide_full, USES * hp + i + 1)
                        nc.scalar.activation(dst[:], wide[i][:], ACT.Copy,
                                             scale=HD ** -0.5 if i == 0 else 1.0).then_inc(wide_free, 1)

                    def sigmoids(u):
                        w = (u // 2 + 1) * P
                        act.wait_ge(wide_full, USES * hp + 2 + u + 1)
                        v = u - 2
                        ahead = first_group[v % UNITS] + n_groups[v % UNITS] - (0 if v >= 0 else G)
                        act.wait_ge(tp_full, G * hp + TP_AHEAD + ahead)
                        nc.scalar.activation(beta[u % 2][:, 0:w], wide[u % 2][:, 0:w], ACT.Sigmoid).then_inc(sig_ok, 1)
                        nc.scalar.activation(stay[u % 2][:, 0:w], wide[u % 2][:, 0:w], ACT.Sigmoid,
                                             scale=-1.0).then_inc(wide_free, 1)

                    sigmoids(0)
                    for u in range(UNITS):
                        if u + 1 < UNITS:
                            sigmoids(u + 1)
                        for g in range(n_groups[u]):
                            n = first_group[u] + g
                            wk = min(4, u // 2 + 1 - 4 * g) * P
                            act.wait_ge(tp_full, G * hp + TP_AHEAD + n + 1)
                            act.wait_ge(av_group, G * hp + n + 1)
                            nc.scalar.activation(wT[n % WT][:, 0:wk], tp[n % 2][:, 0:wk], ACT.Copy).then_inc(tp_read, 1)

            @block.gpsimd
            def _(pool):
                for i in range(2):
                    last = nc.gpsimd.memset(prod[i][:, T:T + 1], 1.0)
                last.then_inc(one_ok, 1)
                with pool.Fori(0, PAIRS) as hp:
                    for u in range(UNITS):
                        i = u // 2
                        pool.wait_ge(wide_free, USES * hp + 2 + 2 + u + 1)
                        pool.sem_inc(pool_turn, 1)
                        for buf, fill in ((beta, 0.0), (stay, 1.0)):
                            tile = buf[u % 2][:, i * P:(i + 1) * P]
                            last = nc.gpsimd.affine_select(out=tile, in_=tile, compare_op=ALU.is_gt, fill=fill, base=0,
                                                           pattern=[[-1, P]], channel_multiplier=1)
                        last.then_inc(mask_ok, 1)

            @block.vector
            def _(dve):
                dve.wait_ge(one_ok, 1)
                with dve.Fori(0, PAIRS) as hp:
                    def take(u):
                        dve.wait_ge(av_full, UNITS * hp + u + 1)
                        nc.vector.tensor_copy(attn[:, u // 2, bass.ds(hp * P + (u % 2) * HD, HD)],
                                              av[u % 2][:, 0:HD]).then_inc(av_read, 1)

                    for u in range(UNITS):
                        w = (u // 2 + 1) * P
                        dve.wait_ge(mask_ok, UNITS * hp + u + 1)
                        nc.vector.tensor_tensor_scan(prod[u % 2][:, T - w:T][:, ::-1], stay[u % 2][:, 0:w][:, ::-1],
                                                     stay[u % 2][:, 0:w][:, ::-1], 1.0, ALU.mult,
                                                     ALU.bypass).then_inc(scan_ok, 1)
                        dve.wait_ge(scan_ok, UNITS * hp + u + 1)
                        nc.vector.tensor_tensor(beta[u % 2][:, 0:w], beta[u % 2][:, 0:w], prod[u % 2][:, T - w + 1:T + 1],
                                                ALU.mult).then_inc(weight_ok, 1)
                        if u:
                            take(u - 1)
                    take(UNITS - 1)
                for t in range(TT):
                    dve.wait_ge(fin_full, t + 1)
                    nc.vector.tensor_copy(mixedT[:, 0:KO // 2, t * P:(t + 1) * P],
                                          fin[:].rearrange("p (k t) -> p k t", t=P)).then_inc(fin_read, 1)

            @block.tensor
            def _(pe):
                pe.sem_inc(tp_full, TP_AHEAD)
                pe.sem_inc(av_group, WT)
                with pe.Fori(0, PAIRS) as hp:
                    pe.wait_ge(w_qk_in, 32 * hp + 32)
                    for i in range(2):
                        pe.wait_ge(wide_free, USES * hp + i + 1)
                        for half in range(2):
                            for ko in range(KO):
                                ins = nc.tensor.matmul(wide[i][:, half * HALF:(half + 1) * HALF], w_qk[:, i, ko, :],
                                                       hT[:, ko, half * HALF:(half + 1) * HALF],
                                                       start=ko == 0, stop=ko == KO - 1)
                        ins.then_inc(wide_full, 1)
                    pe.wait_ge(wide_free, USES * hp + 2 + 2)

                    def scores(u):
                        i, h = divmod(u, 2)
                        w = (i + 1) * P
                        pe.wait_ge(wide_free, USES * hp + 2 + u + 1)
                        for a in range(0, w, HALF):
                            b = min(w, a + HALF)
                            ins = nc.tensor.matmul(wide[u % 2][:, a:b], qT[h * HD:(h + 1) * HD, i * P:(i + 1) * P],
                                                   kT[h * HD:(h + 1) * HD, a:b], start=True, stop=True)
                        ins.then_inc(wide_full, 1)

                    scores(0)
                    scores(1)
                    for u in range(UNITS):
                        i, h = divmod(u, 2)
                        pe.wait_ge(weight_ok, UNITS * hp + u + 1)
                        for g in range(n_groups[u]):
                            n = first_group[u] + g
                            if n >= 2:
                                pe.wait_ge(tp_read, G * hp + n - 1)
                            for kb in range(4 * g, min(4 * g + 4, i + 1)):
                                ins = nc.tensor.transpose(tp[n % 2][:, (kb % 4) * P:(kb % 4 + 1) * P],
                                                          beta[u % 2][:, kb * P:(kb + 1) * P], k["ident"][:])
                            ins.then_inc(tp_full, 1)
                        if u + 2 < UNITS:
                            scores(u + 2)
                        if u >= 2:
                            pe.wait_ge(av_read, UNITS * hp + u - 1)
                        for g in range(n_groups[u]):
                            n = first_group[u] + g
                            pe.wait_ge(tp_read, G * hp + n + 1)
                            for kb in range(4 * g, min(4 * g + 4, i + 1)):
                                ins = nc.tensor.matmul(av[u % 2][:, 0:HD], wT[n % WT][:, (kb % 4) * P:(kb % 4 + 1) * P],
                                                       v_all[:, kb, bass.ds(hp * P + h * HD, HD)],
                                                       start=kb == 0, stop=kb == i)
                            if g < n_groups[u] - 1:
                                ins.then_inc(av_group, 1)
                            else:
                                ins.then_inc(av_full, 1)
                        pe.wait_ge(av_full, UNITS * hp + u + 1)
                        pe.sem_inc(av_group, 1)
                    pe.wait_ge(av_read, UNITS * hp + UNITS)
                for t in range(TT):
                    if t:
                        pe.wait_ge(fin_read, t)
                    for ko in range(KO // 2):
                        ins = nc.tensor.transpose(fin[:, ko * P:(ko + 1) * P], attn[:, t, ko * P:(ko + 1) * P], k["ident"][:])
                    ins.then_inc(fin_full, 1)


def route(nc, k, x_tiles, g_moe, w_router, b_router, mixedT, w_out_sb, h_rows, x2_rows):
    with ExitStack() as c:
        sb = lambda n, s, d=F32: c.enter_context(nc.sbuf_tensor(n, s, d))
        ps = lambda n, s: c.enter_context(nc.psum_tensor(n, s, F32))
        sem = lambda n: c.enter_context(nc.semaphore(n))
        X = sb("X2", [P, TT, D])
        H = [sb(f"H{i}", [P, D]) for i in range(2)]
        hT2 = [sb(f"hT2{i}", [P, KO, P]) for i in range(2)]
        junk = sb("junk", [P, D])
        g_row = sb("g_row", [P, D])
        w_r, b_r = sb("w_r", [P, KO, E_]), sb("b_r", [P, E_])
        ms, rms, rstd = sb("ms", [P, TT]), sb("rms2", [P, TT]), sb("rstd2", [P, TT])
        logits = sb("logits", [P, TT, E_])
        top, top_i = sb("top", [P, TT, 8]), sb("top_i", [P, TT, 8], U32)
        top_f = sb("top_f", [P, TT, K_])
        ex, den, rden = sb("ex", [P, TT, K_]), sb("den", [P, TT]), sb("rden", [P, TT])
        iota_e = sb("iota_e", [P, E_])
        iota_b = sb("iota_b", [P, TABLE])
        iota_p, tile_no = sb("iota_p", [P, 1]), sb("tile_no", [P, TT])
        hot = sb("hot", [P, TT, K_, E_])
        mask = sb("mask", [P, TT, E_])
        mask_b = sb("mask_b", [P, TT, E_], BF16)
        before, ones = sb("before", [P, P], BF16), sb("ones", [P, P], BF16)
        cnt, nb, nb_end, base = (sb(n, [P, E_]) for n in ("cnt", "nb", "nb_end", "base"))
        rank, where = sb("rank", [P, TT, E_]), sb("where", [P, TT, E_])
        picked = sb("picked", [P, TT, K_, E_])
        dest_f = sb("dest_f", [P, TT, K_])
        le, le_nb = sb("le", [P, TABLE, E_]), sb("le_nb", [P, TABLE, E_])
        be_f, done_b = sb("be_f", [P, TABLE]), sb("done_b", [P, TABLE])
        op = [[ps(f"op{i}{j}", [P, HALF]) for j in range(2)] for i in range(2)]
        xp = [ps(f"xp{i}", [P, HALF]) for i in range(2)]
        lp = ps("lp", [P, TT + 1, E_])
        rp = ps("rp", [P, TT + 1, E_])
        x_in, row_in = sem("x_in2"), sem("row_in")
        const_ok = sem("const_ok")
        proj_ok, res_ok, res_read, ms_ok, ms2_ok, rms_ok, rstd_ok, h_ok = (
            sem(n) for n in ("proj_ok", "res_ok", "res_read", "ms_ok", "ms2_ok", "rms_ok2", "rstd_ok2", "h_ok"))
        x2_out, h_out = sem("x2_out"), [sem("h_out0"), sem("h_out1")]
        xp_full, xp_read, lg_full = sem("xp_full"), sem("xp_read"), sem("lg_full")
        mask_ok, rank_full, ex_in, ex_ok, step = (sem(n) for n in ("mask_ok2", "rank_full", "ex_in", "ex_ok", "step"))

        with nc.Block() as block:

            @block.sync
            def _(sp):
                for t in range(TT):
                    sp.dma_start(X[:, t, :], x_tiles[:, t, :]).then_inc(x_in, 16)
                sp.dma_start(g_row[:], g_moe.partition_broadcast(P)[:, 0, :] if False else g_moe.to_broadcast([P, D])).then_inc(row_in, 16)
                sp.dma_start(b_r[:], b_router.to_broadcast([P, E_])).then_inc(row_in, 16)
                sp.dma_start(w_r[:], w_router[0].rearrange("(k p) e -> p k e", p=P)).then_inc(row_in, 16)
                for t in range(TT):
                    sp.wait_ge(res_ok, 2 * t + 2)
                    sp.dma_start(x2_rows[t * P:(t + 1) * P, :], X[:, t, :]).then_inc(x2_out, 16)
                    sp.wait_ge(h_ok, t + 1)
                    sp.dma_start(h_rows[t * P:(t + 1) * P, :], H[t % 2][:]).then_inc(h_out[t % 2], 16)
                sp.wait_ge(x2_out, 16 * TT)
                for stored in h_out:
                    sp.wait_ge(stored, 16 * TT // 2)

            @block.gpsimd
            def _(pool):
                iota = lambda o, pattern, base, cm: nc.gpsimd.iota(o, pattern, base=base, channel_multiplier=cm,
                                                                   allow_small_or_imprecise_dtypes=True)
                iota(iota_e[:], [[1, E_]], 0, 0)
                iota(iota_b[:], [[1, TABLE]], 0, 0)
                iota(k["token_of"][:, :, 0], [[P, TT]], 0, 0)
                iota(k["token_of"][:, :, 1], [[0, TT]], 0, 1)
                nc.gpsimd.memset(ones[:], 1.0)
                nc.gpsimd.memset(before[:], 1.0).then_inc(const_ok, 1)
                pool.wait_ge(const_ok, 1)
                nc.gpsimd.affine_select(out=before[:], in_=before[:], compare_op=ALU.is_gt, fill=0.0, base=0,
                                        pattern=[[1, P]], channel_multiplier=-1).then_inc(const_ok, 1)

            @block.scalar
            def _(act):
                for t in range(TT):
                    act.wait_ge(ms2_ok, t + 1)
                    nc.scalar.activation(rms[:, t:t + 1], ms[:, t:t + 1], ACT.Sqrt).then_inc(rms_ok, 1)
                    for g in range(2):
                        act.wait_ge(xp_full, 2 * t + g + 1)
                        if t >= 2:
                            act.wait_ge(lg_full, t - 1)
                        nc.scalar.activation(hT2[t % 2][:, 4 * g:4 * g + 4, :].rearrange("p k t -> p (k t)"), xp[g][:],
                                             ACT.Copy).then_inc(xp_read, 1)
                act.wait_ge(ex_in, 1)
                nc.scalar.activation(ex[:], ex[:], ACT.Exp).then_inc(ex_ok, 1)

            @block.tensor
            def _(pe):
                def project_out(t):
                    if t >= 2:
                        pe.wait_ge(res_ok, 2 * t - 2)
                    for half in range(2):
                        for ko in range(KO):
                            ins = nc.tensor.matmul(op[t % 2][half][:], mixedT[:, ko, t * P:(t + 1) * P],
                                                   w_out_sb[:, ko, half * HALF:(half + 1) * HALF],
                                                   start=ko == 0, stop=ko == KO - 1)
                    ins.then_inc(proj_ok, 1)

                project_out(0)
                for t in range(TT):
                    if t + 1 < TT:
                        project_out(t + 1)
                    pe.wait_ge(h_ok, t + 1)
                    for g in range(2):
                        if t:
                            pe.wait_ge(xp_read, 2 * t + g - 1)
                        for i in range(4):
                            ins = nc.tensor.transpose(xp[g][:, i * P:(i + 1) * P],
                                                      H[t % 2][:, (4 * g + i) * P:(4 * g + i + 1) * P], k["ident"][:])
                        ins.then_inc(xp_full, 1)
                    pe.wait_ge(xp_read, 2 * t + 2)
                    if t == 0:
                        pe.wait_ge(row_in, 48)
                    for ko in range(KO):
                        ins = nc.tensor.matmul(lp[:, t, :], hT2[t % 2][:, ko, :], w_r[:, ko, :],
                                               start=ko == 0, stop=ko == KO - 1)
                    ins.then_inc(lg_full, 1)
                pe.wait_ge(mask_ok, 1)
                pe.wait_ge(const_ok, 2)
                for t in range(TT + 1):
                    for j in range(min(t + 1, TT)):
                        ins = nc.tensor.matmul(rp[:, t, :], before[:] if j == t else ones[:], mask_b[:, j, :],
                                               start=j == 0, stop=j == min(t, TT - 1))
                ins.then_inc(rank_full, 1)

            @block.vector
            def _(dve):
                for t in range(TT):
                    dve.wait_ge(proj_ok, t + 1)
                    if t == 0:
                        dve.wait_ge(x_in, 16 * TT)
                        dve.wait_ge(row_in, 48)
                    for half in range(2):
                        tile = X[:, t, half * HALF:(half + 1) * HALF]
                        nc.vector.tensor_tensor(tile, op[t % 2][half][:], tile, ALU.add).then_inc(res_ok, 1)
                    dve.wait_ge(res_ok, 2 * t + 2)
                    if t:
                        dve.wait_ge(ms_ok, t)
                    nc.vector.scalar_tensor_tensor(junk[:], X[:, t, :], 1.0 / D, X[:, t, :], ALU.mult, ALU.mult,
                                                   accum_out=ms[:, t:t + 1]).then_inc(ms_ok, 1)
                    dve.wait_ge(ms_ok, t + 1)
                    nc.vector.tensor_scalar(ms[:, t:t + 1], ms[:, t:t + 1], EPS, None, ALU.add).then_inc(ms2_ok, 1)
                    dve.wait_ge(rms_ok, t + 1)
                    nc.vector.reciprocal(rstd[:, t:t + 1], rms[:, t:t + 1]).then_inc(rstd_ok, 1)
                    dve.wait_ge(rstd_ok, t + 1)
                    if t >= 2:
                        dve.wait_ge(xp_full, 2 * (t - 1))
                        dve.wait_ge(h_out[t % 2], 16 * (t // 2))
                    nc.vector.scalar_tensor_tensor(H[t % 2][:], X[:, t, :], rstd[:, t:t + 1], g_row[:], ALU.mult,
                                                   ALU.mult).then_inc(h_ok, 1)
                count = [0]

                def done(ins):
                    count[0] += 1
                    ins.then_inc(step, 1)
                    dve.wait_ge(step, count[0])

                dve.wait_ge(lg_full, TT)
                dve.wait_ge(const_ok, 2)
                done(nc.vector.tensor_tensor(logits[:], lp[:, 0:TT, :], b_r[:, None, :].to_broadcast([P, TT, E_]), ALU.add))
                for t in range(TT):
                    done(nc.vector.max(top[:, t, :], logits[:, t, :]))
                    done(nc.vector.max_index(top_i[:, t, :], top[:, t, :], logits[:, t, :]))
                nc.vector.tensor_tensor(ex[:], top[:, :, 0:K_], top[:, :, 0:1].to_broadcast([P, TT, K_]),
                                        ALU.subtract).then_inc(ex_in, 1)
                done(nc.vector.tensor_copy(top_f[:], top_i[:, :, 0:K_]))
                done(nc.vector.tensor_tensor(hot[:].rearrange("p t k e -> p (t k) e"),
                                             iota_e[:, None, :].to_broadcast([P, TT * K_, E_]),
                                             top_f[:].rearrange("p t k -> p (t k)")[:, :, None].to_broadcast([P, TT * K_, E_]),
                                             ALU.is_equal))
                done(nc.vector.tensor_reduce(mask[:], hot[:].rearrange("p t k e -> p t e k"), AX.X, ALU.add))
                nc.vector.tensor_copy(mask_b[:], mask[:]).then_inc(mask_ok, 1)
                dve.wait_ge(ex_ok, 1)
                done(nc.vector.tensor_reduce(den[:], ex[:], AX.X, ALU.add))
                done(nc.vector.reciprocal(rden[:], den[:]))
                done(nc.vector.tensor_tensor(k["gates"][:], ex[:], rden[:, :, None].to_broadcast([P, TT, K_]), ALU.mult))
                dve.wait_ge(rank_full, 1)
                done(nc.vector.tensor_copy(rank[:], rp[:, 0:TT, :]))
                done(nc.vector.tensor_copy(cnt[:], rp[:, TT, :]))
                done(nc.vector.tensor_scalar(nb[:], cnt[:], 0.0, 1.0, ALU.mult, ALU.add))
                for i in range(1, MAX_BLOCKS_PER_EXPERT):
                    done(nc.vector.scalar_tensor_tensor(nb[:], cnt[:], float(i * SLOTS), nb[:], ALU.is_gt, ALU.add))
                done(nc.vector.tensor_tensor_scan(nb_end[:], nb[:], nb[:], 0.0, ALU.add, ALU.bypass))
                done(nc.vector.tensor_tensor_scan(base[:], cnt[:], cnt[:], 0.0, ALU.add, ALU.bypass))
                done(nc.vector.tensor_tensor(base[:], base[:], cnt[:], ALU.subtract))
                done(nc.vector.tensor_scalar(k["last_block"][:], nb_end[:, E_ - 1:E_], -1.0, None, ALU.add))
                done(nc.vector.tensor_tensor(where[:], rank[:], base[:, None, :].to_broadcast([P, TT, E_]), ALU.add))
                for t in range(TT):
                    done(nc.vector.tensor_tensor(picked[:, t], hot[:, t], where[:, t, None, :].to_broadcast([P, K_, E_]), ALU.mult))
                done(nc.vector.tensor_reduce(dest_f[:], picked[:], AX.X, ALU.add))
                done(nc.vector.tensor_copy(k["dest"][:], dest_f[:]))
                done(nc.vector.scalar_tensor_tensor(rank[:], rank[:], 1.0, mask[:], ALU.add, ALU.mult))
                done(nc.vector.tensor_scalar(k["ranks"][:], rank[:], -1.0, None, ALU.add))
                done(nc.vector.tensor_tensor(le[:], nb_end[:, None, :].to_broadcast([P, TABLE, E_]),
                                             iota_b[:, :, None].to_broadcast([P, TABLE, E_]), ALU.is_le))
                done(nc.vector.tensor_reduce(be_f[:], le[:], AX.X, ALU.add))
                done(nc.vector.tensor_scalar(be_f[:], be_f[:], float(E_ - 1), None, ALU.min))
                done(nc.vector.tensor_copy(k["block_expert"][:], be_f[:]))
                done(nc.vector.tensor_tensor(le_nb[:], le[:], nb[:, None, :].to_broadcast([P, TABLE, E_]), ALU.mult))
                done(nc.vector.tensor_reduce(done_b[:], le_nb[:], AX.X, ALU.add))
                done(nc.vector.tensor_tensor(done_b[:], iota_b[:], done_b[:], ALU.subtract))
                done(nc.vector.tensor_scalar(k["block_first"][:], done_b[:], float(SLOTS), None, ALU.mult))
                done(nc.vector.tensor_tensor(le[:], le[:], cnt[:, None, :].to_broadcast([P, TABLE, E_]), ALU.mult))
                done(nc.vector.tensor_reduce(done_b[:], le[:], AX.X, ALU.add))
                done(nc.vector.tensor_tensor(done_b[:], done_b[:], k["block_first"][:], ALU.add))
                done(nc.vector.tensor_copy(k["block_row"][:], done_b[:]))


def experts(nc, k, w_gate_up, w_down, h_rows, y_rows):
    with ExitStack() as c:
        sb = lambda n, s, d=F32: c.enter_context(nc.sbuf_tensor(n, s, d))
        ps = lambda n, s: c.enter_context(nc.psum_tensor(n, s, F32))
        sem = lambda n: c.enter_context(nc.semaphore(n))
        raw = [sb(f"raw{i}", [P, KO, CC]) for i in range(RAW)]
        w_hi = [sb(f"w_hi{i}", [P, KO, CC], F32R) for i in range(SPLIT)]
        w_lo = [sb(f"w_lo{i}", [P, KO, CC], F32R) for i in range(SPLIT)]
        rows = [sb(f"rows{i}", [n, D]) for i, n in enumerate(SEG)]
        x_s = sb("x_s", [P, KO, 2, SLOTS], F32R)
        a_s = sb("a_s", [P, KO, 2, SLOTS], F32R)
        half = [sb(f"half{i}", [P, SLOTS]) for i in range(BANKS)]
        gate = [sb(f"gate{i}", [P, MC, SLOTS]) for i in range(2)]
        sig = [sb(f"sig{i}", [P, MC, SLOTS]) for i in range(2)]
        up = [sb(f"up{i}", [P, MC, SLOTS]) for i in range(2)]
        glu = [sb(f"glu{i}", [P, MC, SLOTS]) for i in range(2)]
        y_col = [sb(f"y_col{i}", [P, MC, SLOTS]) for i in range(2)]
        y_st = [sb(f"y_st{i}", [n, D]) for i, n in enumerate(SEG)]
        rank_cur = sb("rank_cur", [P, TT])
        slot_no = sb("slot_no", [P, SLOTS])
        hot = sb("hot_slot", [P, TT, SLOTS], BF16)
        idx = sb("idx", [P, 2], I32)
        b_gu, b_dn = sb("b_gu", [P, 2 * D // P]), sb("b_dn", [P, D // P])
        mm = [ps(f"mm{i}", [P, 2, SLOTS]) for i in range(BANKS)]
        xt = [ps(f"xt{i}", [P, HALF]) for i in range(3)]
        yt = ps("yt", [P, 2, CC])
        LIST = HALF - 8

        raw_in = [sem(f"raw_in{i}") for i in range(RAW)]
        hi_done, lo_done, mm_done = sem("hi_done"), sem("lo_done"), sem("mm_done")
        half_ok, sum_ok = sem("half_ok"), sem("sum_ok3")
        gate_ok, up_ok, sig_ok, pre_ok, glu_ok, a_hi_ok, a_lo_ok = (
            sem(n) for n in ("gate_ok", "up_ok", "sig_ok2", "pre_ok", "glu_ok", "a_hi_ok", "a_lo_ok"))
        slot_ok, rank_ok, hot_ok, list_full, idx_ok, rows_in = (
            sem(n) for n in ("slot_ok", "rank_ok", "hot_ok", "list_full", "idx_ok", "rows_in"))
        xt_full, x_hi_ok, x_lo_ok = sem("xt_full"), sem("x_hi_ok"), sem("x_lo_ok")
        b_gu_ok, b_dn_ok = sem("b_gu_ok"), sem("b_dn_ok")
        yt_full, yt_read, y_out, y_free = (sem(n) for n in ("yt_full", "yt_read", "y_out", "y_free"))
        pool_turn = sem("pool_turn2")
        AHEAD = SPLIT - 1
        PC = PAIR_CHUNKS
        TILES = CHUNKS * MC
        MM_AHEAD = SPLIT * MC
        SUM_AHEAD = BANKS
        YT_AHEAD = 3

        def last_block(eng):
            return eng.value_load(k["last_block"][0:1, 0:1], min_val=E_ - 1, max_val=MAX_BLOCKS - 1)

        with nc.Block() as block:

            @block.sync
            def _(sp):
                final = last_block(sp)

                def load(c_, e, turn):
                    slot = raw[c_ % RAW]
                    if c_ < 2 * PC:
                        col = (c_ % 2) * D + (c_ // 2) * CC
                        src = w_gate_up[0, bass.ds(e, 1), :, col:col + CC]
                    else:
                        src = w_down[0, bass.ds(e, 1), :, (c_ - 2 * PC) * CC:(c_ - 2 * PC + 1) * CC]
                    if turn is not None:
                        sp.wait_ge(hi_done, turn)
                        sp.wait_ge(lo_done, turn)
                    sp.dma_start(slot[:], src.rearrange("a (k p) n -> p (a k) n", p=P)).then_inc(raw_in[c_ % RAW], 16)

                def expert_of(b):
                    return sp.value_load(k["block_expert"][0:1, bass.ds(b, 1)], min_val=0, max_val=E_ - 1)

                for c_ in range(RAW):
                    load(c_, 0, None)
                with sp.Fori(0, final) as b:
                    e = expert_of(b)
                    for c_ in range(RAW, CHUNKS):
                        load(c_, e, CHUNKS * b + c_ - RAW + 1)
                    e = expert_of(b + 1)
                    for c_ in range(RAW):
                        load(c_, e, CHUNKS * b + CHUNKS + c_ - RAW + 1)
                e = expert_of(final)
                for c_ in range(RAW, CHUNKS):
                    load(c_, e, CHUNKS * final + c_ - RAW + 1)

            @block.gpsimd
            def _(pool):
                final = last_block(pool)

                def until(semaphore, value):
                    pool.wait_ge(semaphore, value)
                    pool.sem_inc(pool_turn, 1)

                def expert_of(b):
                    return pool.value_load(k["block_expert"][0:1, bass.ds(b, 1)], min_val=0, max_val=E_ - 1)

                def ranks(e, b):
                    nc.gpsimd.tensor_tensor(rank_cur[:], k["ranks"][:, :, bass.ds(e, 1)].rearrange("p t a -> p (t a)"),
                                            k["block_first"][:, bass.ds(b, 1)].to_broadcast([P, TT]),
                                            ALU.subtract).then_inc(rank_ok, 1)

                def gather(turn):
                    until(idx_ok, turn)
                    for s, n in enumerate(SEG):
                        nc.gpsimd.indirect_dma_start(
                            out=rows[s][:], out_offset=None, in_=h_rows,
                            in_offset=bass.IndirectOffsetOnAxis(ap=idx[0:n, s:s + 1], axis=0)).then_inc(rows_in, 16)

                def bias_gu(e):
                    nc.gpsimd.tensor_copy(b_gu[:], k["bias_gu"][:, :, bass.ds(e, 1)].rearrange("p m a -> p (m a)")).then_inc(b_gu_ok, 1)

                nc.gpsimd.iota(slot_no[:], [[1, SLOTS]], base=0, channel_multiplier=0,
                               allow_small_or_imprecise_dtypes=True).then_inc(slot_ok, 1)
                pool.sem_inc(y_free, 1)
                e = expert_of(0)
                ranks(e, 0)
                bias_gu(e)
                gather(1)

                def body(b, last):
                    e_ = expert_of(b)
                    until(sum_ok, SUM_AHEAD + TILES * b)
                    nc.gpsimd.tensor_copy(b_dn[:], k["bias_dn"][:, :, bass.ds(e_, 1)].rearrange("p m a -> p (m a)")).then_inc(b_dn_ok, 1)
                    if not last:
                        en = expert_of(b + 1)
                        until(hot_ok, b + 1)
                        ranks(en, b + 1)
                    for j in range(PC):
                        until(sig_ok, PC * b + j + 1)
                        nc.gpsimd.tensor_tensor(sig[j % 2][:], gate[j % 2][:], sig[j % 2][:], ALU.mult).then_inc(pre_ok, 1)
                        if j == 2 and not last:
                            gather(b + 2)
                    if not last:
                        until(sum_ok, SUM_AHEAD + TILES * b + 2 * PC * MC)
                        bias_gu(en)
                    row = pool.value_load(k["block_row"][0:1, bass.ds(b, 1)], min_val=0, max_val=T * K_)
                    until(yt_read, PC * b + PC)
                    for s, n in enumerate(SEG):
                        pool.dma_start(y_rows[bass.ds(row + s * P, n), :], y_st[s][:]).then_inc(y_out, 16)
                    until(y_out, 32 * b + 32)
                    pool.sem_inc(y_free, 1)

                with pool.Fori(0, final) as b:
                    body(b, False)
                body(final, True)

            @block.scalar
            def _(act):
                final = last_block(act)

                def hi(b, c_, first=False):
                    act.wait_ge(raw_in[c_ % RAW], 16 * (CHUNKS // RAW * b + c_ // RAW + 1))
                    if not first:
                        act.wait_ge(mm_done, TILES * b + MC * c_ + MM_AHEAD - (SPLIT - 1) * MC)
                    nc.scalar.activation(w_hi[c_ % SPLIT][:], raw[c_ % RAW][:], ACT.Copy).then_inc(hi_done, 1)

                def x_high(turn):
                    ko = 0
                    for g, n in enumerate(XG):
                        act.wait_ge(xt_full, len(XG) * turn + g + 1)
                        nc.scalar.activation(x_s[:, ko:ko + n, 0, :], xt[g][:, 0:n * SLOTS].rearrange("p (k t) -> p k t", k=n),
                                             ACT.Copy).then_inc(x_hi_ok, 1)
                        ko += n

                def a_high(b, j):
                    act.wait_ge(glu_ok, PC * b + j + 1)
                    nc.scalar.activation(a_s[:, MC * j:MC * j + MC, 0, :], glu[j % 2][:], ACT.Copy).then_inc(a_hi_ok, 1)

                def halves(b, c_):
                    if c_ == 0:
                        act.wait_ge(b_gu_ok, b + 1)
                    if c_ == 2 * PC:
                        act.wait_ge(b_dn_ok, b + 1)
                    for m in range(MC):
                        if c_ < 2 * PC:
                            col = (c_ % 2) * (D // P) + MC * (c_ // 2) + m
                            bias = b_gu[:, col:col + 1]
                        else:
                            col = MC * (c_ - 2 * PC) + m
                            bias = b_dn[:, col:col + 1]
                        t = MC * c_ + m
                        act.wait_ge(mm_done, TILES * b + MM_AHEAD + t + 1)
                        act.wait_ge(sum_ok, TILES * b + SUM_AHEAD + t - BANKS + 1)
                        nc.scalar.activation(half[t % BANKS][:], mm[t % BANKS][:, 1, :], ACT.Identity,
                                             bias=bias).then_inc(half_ok, 1)

                def y_rows_out(b, q):
                    act.wait_ge(yt_full, YT_AHEAD + PC * b + q + 1)
                    if q == 0:
                        act.wait_ge(y_free, b + 1)
                    for s, n in enumerate(SEG):
                        ins = nc.scalar.activation(y_st[s][:, q * CC:(q + 1) * CC], yt[0:n, s, :], ACT.Copy)
                    ins.then_inc(yt_read, 1)

                hi(0, 0, True)
                x_high(0)
                hi(0, 1, True)
                hi(0, 2, True)
                halves(0, 0)

                def body(b, last):
                    for c_ in range(1, CHUNKS + 1):
                        nb, nc_ = (b + 1, c_ - CHUNKS) if c_ == CHUNKS else (b, c_)
                        if c_ + AHEAD < CHUNKS:
                            hi(b, c_ + AHEAD)
                        elif not last:
                            hi(b + 1, c_ + AHEAD - CHUNKS)
                        j = c_ // 2
                        if c_ < 2 * PC and c_ % 2 == 1:
                            act.wait_ge(gate_ok, PC * b + j + 1)
                            nc.scalar.activation(sig[j % 2][:], gate[j % 2][:], ACT.Sigmoid, scale=ALPHA).then_inc(sig_ok, 1)
                            if j:
                                a_high(b, j - 1)
                        if c_ < CHUNKS or not last:
                            halves(nb, nc_)
                        if c_ == 2 * PC - 1:
                            a_high(b, PC - 1)
                            if not last:
                                x_high(b + 1)
                        if c_ > 2 * PC + 1:
                            y_rows_out(b, c_ - 2 * PC - 2)
                    y_rows_out(b, PC - 1)

                with act.Fori(0, final) as b:
                    body(b, False)
                body(final, True)

            @block.vector
            def _(dve):
                final = last_block(dve)
                dve.sem_inc(sum_ok, SUM_AHEAD)

                def lo(b, c_, first=False):
                    dve.wait_ge(hi_done, CHUNKS * b + c_ + 1)
                    if not first:
                        dve.wait_ge(mm_done, TILES * b + MC * c_ + MM_AHEAD - (SPLIT - 1) * MC)
                    nc.vector.tensor_tensor(w_lo[c_ % SPLIT][:], raw[c_ % RAW][:], w_hi[c_ % SPLIT][:].bitcast(F32),
                                            ALU.subtract).then_inc(lo_done, 1)

                def one_hot(turn):
                    dve.wait_ge(rank_ok, turn)
                    nc.vector.tensor_tensor(hot[:], slot_no[:, None, :].to_broadcast([P, TT, SLOTS]),
                                            rank_cur[:, :, None].to_broadcast([P, TT, SLOTS]), ALU.is_equal).then_inc(hot_ok, 1)

                def indices(turn):
                    dve.wait_ge(list_full, turn)
                    with nc.allow_low_precision(reason="whole numbers below 1024"):
                        for s, n in enumerate(SEG):
                            ins = nc.vector.tensor_reduce(idx[0:n, s:s + 1], xt[2][0:n, LIST + 2 * s:LIST + 2 * s + 2],
                                                          AX.X, ALU.add)
                    ins.then_inc(idx_ok, 1)

                def x_low(turn):
                    ko = 0
                    for g, n in enumerate(XG):
                        dve.wait_ge(x_hi_ok, len(XG) * turn + g + 1)
                        nc.vector.tensor_tensor(x_s[:, ko:ko + n, 1, :], xt[g][:, 0:n * SLOTS].rearrange("p (k t) -> p k t", k=n),
                                                x_s[:, ko:ko + n, 0, :].bitcast(F32), ALU.subtract).then_inc(x_lo_ok, 1)
                        ko += n

                def swiglu(b, j):
                    dve.wait_ge(pre_ok, PC * b + j + 1)
                    nc.vector.scalar_tensor_tensor(glu[j % 2][:], up[j % 2][:], 1.0, sig[j % 2][:], ALU.add,
                                                   ALU.mult).then_inc(glu_ok, 1)

                def a_low(b, j):
                    dve.wait_ge(a_hi_ok, PC * b + j + 1)
                    nc.vector.tensor_tensor(a_s[:, MC * j:MC * j + MC, 1, :], glu[j % 2][:],
                                            a_s[:, MC * j:MC * j + MC, 0, :].bitcast(F32), ALU.subtract).then_inc(a_lo_ok, 1)

                def sums(b, c_):
                    j = c_ // 2
                    down = c_ >= 2 * PC
                    dst = y_col[c_ % 2] if down else (gate, up)[c_ % 2][j % 2]
                    if down:
                        dve.wait_ge(yt_full, YT_AHEAD + PC * b + c_ - 2 * PC - 1)
                    for m in range(MC):
                        t = MC * c_ + m
                        dve.wait_ge(half_ok, TILES * b + t + 1)
                        nc.vector.tensor_tensor(dst[:, m, :], mm[t % BANKS][:, 0, :], half[t % BANKS][:],
                                                ALU.add).then_inc(sum_ok, 1)
                    if not down:
                        dve.wait_ge(sum_ok, TILES * b + SUM_AHEAD + MC * (c_ + 1))
                        if c_ % 2 == 0:
                            nc.vector.tensor_scalar(dst[:], dst[:], LIMIT, None, ALU.min).then_inc(gate_ok, 1)
                        else:
                            nc.vector.tensor_scalar(dst[:], dst[:], LIMIT, -LIMIT, ALU.min, ALU.max).then_inc(up_ok, 1)
                            dve.wait_ge(up_ok, PC * b + j + 1)

                dve.wait_ge(slot_ok, 1)
                one_hot(1)
                indices(1)
                lo(0, 0, True)
                x_low(0)
                lo(0, 1, True)
                lo(0, 2, True)
                sums(0, 0)

                def body(b, last):
                    for c_ in range(1, CHUNKS + 1):
                        if c_ + AHEAD < CHUNKS:
                            lo(b, c_ + AHEAD)
                        elif not last:
                            lo(b + 1, c_ + AHEAD - CHUNKS)
                        j = c_ // 2
                        if c_ < 2 * PC and c_ % 2 == 1 and j:
                            a_low(b, j - 1)
                        if c_ < CHUNKS:
                            sums(b, c_)
                        elif not last:
                            sums(b + 1, 0)
                        if c_ < 2 * PC and c_ % 2 == 0:
                            swiglu(b, j - 1)
                        if c_ == 2 * PC - 1:
                            swiglu(b, PC - 1)
                            a_low(b, PC - 1)
                            if not last:
                                x_low(b + 1)
                        if not last:
                            if c_ == 1:
                                one_hot(b + 2)
                            if c_ == 4:
                                indices(b + 2)

                with dve.Fori(0, final) as b:
                    body(b, False)
                body(final, True)

            @block.tensor
            def _(pe):
                final = last_block(pe)
                pe.sem_inc(mm_done, MM_AHEAD)
                pe.sem_inc(yt_full, YT_AHEAD)

                def token_list(turn):
                    pe.wait_ge(hot_ok, turn)
                    for s, n in enumerate(SEG):
                        for t in range(TT):
                            ins = nc.tensor.matmul(xt[2][0:n, LIST + 2 * s:LIST + 2 * s + 2], hot[:, t, s * P:s * P + n],
                                                   k["token_of"][:, t, :], start=t == 0, stop=t == TT - 1)
                    ins.then_inc(list_full, 1)

                def x_transposes(turn):
                    pe.wait_ge(rows_in, 32 * turn + 32)
                    ko = 0
                    for g, n in enumerate(XG):
                        for i in range(n):
                            for s, rows_n in enumerate(SEG):
                                ins = nc.tensor.transpose(xt[g][:, i * SLOTS + s * P:i * SLOTS + s * P + rows_n],
                                                          rows[s][:, (ko + i) * P:(ko + i + 1) * P],
                                                          k["ident"][0:rows_n, 0:rows_n])
                        ins.then_inc(xt_full, 1)
                        ko += n

                def y_transposes(b, q):
                    pe.wait_ge(sum_ok, TILES * b + SUM_AHEAD + MC * (2 * PC + q + 1))
                    if q:
                        pe.wait_ge(yt_read, PC * b + q)
                    for s, n in enumerate(SEG):
                        for m in range(MC):
                            ins = nc.tensor.transpose(yt[0:n, s, m * P:(m + 1) * P], y_col[q % 2][:, m, s * P:s * P + n],
                                                      k["ident"][:])
                    ins.then_inc(yt_full, 1)

                def chunk(b, c_):
                    in_s = a_s if c_ >= 2 * PC else x_s
                    hi_, lo_ = w_hi[c_ % SPLIT], w_lo[c_ % SPLIT]
                    if c_ == 0:
                        pe.wait_ge(x_lo_ok, len(XG) * b + len(XG))
                    pe.wait_ge(lo_done, CHUNKS * b + c_ + 1)
                    parts = [range(0, KO - MC), range(KO - MC, KO)] if c_ == 2 * PC else [range(KO)]
                    for n, part in enumerate(parts):
                        if c_ == 2 * PC:
                            pe.wait_ge(a_lo_ok, PC * b + PC - 1 + n)
                        for m in range(MC):
                            t = MC * c_ + m
                            if n == 0:
                                pe.wait_ge(sum_ok, TILES * b + SUM_AHEAD + t - BANKS + 1)
                            for ko in part:
                                nc.tensor.matmul(mm[t % BANKS][:], hi_[:, ko, m * P:(m + 1) * P], in_s[:, ko, :, :],
                                                 start=ko == 0, stop=False)
                                ins = nc.tensor.matmul(mm[t % BANKS][:, 0, :], lo_[:, ko, m * P:(m + 1) * P],
                                                       in_s[:, ko, 0, :], start=False, stop=ko == KO - 1)
                            if part[-1] == KO - 1:
                                ins.then_inc(mm_done, 1)

                token_list(1)
                x_transposes(0)
                chunk(0, 0)

                def body(b, last):
                    for c_ in range(1, CHUNKS):
                        chunk(b, c_)
                        if c_ == 3 and not last:
                            token_list(b + 2)
                        if c_ == 2 * PC - 1 and not last:
                            x_transposes(b + 1)
                        if c_ > 2 * PC:
                            y_transposes(b, c_ - 2 * PC - 1)
                    if not last:
                        chunk(b + 1, 0)
                    y_transposes(b, PC - 1)

                with pe.Fori(0, final) as b:
                    body(b, False)
                body(final, True)


def combine(nc, k, g_final, x2_rows, y_rows, out_tiles):
    with ExitStack() as c:
        sb = lambda n, s, d=F32: c.enter_context(nc.sbuf_tensor(n, s, d))
        sem = lambda n: c.enter_context(nc.semaphore(n))
        RING = 3
        X = sb("X3", [P, TT, D])
        Y = [sb(f"Y{i}", [P, K_, D]) for i in range(RING)]
        junk, g_row = sb("junk3", [P, D]), sb("g_row3", [P, D])
        ms, rms, rstd = sb("ms3", [P, TT]), sb("rms3", [P, TT]), sb("rstd3", [P, TT])
        x_in, g_in, out_done = sem("x_in3"), sem("g_in3"), sem("out_done")
        y_in = [sem(f"y_in{i}") for i in range(RING)]
        y_used, acc, ms_ok, ms2_ok, rms_ok, rstd_ok, out_ok = (
            sem(n) for n in ("y_used", "acc3", "ms_ok3", "ms2_ok3", "rms_ok3", "rstd_ok3", "out_ok3"))

        with nc.Block() as block:

            @block.sync
            def _(sp):
                sp.dma_start(X[:], x2_rows.rearrange("(t p) d -> p t d", p=P)).then_inc(x_in, 16)
                sp.dma_start(g_row[:], g_final.rearrange("(a d) -> a d", a=1).to_broadcast([P, D])).then_inc(g_in, 16)
                for t in range(TT):
                    sp.wait_ge(out_ok, t + 1)
                    sp.dma_start(out_tiles[:, t, :], X[:, t, :]).then_inc(out_done, 16)
                sp.wait_ge(out_done, 16 * TT)

            @block.gpsimd
            def _(pool):
                for t in range(TT):
                    if t >= RING:
                        pool.wait_ge(y_used, t - RING + 1)
                    for i in range(K_):
                        nc.gpsimd.indirect_dma_start(
                            out=Y[t % RING][:, i, :], out_offset=None, in_=y_rows[0:T * K_, :],
                            in_offset=bass.IndirectOffsetOnAxis(ap=k["dest"][:, t, i:i + 1], axis=0)).then_inc(y_in[t % RING], 16)

            @block.scalar
            def _(act):
                for t in range(TT):
                    act.wait_ge(ms2_ok, t + 1)
                    nc.scalar.activation(rms[:, t:t + 1], ms[:, t:t + 1], ACT.Sqrt).then_inc(rms_ok, 1)

            @block.vector
            def _(dve):
                dve.wait_ge(x_in, 16)
                dve.wait_ge(g_in, 16)
                n = 0
                for t in range(TT):
                    dve.wait_ge(y_in[t % RING], 16 * K_ * (t // RING + 1))
                    for i in range(K_):
                        ins = nc.vector.scalar_tensor_tensor(X[:, t, :], Y[t % RING][:, i, :], k["gates"][:, t, i:i + 1],
                                                             X[:, t, :], ALU.mult, ALU.add).then_inc(acc, 1)
                        n += 1
                        dve.wait_ge(acc, n)
                    if t:
                        dve.wait_ge(ms_ok, t)
                    nc.vector.scalar_tensor_tensor(junk[:], X[:, t, :], 1.0 / D, X[:, t, :], ALU.mult, ALU.mult,
                                                   accum_out=ms[:, t:t + 1]).then_inc(ms_ok, 1)
                    dve.wait_ge(ms_ok, t + 1)
                    nc.vector.tensor_scalar(ms[:, t:t + 1], ms[:, t:t + 1], EPS, None, ALU.add).then_inc(ms2_ok, 1)
                    dve.sem_inc(y_used, 1)
                    dve.wait_ge(rms_ok, t + 1)
                    nc.vector.reciprocal(rstd[:, t:t + 1], rms[:, t:t + 1]).then_inc(rstd_ok, 1)
                    dve.wait_ge(rstd_ok, t + 1)
                    nc.vector.scalar_tensor_tensor(X[:, t, :], X[:, t, :], rstd[:, t:t + 1], g_row[:], ALU.mult,
                                                   ALU.mult).then_inc(out_ok, 1)


_INS = ["x", "g_mix", "w_in", "pool_w", "pool_scale", "w_out", "g_moe", "w_router", "b_router",
        "w_gate_up", "b_gate_up", "w_down", "b_down", "g_final"]


def kernel(**inputs):
    import numpy as np
    import concourse.bacc as bacc
    from concourse.bass_utils import run_bass_kernel_spmd

    nc = bacc.Bacc("TRN2", target_bir_lowering=False, num_devices=1)
    arrays, args = {}, []
    for name in _INS:
        a = np.ascontiguousarray(inputs[name])
        arrays[f"in_{name}"] = a
        args.append(nc.dram_tensor(f"in_{name}", a.shape, mybir.dt.from_np(a.dtype), kind="ExternalInput").ap())
    out = nc.dram_tensor("out_0", (1, T, D), F32, kind="ExternalOutput").ap()
    hybrid_moe_kernel(nc, *args, out)
    r = run_bass_kernel_spmd(nc, [arrays], core_ids=[0])
    return r.results[0]["out_0"]
```

```python
from contextlib import ExitStack

import concourse.bass as bass
from concourse import mybir

F32 = mybir.dt.float32
F32R = mybir.dt.float32r
BF16 = mybir.dt.bfloat16
I32 = mybir.dt.int32
U32 = mybir.dt.uint32
ALU = mybir.AluOpType
ACT = mybir.ActivationFunctionType
AX = mybir.AxisListType

P = 128
D = 1024
T = 1024
KO = D // P
TT = T // P
HALF = 512
HEADS, HD = 8, 64
PAIRS = HEADS // 2
QKV = HEADS * HD
WINDOWS = (2, 4, 8, 16)
PAD = max(WINDOWS)
EPS = 1e-5
E_, K_ = 32, 4
LIMIT, ALPHA = 7.0, 1.702

SLOTS = 160
SEG = (128, SLOTS - 128)
MAX_BLOCKS_PER_EXPERT = -(-T // SLOTS)
MAX_BLOCKS = E_ + T * K_ // SLOTS
TABLE = 64
assert MAX_BLOCKS + 1 < TABLE

CC = 256
MC = CC // P
PAIR_CHUNKS = D // CC
CHUNKS = 3 * PAIR_CHUNKS
RAW = 6
SPLIT = 4
BANKS = 4
XG = (3, 3, 2)


def hybrid_moe_kernel(nc, x, g_mix, w_in, pool_w, pool_scale, w_out, g_moe, w_router, b_router,
                      w_gate_up, b_gate_up, w_down, b_down, g_final, out):
    h_rows = nc.dram_tensor("h_rows", [T, D], F32, kind="Internal").ap()
    y_rows = nc.dram_tensor("y_rows", [T * K_ + SLOTS, D], F32, kind="Internal").ap()
    x_tiles = x.rearrange("a (t p) d -> p (a t) d", p=P)
    out_tiles = out.rearrange("a (t p) d -> p (a t) d", p=P)

    with ExitStack() as keep:
        sb = lambda n, s, d=F32: keep.enter_context(nc.sbuf_tensor(n, s, d))
        k = {}
        k["ident"] = sb("ident", [P, P])
        k["logits"] = sb("logits", [P, TT, E_])
        k["bias_gu"] = sb("bias_gu", [P, 2 * D // P, E_])
        k["bias_dn"] = sb("bias_dn", [P, D // P, E_])
        k["ranks"] = sb("ranks", [P, TT, E_])
        k["gates"] = sb("gates", [P, TT, K_])
        k["dest"] = sb("dest", [P, TT, K_], I32)
        k["block_expert"] = sb("block_expert", [P, TABLE], I32)
        k["block_first"] = sb("block_first", [P, TABLE])
        k["block_row"] = sb("block_row", [P, TABLE], I32)
        k["block_tokens"] = sb("block_tokens", [P, TABLE], I32)
        k["last_block"] = sb("last_block", [P, 1], I32)
        k["token_of"] = sb("token_of", [P, TT, 2], BF16)
        with ExitStack() as mix:
            pool_T = mix.enter_context(nc.sbuf_tensor("pool_T", [P, KO // 2, T], F32))
            attn = mix.enter_context(nc.sbuf_tensor("attn", [P, TT, QKV], F32))
            with ExitStack() as at:
                h_hi = at.enter_context(nc.sbuf_tensor("h_hi", [P, KO, T], F32R))
                h_lo = at.enter_context(nc.sbuf_tensor("h_lo", [P, KO, T], F32R))
                v_all = at.enter_context(nc.sbuf_tensor("v_all", [P, TT, QKV], F32))
                project(nc, k, x_tiles, g_mix, w_in, pool_w, pool_scale, h_hi, h_lo, v_all, pool_T, attn)
                attend(nc, k, w_in, h_hi, h_lo, v_all, attn)
            k["x2"] = keep.enter_context(nc.sbuf_tensor("x2", [P, TT, D], F32, side="right"))
            project_out(nc, k, x_tiles, g_moe, w_out, w_router, b_router, attn, pool_T, h_rows)
        with ExitStack() as moe:
            raw = [moe.enter_context(nc.sbuf_tensor(f"raw{i}", [P, KO, CC], F32)) for i in range(RAW)]
            raw_in = [moe.enter_context(nc.semaphore(f"raw_in{i}")) for i in range(RAW)]
            route(nc, k, w_gate_up, w_down, b_gate_up, b_down, raw, raw_in)
            experts(nc, k, w_gate_up, w_down, h_rows, y_rows, raw, raw_in)
        combine(nc, k, g_final, y_rows, out_tiles)


def three_passes(nc, out, still, moving, first, last):
    nc.tensor.matmul(out, still[0], moving[0], start=first, stop=False)
    nc.tensor.matmul(out, still[0], moving[1], start=False, stop=False)
    return nc.tensor.matmul(out, still[1], moving[0], start=False, stop=last)


def project(nc, k, x_tiles, g_mix, w_in, pool_w, pool_scale, h_hi, h_lo, v_all, pool_T, spare):
    with ExitStack() as c:
        sb = lambda n, s, d=F32: c.enter_context(nc.sbuf_tensor(n, s, d))
        ps = lambda n, s: c.enter_context(nc.psum_tensor(n, s, F32))
        sem = lambda n: c.enter_context(nc.semaphore(n))
        X = sb("X", [P, TT, D])
        spare = spare[:].rearrange("p t d -> p (t d)")
        square = spare[:, 0:D]
        w_u = spare[:, D:D + KO * P].rearrange("p (k n) -> p k n", k=KO)
        pw = spare[:, D + KO * P:D + (KO + len(WINDOWS)) * P].rearrange("p (k n) -> p k n", k=len(WINDOWS))
        mean_sq, rms, rstd = sb("mean_sq", [P, TT]), sb("rms", [P, TT]), sb("rstd", [P, TT])
        g_col = sb("g_col", [P, KO])
        scale_col = sb("scale_col", [P, len(WINDOWS)])
        w_v, wv_hi, wv_lo = sb("w_v", [P, KO, QKV]), sb("wv_hi", [P, KO, QKV], F32R), sb("wv_lo", [P, KO, QKV], F32R)
        wu_hi, wu_lo = sb("wu_hi", [P, KO, P], F32R), sb("wu_lo", [P, KO, P], F32R)
        count, inv = sb("count", [P, PAD]), sb("inv", [P, len(WINDOWS), PAD])
        iota1 = sb("iota1", [P, PAD])
        X_flat = X[:].rearrange("p t d -> p (t d)")
        u, *sums = (X_flat[:, i * (PAD + T):(i + 1) * (PAD + T)] for i in range(3))
        pooled = X_flat[:, 3 * (PAD + T):3 * (PAD + T) + T]
        bank = [ps(f"pj{i}", [P, HALF]) for i in range(8)]
        x_in = [sem(f"x_in{i}") for i in range(TT)]
        cols_in, wv_in, wu_in, pw_in = (sem(n) for n in ("cols_in", "wv_in", "wu_in", "pw_in"))
        ident_ok, iota_ok, pad_ok = sem("ident_ok"), sem("iota_ok"), sem("pad_ok")
        sq_done, mean_ok, rms_ok, rstd_ok, x_scaled = (sem(n) for n in ("sq_done", "mean_ok", "rms_ok", "rstd_ok", "x_scaled"))
        pe_bank, act_read, dve_read = sem("pe_bank"), sem("act_read"), sem("dve_read")
        wv_hi_ok, wv_lo_ok, wu_hi_ok, wu_lo_ok = (sem(n) for n in ("wv_hi_ok", "wv_lo_ok", "wu_hi_ok", "wu_lo_ok"))
        inv_ok, sum_ok, pooled_ok = sem("inv_ok"), sem("sum_ok"), sem("pooled_ok")
        NW = len(WINDOWS)

        uses = [("h", n) for n in range(2 * KO)] + [("v", t) for t in range(TT)]
        for g in range(NW):
            uses += [("u", 2 * g), ("u", 2 * g + 1)]
            if g:
                uses += [("mix", 2 * g - 2), ("mix", 2 * g - 1)]
        uses += [("mix", 2 * NW - 2), ("mix", 2 * NW - 1)]
        at = {use: n for n, use in enumerate(uses)}

        with nc.Block() as block:

            @block.sync
            def _(sp):
                for t in range(TT):
                    sp.dma_start(X[:, t, :], x_tiles[:, t, :]).then_inc(x_in[t], 16)
                with nc.allow_non_contiguous_dma(reason="columns of a small vector"):
                    sp.dma_start(g_col[:], g_mix.rearrange("a (k p) -> p (a k)", p=P)).then_inc(cols_in, 16)
                    sp.dma_start(scale_col[:], pool_scale.rearrange("a (k p) -> p (a k)", p=P)).then_inc(cols_in, 16)
                sp.dma_start(w_v[:], w_in[0, :, 2 * QKV:3 * QKV].rearrange("(k p) n -> p k n", p=P)).then_inc(wv_in, 16)
                for g in range(NW):
                    if g:
                        sp.wait_ge(wu_lo_ok, g)
                    sp.dma_start(w_u, w_in[0, :, 3 * QKV + g * P:3 * QKV + (g + 1) * P]
                                 .rearrange("(k p) n -> p k n", p=P)).then_inc(wu_in, 16)
                    if g == 0:
                        sp.dma_start(pw, pool_w[0].rearrange("g c d -> c g d")).then_inc(pw_in, 16)

            @block.gpsimd
            def _(pool):
                nc.gpsimd.memset(k["ident"][:], 0.0).then_inc(ident_ok, 1)
                pool.wait_ge(ident_ok, 1)
                nc.gpsimd.affine_select(out=k["ident"][:], in_=k["ident"][:], compare_op=ALU.not_equal, fill=1.0,
                                        base=0, pattern=[[-1, P]], channel_multiplier=1).then_inc(ident_ok, 1)
                nc.gpsimd.iota(iota1[:], [[1, PAD]], base=1, channel_multiplier=0,
                               allow_small_or_imprecise_dtypes=True).then_inc(iota_ok, 1)
                pool.wait_ge(pe_bank, 2 * KO)
                for buf in (u, *sums):
                    last = nc.gpsimd.memset(buf[:, 0:PAD], 0.0)
                last.then_inc(pad_ok, 1)

            @block.scalar
            def _(act):
                def split_u(g):
                    act.wait_ge(wu_in, 16 * (g + 1))
                    if g:
                        act.wait_ge(pe_bank, at[("u", 2 * g - 1)] + 1)
                    nc.scalar.activation(wu_hi[:], w_u, ACT.Copy).then_inc(wu_hi_ok, 1)

                for t in range(TT):
                    act.wait_ge(x_in[t], 16)
                    if t:
                        act.wait_ge(sq_done, t)
                    nc.scalar.activation(square, X[:, t, :], ACT.Square, scale=D ** -0.5,
                                         accum_out=mean_sq[:, t:t + 1]).then_inc(sq_done, 1)
                act.wait_ge(mean_ok, 1)
                nc.scalar.activation(rms[:], mean_sq[:], ACT.Sqrt).then_inc(rms_ok, 1)
                act.wait_ge(cols_in, 32)
                for n, (kind, i) in enumerate(uses):
                    if (kind, i) == ("h", KO):
                        act.wait_ge(wv_in, 16)
                        nc.scalar.activation(wv_hi[:], w_v[:], ACT.Copy).then_inc(wv_hi_ok, 1)
                        split_u(0)
                    act.wait_ge(pe_bank, n + 1)
                    src = bank[n % 8]
                    if kind == "h":
                        half, ko = divmod(i, KO)
                        ins = nc.scalar.activation(h_hi[:, ko, half * HALF:(half + 1) * HALF], src[:], ACT.Copy,
                                                   scale=g_col[:, ko:ko + 1])
                    elif kind == "v":
                        ins = nc.scalar.activation(v_all[:, i, :], src[:], ACT.Copy)
                    elif kind == "u":
                        g, half = divmod(i, 2)
                        if half == 0:
                            if g == 0:
                                act.wait_ge(pad_ok, 1)
                            else:
                                act.wait_ge(pooled_ok, g)
                        ins = nc.scalar.activation(u[:, PAD + half * HALF:PAD + (half + 1) * HALF], src[:], ACT.Copy)
                    else:
                        g, half = divmod(i, 2)
                        ins = nc.scalar.activation(pool_T[:, g, half * HALF:(half + 1) * HALF], src[:],
                                                   ACT.Copy, scale=scale_col[:, g:g + 1])
                    ins.then_inc(act_read, 1)
                    if kind == "u" and i % 2 == 1 and i // 2 + 1 < NW:
                        split_u(i // 2 + 1)

            @block.vector
            def _(dve):
                def split_u(g):
                    dve.wait_ge(wu_hi_ok, g + 1)
                    nc.vector.tensor_tensor(wu_lo[:], w_u, wu_hi[:].bitcast(F32), ALU.subtract).then_inc(wu_lo_ok, 1)

                dve.wait_ge(sq_done, TT)
                nc.vector.tensor_scalar(mean_sq[:], mean_sq[:], EPS, None, ALU.add).then_inc(mean_ok, 1)
                dve.wait_ge(rms_ok, 1)
                nc.vector.reciprocal(rstd[:], rms[:]).then_inc(rstd_ok, 1)
                dve.wait_ge(rstd_ok, 1)
                for t in range(TT):
                    nc.vector.tensor_scalar(X[:, t, :], X[:, t, :], rstd[:, t:t + 1], None, ALU.mult).then_inc(x_scaled, 1)
                for n in range(2 * KO):
                    half, ko = divmod(n, KO)
                    at_ = (slice(None), ko, slice(half * HALF, (half + 1) * HALF))
                    dve.wait_ge(act_read, n + 1)
                    nc.vector.scalar_tensor_tensor(h_lo[at_], bank[n % 8][:], g_col[:, ko:ko + 1], h_hi[at_].bitcast(F32),
                                                   ALU.mult, ALU.subtract).then_inc(dve_read, 1)
                    if n == KO - 1:
                        dve.wait_ge(wv_hi_ok, 1)
                        nc.vector.tensor_tensor(wv_lo[:], w_v[:], wv_hi[:].bitcast(F32), ALU.subtract).then_inc(wv_lo_ok, 1)
                        split_u(0)
                dve.wait_ge(iota_ok, 1)
                for g, w in enumerate(WINDOWS):
                    if g:
                        dve.wait_ge(inv_ok, 2 * g)
                    nc.vector.tensor_scalar(count[:], iota1[:], float(w), None, ALU.min).then_inc(inv_ok, 1)
                    dve.wait_ge(inv_ok, 2 * g + 1)
                    nc.vector.reciprocal(inv[:, g, :], count[:]).then_inc(inv_ok, 1)
                dve.wait_ge(inv_ok, 2 * NW)
                dve.wait_ge(pad_ok, 1)
                done = 0
                for g, w in enumerate(WINDOWS):
                    dve.wait_ge(act_read, at[("u", 2 * g + 1)] + 1)
                    if g + 1 < NW:
                        split_u(g + 1)
                    src = u
                    for s in range(g + 1):
                        dst = sums[s % 2]
                        nc.vector.tensor_tensor(dst[:, PAD:], src[:, PAD:], src[:, PAD - 2 ** s:PAD + T - 2 ** s],
                                                ALU.add).then_inc(sum_ok, 1)
                        done += 1
                        dve.wait_ge(sum_ok, done)
                        src = dst
                    if g:
                        dve.wait_ge(pe_bank, at[("mix", 2 * g - 1)] + 1)
                    nc.vector.scalar_tensor_tensor(pooled, src[:, PAD:], 1.0 / w, u[:, PAD:], ALU.mult,
                                                   ALU.subtract).then_inc(sum_ok, 1)
                    dve.wait_ge(sum_ok, done + 1)
                    nc.vector.tensor_tensor(src[:, PAD:2 * PAD], src[:, PAD:2 * PAD], inv[:, g, :], ALU.mult).then_inc(sum_ok, 1)
                    done += 2
                    dve.wait_ge(sum_ok, done)
                    nc.vector.tensor_tensor(pooled[:, 0:PAD], src[:, PAD:2 * PAD], u[:, PAD:2 * PAD],
                                            ALU.subtract).then_inc(pooled_ok, 1)
                    dve.wait_ge(pooled_ok, g + 1)

            @block.tensor
            def _(pe):
                pe.wait_ge(ident_ok, 2)
                for n, (kind, i) in enumerate(uses):
                    dst = bank[n % 8]
                    if n >= 8:
                        if n - 8 < 2 * KO:
                            pe.wait_ge(dve_read, n - 7)
                        else:
                            pe.wait_ge(act_read, n - 7)
                    if kind == "h":
                        half, ko = divmod(i, KO)
                        pe.wait_ge(x_scaled, 4 * (half + 1))
                        for t in range(4):
                            ins = nc.tensor.transpose(dst[:, t * P:(t + 1) * P],
                                                      X[:, 4 * half + t, ko * P:(ko + 1) * P], k["ident"][:])
                    elif kind == "v":
                        if i == 0:
                            pe.wait_ge(wv_lo_ok, 1)
                            pe.wait_ge(dve_read, 2 * KO)
                        tile = (slice(None), slice(i * P, (i + 1) * P))
                        for ko in range(KO):
                            ins = three_passes(nc, dst[:], [h[:, ko, tile[1]] for h in (h_hi, h_lo)],
                                               [w[:, ko, :] for w in (wv_hi, wv_lo)], ko == 0, ko == KO - 1)
                    elif kind == "u":
                        g, half = divmod(i, 2)
                        pe.wait_ge(wu_lo_ok, g + 1)
                        for ko in range(KO):
                            ins = three_passes(nc, dst[:], [w[:, ko, :] for w in (wu_hi, wu_lo)],
                                               [h[:, ko, half * HALF:(half + 1) * HALF] for h in (h_hi, h_lo)],
                                               ko == 0, ko == KO - 1)
                    else:
                        g, half = divmod(i, 2)
                        pe.wait_ge(pw_in, 16)
                        pe.wait_ge(pooled_ok, g + 1)
                        ins = nc.tensor.matmul(dst[:], pw[:, g, :], pooled[:, half * HALF:(half + 1) * HALF],
                                               start=True, stop=True)
                    ins.then_inc(pe_bank, 1)


def attend(nc, k, w_in, h_hi, h_lo, v_all, attn):
    UNITS = 2 * TT
    USES = 2 + UNITS
    groups = [(u, g) for u in range(UNITS) for g in range((u // 2) // 4 + 1)]
    first_group = {u: next(n for n, (v, _) in enumerate(groups) if v == u) for u in range(UNITS)}
    n_groups = {u: (u // 2) // 4 + 1 for u in range(UNITS)}
    G = len(groups)
    WT = 6
    BETA = 4
    TP_AHEAD = G
    AV_AHEAD = WT
    assert USES % 2 == 0 and G % WT == 0 and UNITS % BETA == 0
    with ExitStack() as c:
        sb = lambda n, s, d=F32: c.enter_context(nc.sbuf_tensor(n, s, d))
        ps = lambda n, s: c.enter_context(nc.psum_tensor(n, s, F32))
        sem = lambda n: c.enter_context(nc.semaphore(n))
        w_qk = sb("w_qk", [P, 2, KO, P])
        wq_hi, wq_lo = sb("wq_hi", [P, 2, KO, P], F32R), sb("wq_lo", [P, 2, KO, P], F32R)
        qT, kT = sb("qT", [P, T]), sb("kT", [P, T])
        beta = [sb(f"beta{i}", [P, T]) for i in range(BETA)]
        stay = [sb(f"stay{i}", [P, T]) for i in range(2)]
        prod = [sb(f"prod{i}", [P, T + 1]) for i in range(2)]
        wT = [sb(f"wT{i}", [P, HALF]) for i in range(WT)]
        wide = [ps(f"wide{i}", [P, T]) for i in range(2)]
        tp = [ps(f"tp{i}", [P, HALF]) for i in range(2)]
        av = [ps(f"av{i}", [P, HD]) for i in range(2)]
        w_qk_in, wq_hi_ok, wq_lo_ok = sem("w_qk_in"), sem("wq_hi_ok"), sem("wq_lo_ok")
        wide_full, wide_free = sem("wide_full"), sem("wide_free")
        one_ok, mask_ok, scan_ok, weight_ok = (sem(n) for n in ("one_ok", "mask_ok", "scan_ok", "weight_ok"))
        tp_full, tp_read, av_group, av_full, av_read = (sem(n) for n in ("tp_full", "tp_read", "av_group", "av_full", "av_read"))
        pool_turn = sem("pool_turn")

        with nc.Block() as block:

            @block.sync
            def _(sp):
                def load(hp):
                    for i in range(2):
                        sp.dma_start(w_qk[:, i], w_in[0, :, bass.ds(i * QKV + hp * P, P)]
                                     .rearrange("(k p) n -> p k n", p=P)).then_inc(w_qk_in, 16)
                load(0)
                with sp.Fori(0, PAIRS - 1) as hp:
                    sp.wait_ge(wq_lo_ok, hp + 1)
                    load(hp + 1)

            @block.scalar
            def _(act):
                act.sem_inc(wide_free, 2)

                def split(hp):
                    act.wait_ge(w_qk_in, 32 * hp + 32)
                    nc.scalar.activation(wq_hi[:], w_qk[:], ACT.Copy).then_inc(wq_hi_ok, 1)

                split(0)

                def body(hp, last):
                    for i, dst in enumerate((qT, kT)):
                        act.wait_ge(wide_full, USES * hp + i + 1)
                        nc.scalar.activation(dst[:], wide[i][:], ACT.Copy,
                                             scale=HD ** -0.5 if i == 0 else 1.0).then_inc(wide_free, 1)

                    def sigmoids(u):
                        w = (u // 2 + 1) * P
                        v = u - BETA
                        ahead = first_group[v % UNITS] + n_groups[v % UNITS] - (0 if v >= 0 else G)
                        act.wait_ge(tp_full, G * hp + TP_AHEAD + ahead)
                        act.wait_ge(wide_full, USES * hp + 2 + u + 1)
                        if u >= 2:
                            act.wait_ge(scan_ok, UNITS * hp + u - 1)
                        nc.scalar.activation(stay[u % 2][:, 0:w], wide[u % 2][:, 0:w], ACT.Sigmoid, scale=-1.0)
                        nc.scalar.activation(beta[u % BETA][:, 0:w], wide[u % 2][:, 0:w], ACT.Sigmoid).then_inc(wide_free, 1)

                    def copies(u):
                        for g in range(n_groups[u]):
                            n = first_group[u] + g
                            wk = min(4, u // 2 + 1 - 4 * g) * P
                            act.wait_ge(tp_full, G * hp + TP_AHEAD + n + 1)
                            act.wait_ge(av_group, G * hp + AV_AHEAD + n - WT + 1)
                            nc.scalar.activation(wT[n % WT][:, 0:wk], tp[n % 2][:, 0:wk], ACT.Copy).then_inc(tp_read, 1)

                    sigmoids(0)
                    sigmoids(1)
                    for u in range(UNITS):
                        if u + 2 < UNITS:
                            sigmoids(u + 2)
                        if u == 4 and not last:
                            split(hp + 1)
                        copies(u)

                with act.Fori(0, PAIRS - 1) as hp:
                    body(hp, False)
                body(PAIRS - 1, True)

            @block.gpsimd
            def _(pool):
                for i in range(2):
                    last = nc.gpsimd.memset(prod[i][:, T:T + 1], 1.0)
                last.then_inc(one_ok, 1)
                with pool.Fori(0, PAIRS) as hp:
                    for u in range(UNITS):
                        i = u // 2
                        pool.wait_ge(wide_free, USES * hp + 2 + 2 + u + 1)
                        pool.sem_inc(pool_turn, 1)
                        for buf, fill in ((stay[u % 2], 1.0), (beta[u % BETA], 0.0)):
                            tile = buf[:, i * P:(i + 1) * P]
                            nc.gpsimd.affine_select(out=tile, in_=tile, compare_op=ALU.is_gt, fill=fill, base=0,
                                                    pattern=[[-1, P]], channel_multiplier=1).then_inc(mask_ok, 1)

            @block.vector
            def _(dve):
                dve.wait_ge(one_ok, 1)

                def split(hp):
                    dve.wait_ge(wq_hi_ok, hp + 1)
                    nc.vector.tensor_tensor(wq_lo[:], w_qk[:], wq_hi[:].bitcast(F32), ALU.subtract).then_inc(wq_lo_ok, 1)

                split(0)

                def body(hp, last):
                    def take(u):
                        dve.wait_ge(av_full, UNITS * hp + u + 1)
                        nc.vector.tensor_copy(attn[:, u // 2, bass.ds(hp * P + (u % 2) * HD, HD)],
                                              av[u % 2][:]).then_inc(av_read, 1)

                    for u in range(UNITS):
                        w = (u // 2 + 1) * P
                        dve.wait_ge(mask_ok, 2 * UNITS * hp + 2 * u + 1)
                        nc.vector.tensor_tensor_scan(prod[u % 2][:, T - w:T][:, ::-1], stay[u % 2][:, 0:w][:, ::-1],
                                                     stay[u % 2][:, 0:w][:, ::-1], 1.0, ALU.mult,
                                                     ALU.bypass).then_inc(scan_ok, 1)
                        dve.wait_ge(scan_ok, UNITS * hp + u + 1)
                        dve.wait_ge(mask_ok, 2 * UNITS * hp + 2 * u + 2)
                        nc.vector.tensor_tensor(beta[u % BETA][:, 0:w], beta[u % BETA][:, 0:w],
                                                prod[u % 2][:, T - w + 1:T + 1], ALU.mult).then_inc(weight_ok, 1)
                        if u == 5 and not last:
                            split(hp + 1)
                        if u >= 2:
                            take(u - 2)
                    take(UNITS - 2)
                    take(UNITS - 1)

                with dve.Fori(0, PAIRS - 1) as hp:
                    body(hp, False)
                body(PAIRS - 1, True)

            @block.tensor
            def _(pe):
                pe.sem_inc(tp_full, TP_AHEAD)
                pe.sem_inc(av_group, AV_AHEAD)
                with pe.Fori(0, PAIRS) as hp:
                    pe.wait_ge(wq_lo_ok, hp + 1)
                    for i in range(2):
                        pe.wait_ge(wide_free, USES * hp + i + 1)
                        for half in range(2):
                            cols = slice(half * HALF, (half + 1) * HALF)
                            for ko in range(KO):
                                ins = three_passes(nc, wide[i][:, cols], [w[:, i, ko, :] for w in (wq_hi, wq_lo)],
                                                   [h[:, ko, cols] for h in (h_hi, h_lo)], ko == 0, ko == KO - 1)
                        ins.then_inc(wide_full, 1)
                    pe.wait_ge(wide_free, USES * hp + 2 + 2)

                    def scores(u):
                        i, h = divmod(u, 2)
                        w = (i + 1) * P
                        pe.wait_ge(wide_free, USES * hp + 2 + u + 1)
                        for a in range(0, w, HALF):
                            b = min(w, a + HALF)
                            ins = nc.tensor.matmul(wide[u % 2][:, a:b], qT[h * HD:(h + 1) * HD, i * P:(i + 1) * P],
                                                   kT[h * HD:(h + 1) * HD, a:b], start=True, stop=True)
                        ins.then_inc(wide_full, 1)

                    def transposes(u):
                        pe.wait_ge(weight_ok, UNITS * hp + u + 1)
                        for g in range(n_groups[u]):
                            n = first_group[u] + g
                            if n >= 2:
                                pe.wait_ge(tp_read, G * hp + n - 1)
                            for kb in range(4 * g, min(4 * g + 4, u // 2 + 1)):
                                ins = nc.tensor.transpose(tp[n % 2][:, (kb % 4) * P:(kb % 4 + 1) * P],
                                                          beta[u % BETA][:, kb * P:(kb + 1) * P], k["ident"][:])
                            ins.then_inc(tp_full, 1)

                    def values(u):
                        i, h = divmod(u, 2)
                        if u >= 2:
                            pe.wait_ge(av_read, UNITS * hp + u - 1)
                        for g in range(n_groups[u]):
                            n = first_group[u] + g
                            pe.wait_ge(tp_read, G * hp + n + 1)
                            for kb in range(4 * g, min(4 * g + 4, i + 1)):
                                ins = nc.tensor.matmul(av[u % 2][:], wT[n % WT][:, (kb % 4) * P:(kb % 4 + 1) * P],
                                                       v_all[:, kb, bass.ds(hp * P + h * HD, HD)],
                                                       start=kb == 0, stop=kb == i)
                            if g < n_groups[u] - 1:
                                ins.then_inc(av_group, 1)
                            else:
                                ins.then_inc(av_full, 1)
                        pe.wait_ge(av_full, UNITS * hp + u + 1)
                        pe.sem_inc(av_group, 1)

                    scores(0)
                    scores(1)
                    for u in range(UNITS):
                        if u + 2 < UNITS:
                            scores(u + 2)
                        transposes(u)
                        if u:
                            values(u - 1)
                    values(UNITS - 1)
                    pe.wait_ge(av_read, UNITS * hp + UNITS)


def project_out(nc, k, x_tiles, g_moe, w_out, w_router, b_router, attn, pool_T, h_rows):
    with ExitStack() as c:
        sb = lambda n, s, d=F32: c.enter_context(nc.sbuf_tensor(n, s, d))
        ps = lambda n, s: c.enter_context(nc.psum_tensor(n, s, F32))
        sem = lambda n: c.enter_context(nc.semaphore(n))
        RAW_W = 4
        KH = KO // 2
        w_raw = [sb(f"w_raw{i}", [P, D]) for i in range(RAW_W)]
        wo_hi, wo_lo = sb("wo_hi", [P, KO, D], F32R), sb("wo_lo", [P, KO, D], F32R)
        m_hi = [sb(f"m_hi{i}", [P, KO, P], F32R) for i in range(2)]
        m_lo = [sb(f"m_lo{i}", [P, KO, P], F32R) for i in range(2)]
        X = k["x2"]
        H = [sb(f"H{i}", [P, D]) for i in range(2)]
        hT2 = [sb(f"hT2{i}", [P, KO, P]) for i in range(2)]
        junk = sb("junk", [P, D])
        g_row = sb("g_row", [P, D])
        w_r, b_r = sb("w_r", [P, KO, E_]), sb("b_r", [P, E_])
        ms, rms, rstd = sb("ms", [P, TT]), sb("rms2", [P, TT]), sb("rstd2", [P, TT])
        op = [[ps(f"op{i}{j}", [P, HALF]) for j in range(2)] for i in range(2)]
        xp = [ps(f"xp{i}", [P, HALF]) for i in range(2)]
        mt = ps("mt", [P, HALF])
        lp = ps("lp", [P, TT, E_])
        x_in, row_in = [sem(f"x_in2{i}") for i in range(TT)], sem("row_in")
        w_in_ = [sem(f"wo_in{i}") for i in range(RAW_W)]
        wo_hi_ok, wo_lo_ok = sem("wo_hi_ok"), sem("wo_lo_ok")
        mt_full, m_hi_ok, m_lo_ok = sem("mt_full"), sem("m_hi_ok"), sem("m_lo_ok")
        proj_ok, res_ok, ms_ok, ms2_ok, rms_ok, rstd_ok, h_ok = (
            sem(n) for n in ("proj_ok", "res_ok", "ms_ok", "ms2_ok", "rms_ok2", "rstd_ok2", "h_ok"))
        h_out = [sem("h_out0"), sem("h_out1")]
        xp_full, xp_read, lg_full, lg_ok = sem("xp_full"), sem("xp_read"), sem("lg_full"), sem("lg_ok")

        with nc.Block() as block:

            @block.sync
            def _(sp):
                for ko in range(KO):
                    if ko >= RAW_W:
                        sp.wait_ge(wo_lo_ok, ko - RAW_W + 1)
                    sp.dma_start(w_raw[ko % RAW_W][:], w_out[0, ko * P:(ko + 1) * P, :]).then_inc(w_in_[ko % RAW_W], 16)
                for t in range(TT):
                    sp.dma_start(X[:, t, :], x_tiles[:, t, :]).then_inc(x_in[t], 16)
                sp.dma_start(g_row[:], g_moe.to_broadcast([P, D])).then_inc(row_in, 16)
                sp.dma_start(b_r[:], b_router.to_broadcast([P, E_])).then_inc(row_in, 16)
                sp.dma_start(w_r[:], w_router[0].rearrange("(k p) e -> p k e", p=P)).then_inc(row_in, 16)
                for t in range(TT):
                    sp.wait_ge(h_ok, t + 1)
                    sp.dma_start(h_rows[t * P:(t + 1) * P, :], H[t % 2][:]).then_inc(h_out[t % 2], 16)
                for stored in h_out:
                    sp.wait_ge(stored, 16 * TT // 2)

            @block.scalar
            def _(act):
                def mixed_high(t):
                    act.wait_ge(mt_full, t + 1)
                    if t >= 2:
                        act.wait_ge(proj_ok, t - 1)
                    nc.scalar.activation(m_hi[t % 2][:, 0:KH, :], mt[:].rearrange("p (k t) -> p k t", t=P), ACT.Copy)
                    nc.scalar.activation(m_hi[t % 2][:, KH:KO, :], pool_T[:, :, t * P:(t + 1) * P],
                                         ACT.Copy).then_inc(m_hi_ok, 1)

                mixed_high(0)
                for ko in range(KO):
                    act.wait_ge(w_in_[ko % RAW_W], 16 * (ko // RAW_W + 1))
                    nc.scalar.activation(wo_hi[:, ko, :], w_raw[ko % RAW_W][:], ACT.Copy).then_inc(wo_hi_ok, 1)
                mixed_high(1)
                for t in range(TT):
                    if t + 2 < TT:
                        mixed_high(t + 2)
                    act.wait_ge(ms2_ok, t + 1)
                    nc.scalar.activation(rms[:, t:t + 1], ms[:, t:t + 1], ACT.Sqrt).then_inc(rms_ok, 1)
                    for g in range(2):
                        act.wait_ge(xp_full, 2 * t + g + 1)
                        if t >= 2:
                            act.wait_ge(lg_full, t - 1)
                        nc.scalar.activation(hT2[t % 2][:, 4 * g:4 * g + 4, :].rearrange("p k t -> p (k t)"), xp[g][:],
                                             ACT.Copy).then_inc(xp_read, 1)

            @block.tensor
            def _(pe):
                def mixed_transposes(t):
                    if t:
                        pe.wait_ge(m_lo_ok, t)
                    for ko in range(KH):
                        ins = nc.tensor.transpose(mt[:, ko * P:(ko + 1) * P], attn[:, t, ko * P:(ko + 1) * P], k["ident"][:])
                    ins.then_inc(mt_full, 1)

                def products(t):
                    pe.wait_ge(m_lo_ok, t + 1)
                    if t >= 2:
                        pe.wait_ge(res_ok, 2 * t - 2)
                    for half in range(2):
                        for ko in range(KO):
                            if t == 0 and half == 0:
                                pe.wait_ge(wo_lo_ok, ko + 1)
                            ins = three_passes(nc, op[t % 2][half][:], [m[t % 2][:, ko, :] for m in (m_hi, m_lo)],
                                               [w[:, ko, half * HALF:(half + 1) * HALF] for w in (wo_hi, wo_lo)],
                                               ko == 0, ko == KO - 1)
                    ins.then_inc(proj_ok, 1)

                mixed_transposes(0)
                mixed_transposes(1)
                products(0)
                for t in range(TT):
                    if t + 2 < TT:
                        mixed_transposes(t + 2)
                    if t + 1 < TT:
                        products(t + 1)
                    pe.wait_ge(h_ok, t + 1)
                    for g in range(2):
                        if t:
                            pe.wait_ge(xp_read, 2 * t + g - 1)
                        for i in range(4):
                            ins = nc.tensor.transpose(xp[g][:, i * P:(i + 1) * P],
                                                      H[t % 2][:, (4 * g + i) * P:(4 * g + i + 1) * P], k["ident"][:])
                        ins.then_inc(xp_full, 1)
                    pe.wait_ge(xp_read, 2 * t + 2)
                    if t == 0:
                        pe.wait_ge(row_in, 48)
                    for ko in range(KO):
                        ins = nc.tensor.matmul(lp[:, t, :], hT2[t % 2][:, ko, :], w_r[:, ko, :],
                                               start=ko == 0, stop=ko == KO - 1)
                    ins.then_inc(lg_full, 1)

            @block.vector
            def _(dve):
                def mixed_low(t):
                    dve.wait_ge(m_hi_ok, t + 1)
                    nc.vector.tensor_tensor(m_lo[t % 2][:, 0:KH, :], mt[:].rearrange("p (k t) -> p k t", t=P),
                                            m_hi[t % 2][:, 0:KH, :].bitcast(F32), ALU.subtract)
                    nc.vector.tensor_tensor(m_lo[t % 2][:, KH:KO, :], pool_T[:, :, t * P:(t + 1) * P],
                                            m_hi[t % 2][:, KH:KO, :].bitcast(F32), ALU.subtract).then_inc(m_lo_ok, 1)

                mixed_low(0)
                for ko in range(KO):
                    dve.wait_ge(wo_hi_ok, ko + 1)
                    nc.vector.tensor_tensor(wo_lo[:, ko, :], w_raw[ko % RAW_W][:], wo_hi[:, ko, :].bitcast(F32),
                                            ALU.subtract).then_inc(wo_lo_ok, 1)
                mixed_low(1)
                for t in range(TT):
                    x2 = X[:, t, :]
                    dve.wait_ge(proj_ok, t + 1)
                    dve.wait_ge(x_in[t], 16)
                    if t == 0:
                        dve.wait_ge(row_in, 48)
                    for half in range(2):
                        tile = x2[:, half * HALF:(half + 1) * HALF]
                        nc.vector.tensor_tensor(tile, op[t % 2][half][:], tile, ALU.add).then_inc(res_ok, 1)
                    dve.wait_ge(res_ok, 2 * t + 2)
                    if t:
                        dve.wait_ge(ms_ok, t)
                    nc.vector.scalar_tensor_tensor(junk[:], x2, 1.0 / D, x2, ALU.mult, ALU.mult,
                                                   accum_out=ms[:, t:t + 1]).then_inc(ms_ok, 1)
                    dve.wait_ge(ms_ok, t + 1)
                    nc.vector.tensor_scalar(ms[:, t:t + 1], ms[:, t:t + 1], EPS, None, ALU.add).then_inc(ms2_ok, 1)
                    if t + 2 < TT:
                        mixed_low(t + 2)
                    dve.wait_ge(rms_ok, t + 1)
                    nc.vector.reciprocal(rstd[:, t:t + 1], rms[:, t:t + 1]).then_inc(rstd_ok, 1)
                    dve.wait_ge(rstd_ok, t + 1)
                    if t >= 2:
                        dve.wait_ge(xp_full, 2 * (t - 1))
                        dve.wait_ge(h_out[t % 2], 16 * (t // 2))
                    nc.vector.scalar_tensor_tensor(H[t % 2][:], x2, rstd[:, t:t + 1], g_row[:], ALU.mult,
                                                   ALU.mult).then_inc(h_ok, 1)
                dve.wait_ge(lg_full, TT)
                nc.vector.tensor_tensor(k["logits"][:], lp[:], b_r[:, None, :].to_broadcast([P, TT, E_]), ALU.add).then_inc(lg_ok, 1)


def route(nc, k, w_gate_up, w_down, b_gate_up, b_down, raw, raw_in):
    with ExitStack() as c:
        sb = lambda n, s, d=F32: c.enter_context(nc.sbuf_tensor(n, s, d))
        ps = lambda n, s: c.enter_context(nc.psum_tensor(n, s, F32))
        sem = lambda n: c.enter_context(nc.semaphore(n))
        bias_rows = sb("bias_rows", [E_, 3 * D])
        logits = k["logits"]
        top, top_i = sb("top", [P, TT, 8]), sb("top_i", [P, TT, 8], U32)
        top_f = sb("top_f", [P, TT, K_])
        ex, den, rden = sb("ex", [P, TT, K_]), sb("den", [P, TT]), sb("rden", [P, TT])
        iota_e = sb("iota_e", [P, E_])
        iota_b = sb("iota_b", [P, TABLE])
        hot = sb("hot", [P, TT, K_, E_])
        mask = sb("mask", [P, TT, E_])
        mask_b = sb("mask_b", [P, TT, E_], BF16)
        before, ones = sb("before", [P, P], BF16), sb("ones", [P, P], BF16)
        steps = sb("steps", [P, MAX_BLOCKS_PER_EXPERT])
        over = sb("over", [P, E_, MAX_BLOCKS_PER_EXPERT])
        cnt, nb, nb_end, base = (sb(n, [P, E_]) for n in ("cnt", "nb", "nb_end", "base"))
        rank, where = sb("rank", [P, TT, E_]), sb("where", [P, TT, E_])
        picked = sb("picked", [P, TT, K_, E_])
        dest_f = sb("dest_f", [P, TT, K_])
        le, le_nb = sb("le", [P, TABLE, E_]), sb("le_nb", [P, TABLE, E_])
        be_f, done_b, first_row = sb("be_f", [P, TABLE]), sb("done_b", [P, TABLE]), sb("first_row", [P, TABLE])
        rp = ps("rp", [P, TT + 1, E_])
        bp = [ps(f"bp{i}", [P, HALF]) for i in range(2)]
        const_ok, b_in, bias_full, bias_ok = sem("const_ok"), sem("b_in"), sem("bias_full"), sem("bias_ok")
        mask_ok, rank_full, ex_in, ex_ok, step = (sem(n) for n in ("mask_ok2", "rank_full", "ex_in", "ex_ok", "step"))

        with nc.Block() as block:

            @block.sync
            def _(sp):
                sp.dma_start(bias_rows[:, 0:2 * D], b_gate_up[0]).then_inc(b_in, 16)
                sp.dma_start(bias_rows[:, 2 * D:3 * D], b_down[0]).then_inc(b_in, 16)
                for c_ in range(RAW):
                    sp.dma_start(raw[c_][:], chunk_source(w_gate_up, w_down, c_, 0)).then_inc(raw_in[c_], 16)
                sp.wait_ge(b_in, 32)

            @block.gpsimd
            def _(pool):
                iota = lambda o, pattern, base, cm: nc.gpsimd.iota(o, pattern, base=base, channel_multiplier=cm,
                                                                   allow_small_or_imprecise_dtypes=True)
                iota(iota_e[:], [[1, E_]], 0, 0)
                iota(iota_b[:], [[1, TABLE]], 0, 0)
                iota(steps[:], [[SLOTS, MAX_BLOCKS_PER_EXPERT]], 0, 0)
                iota(k["token_of"][:, :, 0], [[P, TT]], 0, 0)
                iota(k["token_of"][:, :, 1], [[0, TT]], 0, 1)
                nc.gpsimd.memset(ones[:], 1.0)
                nc.gpsimd.memset(before[:], 1.0).then_inc(const_ok, 1)
                pool.wait_ge(const_ok, 1)
                nc.gpsimd.memset(steps[:, 0:1], -1.0)
                nc.gpsimd.affine_select(out=before[:], in_=before[:], compare_op=ALU.is_gt, fill=0.0, base=0,
                                        pattern=[[1, P]], channel_multiplier=-1).then_inc(const_ok, 1)

            @block.scalar
            def _(act):
                act.wait_ge(ex_in, 1)
                nc.scalar.activation(ex[:], ex[:], ACT.Exp).then_inc(ex_ok, 1)
                act.wait_ge(bias_full, 1)
                nc.scalar.activation(k["bias_gu"][:].rearrange("p m e -> p (m e)"), bp[0][:], ACT.Copy)
                nc.scalar.activation(k["bias_dn"][:].rearrange("p m e -> p (m e)"), bp[1][:, 0:E_ * D // P],
                                     ACT.Copy).then_inc(bias_ok, 1)

            @block.tensor
            def _(pe):
                pe.wait_ge(mask_ok, 1)
                pe.wait_ge(const_ok, 2)
                for t in range(TT + 1):
                    for j in range(min(t + 1, TT)):
                        ins = nc.tensor.matmul(rp[:, t, :], before[:] if j == t else ones[:], mask_b[:, j, :],
                                               start=j == 0, stop=j == min(t, TT - 1))
                ins.then_inc(rank_full, 1)
                pe.wait_ge(b_in, 32)
                for m in range(3 * D // P):
                    ins = nc.tensor.transpose(bp[m // 16][:, (m % 16) * E_:(m % 16 + 1) * E_],
                                              bias_rows[:, m * P:(m + 1) * P], k["ident"][0:E_, 0:E_])
                ins.then_inc(bias_full, 1)

            @block.vector
            def _(dve):
                count = [0]

                def mark(ins):
                    count[0] += 1
                    ins.then_inc(step, 1)

                def done(ins):
                    mark(ins)
                    dve.wait_ge(step, count[0])

                dve.wait_ge(const_ok, 2)
                for t in range(TT):
                    mark(nc.vector.max(top[:, t, :], logits[:, t, :]))
                dve.wait_ge(step, count[0])
                for t in range(TT):
                    mark(nc.vector.max_index(top_i[:, t, :], top[:, t, :], logits[:, t, :]))
                nc.vector.tensor_tensor(ex[:], top[:, :, 0:K_], top[:, :, 0:1].to_broadcast([P, TT, K_]),
                                        ALU.subtract).then_inc(ex_in, 1)
                dve.wait_ge(step, count[0])
                done(nc.vector.tensor_copy(top_f[:], top_i[:, :, 0:K_]))
                done(nc.vector.tensor_tensor(hot[:].rearrange("p t k e -> p (t k) e"),
                                             iota_e[:, None, :].to_broadcast([P, TT * K_, E_]),
                                             top_f[:].rearrange("p t k -> p (t k)")[:, :, None].to_broadcast([P, TT * K_, E_]),
                                             ALU.is_equal))
                done(nc.vector.tensor_reduce(mask[:], hot[:].rearrange("p t k e -> p t e k"), AX.X, ALU.add))
                nc.vector.tensor_copy(mask_b[:], mask[:]).then_inc(mask_ok, 1)
                dve.wait_ge(rank_full, 1)
                mark(nc.vector.tensor_copy(rank[:], rp[:, 0:TT, :]))
                done(nc.vector.tensor_copy(cnt[:], rp[:, TT, :]))
                mark(nc.vector.tensor_tensor_scan(base[:], cnt[:], cnt[:], 0.0, ALU.add, ALU.bypass))
                done(nc.vector.tensor_tensor(over[:], cnt[:, :, None].to_broadcast([P, E_, MAX_BLOCKS_PER_EXPERT]),
                                             steps[:, None, :].to_broadcast([P, E_, MAX_BLOCKS_PER_EXPERT]), ALU.is_gt))
                done(nc.vector.tensor_reduce(nb[:], over[:], AX.X, ALU.add))
                mark(nc.vector.tensor_tensor_scan(nb_end[:], nb[:], nb[:], 0.0, ALU.add, ALU.bypass))
                done(nc.vector.scalar_tensor_tensor(where[:], rank[:], 1.0, mask[:], ALU.add, ALU.mult))
                mark(nc.vector.tensor_scalar(k["ranks"][:], where[:], -1.0, None, ALU.add))
                mark(nc.vector.tensor_scalar(k["last_block"][:], nb_end[:, E_ - 1:E_], -1.0, None, ALU.add))
                mark(nc.vector.tensor_tensor(base[:], base[:], cnt[:], ALU.subtract))
                done(nc.vector.tensor_tensor(le[:], nb_end[:, None, :].to_broadcast([P, TABLE, E_]),
                                             iota_b[:, :, None].to_broadcast([P, TABLE, E_]), ALU.is_le))
                mark(nc.vector.tensor_reduce(be_f[:], le[:], AX.X, ALU.add))
                mark(nc.vector.tensor_tensor(le_nb[:], le[:], nb[:, None, :].to_broadcast([P, TABLE, E_]), ALU.mult))
                done(nc.vector.tensor_tensor(where[:], rank[:], base[:, None, :].to_broadcast([P, TT, E_]), ALU.add))
                mark(nc.vector.tensor_reduce(done_b[:], le_nb[:], AX.X, ALU.add))
                mark(nc.vector.tensor_tensor(le[:], le[:], cnt[:, None, :].to_broadcast([P, TABLE, E_]), ALU.mult))
                for t in range(TT):
                    mark(nc.vector.tensor_tensor(picked[:, t], hot[:, t], where[:, t, None, :].to_broadcast([P, K_, E_]), ALU.mult))
                done(nc.vector.tensor_scalar(k["block_expert"][:], be_f[:], float(E_ - 1), None, ALU.min))
                done(nc.vector.tensor_tensor(done_b[:], iota_b[:], done_b[:], ALU.subtract))
                mark(nc.vector.tensor_reduce(first_row[:], le[:], AX.X, ALU.add))
                done(nc.vector.tensor_scalar(k["block_first"][:], done_b[:], float(SLOTS), None, ALU.mult))
                done(nc.vector.tensor_reduce(dest_f[:], picked[:], AX.X, ALU.add))
                done(nc.vector.tensor_tensor(first_row[:], first_row[:], k["block_first"][:], ALU.add))
                mark(nc.vector.tensor_copy(k["block_row"][:], first_row[:]))
                mark(nc.vector.tensor_tensor(k["block_tokens"][:, 0:TABLE - 1], first_row[:, 1:TABLE],
                                             first_row[:, 0:TABLE - 1], ALU.subtract))
                done(nc.vector.tensor_copy(k["dest"][:], dest_f[:]))
                dve.wait_ge(ex_ok, 1)
                done(nc.vector.tensor_reduce(den[:], ex[:], AX.X, ALU.add))
                done(nc.vector.reciprocal(rden[:], den[:]))
                done(nc.vector.tensor_tensor(k["gates"][:], ex[:], rden[:, :, None].to_broadcast([P, TT, K_]), ALU.mult))


def chunk_source(w_gate_up, w_down, c_, e):
    if c_ < 2 * PAIR_CHUNKS:
        col = (c_ % 2) * D + (c_ // 2) * CC
        src = w_gate_up[0, bass.ds(e, 1), :, col:col + CC]
    else:
        src = w_down[0, bass.ds(e, 1), :, (c_ - 2 * PAIR_CHUNKS) * CC:(c_ - 2 * PAIR_CHUNKS + 1) * CC]
    return src.rearrange("a (k p) n -> p (a k) n", p=P)


def experts(nc, k, w_gate_up, w_down, h_rows, y_rows, raw, raw_in):
    with ExitStack() as c:
        sb = lambda n, s, d=F32: c.enter_context(nc.sbuf_tensor(n, s, d))
        ps = lambda n, s: c.enter_context(nc.psum_tensor(n, s, F32))
        sem = lambda n: c.enter_context(nc.semaphore(n))
        w_hi = [sb(f"w_hi{i}", [P, KO, CC], F32R) for i in range(SPLIT)]
        w_lo = [sb(f"w_lo{i}", [P, KO, CC], F32R) for i in range(SPLIT)]
        rows = [sb(f"rows{i}", [n, D]) for i, n in enumerate(SEG)]
        x_s = sb("x_s", [P, KO, 2, SLOTS], F32R)
        a_s = sb("a_s", [P, KO, 2, SLOTS], F32R)
        half = [sb(f"half{i}", [P, SLOTS]) for i in range(BANKS)]
        gate = [sb(f"gate{i}", [P, MC, SLOTS]) for i in range(2)]
        sig = [sb(f"sig{i}", [P, MC, SLOTS]) for i in range(2)]
        up = [sb(f"up{i}", [P, MC, SLOTS]) for i in range(2)]
        glu = [sb(f"glu{i}", [P, MC, SLOTS]) for i in range(2)]
        y_col = [sb(f"y_col{i}", [P, MC, SLOTS]) for i in range(2)]
        y_st = [sb(f"y_st{i}", [n, D]) for i, n in enumerate(SEG)]
        rank_cur = sb("rank_cur", [P, TT], BF16)
        slot_no = sb("slot_no", [P, SLOTS], BF16)
        hot = sb("hot_slot", [P, TT, SLOTS], BF16)
        idx = sb("idx", [P, 2], I32)
        b_gu, b_dn = sb("b_gu", [P, 2 * D // P]), sb("b_dn", [P, D // P])
        mm = [ps(f"mm{i}", [P, 2, SLOTS]) for i in range(BANKS)]
        xt = [ps(f"xt{i}", [P, HALF]) for i in range(3)]
        yt = ps("yt", [P, 2, CC])
        LIST = HALF - 8

        hi_done, lo_done, mm_done = sem("hi_done"), sem("lo_done"), sem("mm_done")
        half_ok, sum_ok = sem("half_ok"), sem("sum_ok3")
        gate_ok, up_ok, sig_ok, pre_ok, glu_ok, a_hi_ok, a_lo_ok = (
            sem(n) for n in ("gate_ok", "up_ok", "sig_ok2", "pre_ok", "glu_ok", "a_hi_ok", "a_lo_ok"))
        slot_ok, rank_ok, hot_ok, list_full, idx_ok, rows_in = (
            sem(n) for n in ("slot_ok", "rank_ok", "hot_ok", "list_full", "idx_ok", "rows_in"))
        xt_full, x_hi_ok, x_lo_ok = sem("xt_full"), sem("x_hi_ok"), sem("x_lo_ok")
        b_gu_ok, b_dn_ok = sem("b_gu_ok"), sem("b_dn_ok")
        yt_full, yt_read, y_out, y_free = (sem(n) for n in ("yt_full", "yt_read", "y_out", "y_free"))
        pool_turn, mm_clear = sem("pool_turn2"), sem("mm_clear")
        AHEAD = SPLIT - 1
        PC = PAIR_CHUNKS
        TILES = CHUNKS * MC
        MM_AHEAD = SPLIT * MC
        SUM_AHEAD = BANKS
        YT_AHEAD = 3

        def last_block(eng):
            return eng.value_load(k["last_block"][0:1, 0:1], min_val=E_ - 1, max_val=MAX_BLOCKS - 1)

        with nc.Block() as block:

            @block.sync
            def _(sp):
                final = last_block(sp)

                def load(c_, e, turn):
                    sp.wait_ge(hi_done, turn)
                    sp.wait_ge(lo_done, turn)
                    sp.dma_start(raw[c_ % RAW][:], chunk_source(w_gate_up, w_down, c_, e)).then_inc(raw_in[c_ % RAW], 16)

                def expert_of(b):
                    return sp.value_load(k["block_expert"][0:1, bass.ds(b, 1)], min_val=0, max_val=E_ - 1)

                with sp.Fori(0, final) as b:
                    e = expert_of(b)
                    for c_ in range(RAW, CHUNKS):
                        load(c_, e, CHUNKS * b + c_ - RAW + 1)
                    e = expert_of(b + 1)
                    for c_ in range(RAW):
                        load(c_, e, CHUNKS * b + CHUNKS + c_ - RAW + 1)
                e = expert_of(final)
                for c_ in range(RAW, CHUNKS):
                    load(c_, e, CHUNKS * final + c_ - RAW + 1)

            @block.gpsimd
            def _(pool):
                final = last_block(pool)

                def until(semaphore, value):
                    pool.wait_ge(semaphore, value)
                    pool.sem_inc(pool_turn, 1)

                def expert_of(b):
                    return pool.value_load(k["block_expert"][0:1, bass.ds(b, 1)], min_val=0, max_val=E_ - 1)

                def ranks(e, b):
                    nc.gpsimd.tensor_tensor(rank_cur[:], k["ranks"][:, :, bass.ds(e, 1)].rearrange("p t a -> p (t a)"),
                                            k["block_first"][:, bass.ds(b, 1)].to_broadcast([P, TT]),
                                            ALU.subtract).then_inc(rank_ok, 1)

                def gather(turn):
                    until(idx_ok, turn)
                    for s, n in enumerate(SEG):
                        nc.gpsimd.indirect_dma_start(
                            out=rows[s][:], out_offset=None, in_=h_rows,
                            in_offset=bass.IndirectOffsetOnAxis(ap=idx[0:n, s:s + 1], axis=0)).then_inc(rows_in, 16)

                def bias_gu(e):
                    nc.gpsimd.tensor_copy(b_gu[:], k["bias_gu"][:, :, bass.ds(e, 1)].rearrange("p m a -> p (m a)")).then_inc(b_gu_ok, 1)

                nc.gpsimd.iota(slot_no[:], [[1, SLOTS]], base=0, channel_multiplier=0,
                               allow_small_or_imprecise_dtypes=True).then_inc(slot_ok, 1)
                pool.sem_inc(y_free, 1)
                e = expert_of(0)
                ranks(e, 0)
                bias_gu(e)
                gather(1)
                ranks(expert_of(1), 1)

                def body(b, last):
                    e_ = expert_of(b)
                    until(sum_ok, SUM_AHEAD + TILES * b)
                    nc.gpsimd.tensor_copy(b_dn[:], k["bias_dn"][:, :, bass.ds(e_, 1)].rearrange("p m a -> p (m a)")).then_inc(b_dn_ok, 1)
                    if not last:
                        en = expert_of(b + 1)
                    for j in range(PC):
                        until(sig_ok, PC * b + j + 1)
                        nc.gpsimd.tensor_tensor(sig[j % 2][:], gate[j % 2][:], sig[j % 2][:], ALU.mult).then_inc(pre_ok, 1)
                        if j == 1 and not last:
                            gather(b + 2)
                            until(hot_ok, b + 2)
                            ranks(expert_of(b + 2), b + 2)
                    if not last:
                        until(sum_ok, SUM_AHEAD + TILES * b + 2 * PC * MC)
                        bias_gu(en)
                    row = pool.value_load(k["block_row"][0:1, bass.ds(b, 1)], min_val=0, max_val=T * K_)
                    until(yt_read, PC * b + PC)
                    for s, n in enumerate(SEG):
                        pool.dma_start(y_rows[bass.ds(row + s * P, n), :], y_st[s][:]).then_inc(y_out, 16)
                    until(y_out, 32 * b + 32)
                    pool.sem_inc(y_free, 1)

                with pool.Fori(0, final) as b:
                    body(b, False)
                body(final, True)

            @block.scalar
            def _(act):
                final = last_block(act)

                def hi(b, c_, first=False):
                    act.wait_ge(raw_in[c_ % RAW], 16 * (CHUNKS // RAW * b + c_ // RAW + 1))
                    if not first:
                        act.wait_ge(mm_done, TILES * b + MC * c_ + MM_AHEAD - (SPLIT - 1) * MC)
                    nc.scalar.activation(w_hi[c_ % SPLIT][:], raw[c_ % RAW][:], ACT.Copy).then_inc(hi_done, 1)

                def x_high(turn):
                    ko = 0
                    for g, n in enumerate(XG):
                        act.wait_ge(xt_full, len(XG) * turn + g + 1)
                        nc.scalar.activation(x_s[:, ko:ko + n, 0, :], xt[g][:, 0:n * SLOTS].rearrange("p (k t) -> p k t", k=n),
                                             ACT.Copy).then_inc(x_hi_ok, 1)
                        ko += n

                def a_high(b, j):
                    act.wait_ge(glu_ok, PC * b + j + 1)
                    nc.scalar.activation(a_s[:, MC * j:MC * j + MC, 0, :], glu[j % 2][:], ACT.Copy).then_inc(a_hi_ok, 1)

                def halves(b, c_):
                    if c_ == 0:
                        act.wait_ge(b_gu_ok, b + 1)
                    if c_ == 2 * PC:
                        act.wait_ge(b_dn_ok, b + 1)
                    for m in range(MC):
                        if c_ < 2 * PC:
                            col = (c_ % 2) * (D // P) + MC * (c_ // 2) + m
                            bias = b_gu[:, col:col + 1]
                        else:
                            col = MC * (c_ - 2 * PC) + m
                            bias = b_dn[:, col:col + 1]
                        t = MC * c_ + m
                        act.wait_ge(mm_done, TILES * b + MM_AHEAD + t + 1)
                        act.wait_ge(sum_ok, TILES * b + SUM_AHEAD + t - BANKS + 1)
                        nc.scalar.activation(half[t % BANKS][:], mm[t % BANKS][:, 1, :], ACT.Identity,
                                             bias=bias).then_inc(half_ok, 1)

                def y_rows_out(b, q):
                    act.wait_ge(yt_full, YT_AHEAD + PC * b + q + 1)
                    if q == 0:
                        act.wait_ge(y_free, b + 1)
                    for s, n in enumerate(SEG):
                        ins = nc.scalar.activation(y_st[s][:, q * CC:(q + 1) * CC], yt[0:n, s, :], ACT.Copy)
                    ins.then_inc(yt_read, 1)

                hi(0, 0, True)
                x_high(0)
                for c_ in range(1, SPLIT):
                    hi(0, c_, True)
                halves(0, 0)

                def body(b, last):
                    for c_ in range(1, CHUNKS + 1):
                        nb, nc_ = (b + 1, c_ - CHUNKS) if c_ == CHUNKS else (b, c_)
                        if c_ + AHEAD < CHUNKS:
                            hi(b, c_ + AHEAD)
                        elif not last:
                            hi(b + 1, c_ + AHEAD - CHUNKS)
                        j = c_ // 2
                        if c_ < 2 * PC and c_ % 2 == 1:
                            act.wait_ge(gate_ok, PC * b + j + 1)
                            nc.scalar.activation(sig[j % 2][:], gate[j % 2][:], ACT.Sigmoid, scale=ALPHA).then_inc(sig_ok, 1)
                            if j:
                                a_high(b, j - 1)
                        if c_ > 2 * PC + 1:
                            y_rows_out(b, c_ - 2 * PC - 2)
                        if c_ < CHUNKS or not last:
                            halves(nb, nc_)
                        if c_ == 2 * PC - 1:
                            a_high(b, PC - 1)
                        if c_ == 2 * PC + 1 and not last:
                            x_high(b + 1)
                    y_rows_out(b, PC - 1)

                with act.Fori(0, final) as b:
                    body(b, False)
                body(final, True)

            @block.vector
            def _(dve):
                final = last_block(dve)
                dve.sem_inc(sum_ok, SUM_AHEAD)

                def lo(b, c_, first=False):
                    dve.wait_ge(hi_done, CHUNKS * b + c_ + 1)
                    if not first:
                        dve.wait_ge(mm_done, TILES * b + MC * c_ + MM_AHEAD - (SPLIT - 1) * MC)
                    nc.vector.tensor_tensor(w_lo[c_ % SPLIT][:], raw[c_ % RAW][:], w_hi[c_ % SPLIT][:].bitcast(F32),
                                            ALU.subtract).then_inc(lo_done, 1)

                def one_hot(turn):
                    dve.wait_ge(rank_ok, turn)
                    nc.vector.tensor_tensor(hot[:], slot_no[:, None, :].to_broadcast([P, TT, SLOTS]),
                                            rank_cur[:, :, None].to_broadcast([P, TT, SLOTS]), ALU.is_equal).then_inc(hot_ok, 1)

                def indices(turn):
                    dve.wait_ge(list_full, turn)
                    with nc.allow_low_precision(reason="whole numbers below 1024"):
                        for s, n in enumerate(SEG):
                            ins = nc.vector.tensor_reduce(idx[0:n, s:s + 1], xt[2][0:n, LIST + 2 * s:LIST + 2 * s + 2],
                                                          AX.X, ALU.add)
                    ins.then_inc(idx_ok, 1)

                def x_low(turn):
                    ko = 0
                    for g, n in enumerate(XG):
                        dve.wait_ge(x_hi_ok, len(XG) * turn + g + 1)
                        nc.vector.tensor_tensor(x_s[:, ko:ko + n, 1, :], xt[g][:, 0:n * SLOTS].rearrange("p (k t) -> p k t", k=n),
                                                x_s[:, ko:ko + n, 0, :].bitcast(F32), ALU.subtract).then_inc(x_lo_ok, 1)
                        ko += n

                def swiglu(b, j):
                    dve.wait_ge(up_ok, PC * b + j + 1)
                    dve.wait_ge(pre_ok, PC * b + j + 1)
                    nc.vector.scalar_tensor_tensor(glu[j % 2][:], up[j % 2][:], 1.0, sig[j % 2][:], ALU.add,
                                                   ALU.mult).then_inc(glu_ok, 1)

                def a_low(b, j):
                    dve.wait_ge(a_hi_ok, PC * b + j + 1)
                    nc.vector.tensor_tensor(a_s[:, MC * j:MC * j + MC, 1, :], glu[j % 2][:],
                                            a_s[:, MC * j:MC * j + MC, 0, :].bitcast(F32), ALU.subtract).then_inc(a_lo_ok, 1)

                def sums(b, c_):
                    j = c_ // 2
                    down = c_ >= 2 * PC
                    dst = y_col[c_ % 2] if down else (gate, up)[c_ % 2][j % 2]
                    if down:
                        dve.wait_ge(yt_full, YT_AHEAD + PC * b + c_ - 2 * PC - 1)
                    for m in range(MC):
                        t = MC * c_ + m
                        dve.wait_ge(half_ok, TILES * b + t + 1)
                        nc.vector.tensor_tensor(dst[:, m, :], mm[t % BANKS][:, 0, :], half[t % BANKS][:],
                                                ALU.add).then_inc(sum_ok, 1)
                    if not down:
                        dve.wait_ge(sum_ok, TILES * b + SUM_AHEAD + MC * (c_ + 1))
                        if c_ % 2 == 0:
                            nc.vector.tensor_scalar(dst[:], dst[:], LIMIT, None, ALU.min).then_inc(gate_ok, 1)
                        else:
                            nc.vector.tensor_scalar(dst[:], dst[:], LIMIT, -LIMIT, ALU.min, ALU.max).then_inc(up_ok, 1)

                for i in range(BANKS):
                    ins = nc.vector.memset(mm[i][:], 0.0)
                ins.then_inc(mm_clear, 1)
                dve.wait_ge(slot_ok, 1)
                one_hot(1)
                indices(1)
                one_hot(2)
                lo(0, 0, True)
                x_low(0)
                for c_ in range(1, SPLIT):
                    lo(0, c_, True)
                sums(0, 0)

                def body(b, last):
                    for c_ in range(1, CHUNKS + 1):
                        if c_ + AHEAD < CHUNKS:
                            lo(b, c_ + AHEAD)
                        elif not last:
                            lo(b + 1, c_ + AHEAD - CHUNKS)
                        j = c_ // 2
                        if c_ < 2 * PC and c_ % 2 == 1 and j:
                            a_low(b, j - 1)
                        if c_ < CHUNKS:
                            sums(b, c_)
                        elif not last:
                            sums(b + 1, 0)
                        if c_ < 2 * PC and c_ % 2 == 0:
                            swiglu(b, j - 1)
                        if c_ == 2 * PC - 1:
                            swiglu(b, PC - 1)
                            a_low(b, PC - 1)
                        if c_ == 2 * PC + 1 and not last:
                            x_low(b + 1)
                        if not last:
                            if c_ == 3:
                                indices(b + 2)
                            if c_ == 2 * PC + 2:
                                one_hot(b + 3)

                with dve.Fori(0, final) as b:
                    body(b, False)
                body(final, True)

            @block.tensor
            def _(pe):
                final = last_block(pe)
                pe.sem_inc(mm_done, MM_AHEAD)
                pe.sem_inc(yt_full, YT_AHEAD)

                def token_list(turn):
                    pe.wait_ge(hot_ok, turn)
                    for s, n in enumerate(SEG):
                        for t in range(TT):
                            ins = nc.tensor.matmul(xt[2][0:n, LIST + 2 * s:LIST + 2 * s + 2], hot[:, t, s * P:s * P + n],
                                                   k["token_of"][:, t, :], start=t == 0, stop=t == TT - 1)
                    ins.then_inc(list_full, 1)

                def x_transposes(turn):
                    pe.wait_ge(rows_in, 32 * turn + 32)
                    ko = 0
                    for g, n in enumerate(XG):
                        for i in range(n):
                            for s, rows_n in enumerate(SEG):
                                ins = nc.tensor.transpose(xt[g][:, i * SLOTS + s * P:i * SLOTS + s * P + rows_n],
                                                          rows[s][:, (ko + i) * P:(ko + i + 1) * P],
                                                          k["ident"][0:rows_n, 0:rows_n])
                        ins.then_inc(xt_full, 1)
                        ko += n

                def y_transposes(b, q):
                    pe.wait_ge(sum_ok, TILES * b + SUM_AHEAD + MC * (2 * PC + q + 1))
                    if q:
                        pe.wait_ge(yt_read, PC * b + q)
                    for s, n in enumerate(SEG):
                        for m in range(MC):
                            ins = nc.tensor.transpose(yt[0:n, s, m * P:(m + 1) * P], y_col[q % 2][:, m, s * P:s * P + n],
                                                      k["ident"][:])
                    ins.then_inc(yt_full, 1)

                def tiles(b, c_, part, width):
                    in_s = a_s if c_ >= 2 * PC else x_s
                    hi_, lo_ = w_hi[c_ % SPLIT], w_lo[c_ % SPLIT]
                    if part[0] == 0:
                        pe.wait_ge(lo_done, CHUNKS * b + c_ + 1)
                    for m in range(MC):
                        t = MC * c_ + m
                        if part[0] == 0:
                            pe.wait_ge(sum_ok, TILES * b + SUM_AHEAD + t - BANKS + 1)
                        for ko in part:
                            nc.tensor.matmul(mm[t % BANKS][:, :, 0:width], hi_[:, ko, m * P:(m + 1) * P],
                                             in_s[:, ko, :, 0:width], start=ko == 0, stop=False)
                            ins = nc.tensor.matmul(mm[t % BANKS][:, 0, 0:width], lo_[:, ko, m * P:(m + 1) * P],
                                                   in_s[:, ko, 0, 0:width], start=False, stop=ko == KO - 1)
                        if part[-1] == KO - 1:
                            ins.then_inc(mm_done, 1)

                def chunk(b, c_, width=SLOTS):
                    tiles(b, c_, range(KO), width)

                def first_down_chunks(b, width):
                    early, late, newest = range(KO - 2 * MC), range(KO - 2 * MC, KO - MC), range(KO - MC, KO)
                    for c_, part in ((2 * PC, early), (2 * PC, late), (2 * PC + 1, range(KO - MC)),
                                     (2 * PC, newest), (2 * PC + 1, newest)):
                        pe.wait_ge(a_lo_ok, PC * b + part[-1] // MC + 1)
                        tiles(b, c_, part, width)

                token_list(1)
                x_transposes(0)
                pe.wait_ge(mm_clear, 1)
                pe.wait_ge(x_lo_ok, len(XG))
                chunk(0, 0)

                def chunks(b, last, width):
                    for c_ in range(1, CHUNKS):
                        if c_ == 2 * PC:
                            first_down_chunks(b, width)
                        elif c_ != 2 * PC + 1:
                            chunk(b, c_, width)
                        if c_ == 2 and not last:
                            token_list(b + 2)
                        if c_ == 2 * PC + 1 and not last:
                            x_transposes(b + 1)
                        if c_ > 2 * PC:
                            y_transposes(b, c_ - 2 * PC - 1)

                def body(b, last):
                    tokens = pe.value_load(k["block_tokens"][0:1, bass.ds(b, 1)], min_val=0, max_val=SLOTS)
                    with pe.If(tokens > SEG[0]):
                        chunks(b, last, SLOTS)
                    with pe.Else():
                        chunks(b, last, SEG[0])
                    if not last:
                        pe.wait_ge(x_lo_ok, len(XG) * b + 2 * len(XG))
                        chunk(b + 1, 0)
                    y_transposes(b, PC - 1)

                with pe.Fori(0, final) as b:
                    body(b, False)
                body(final, True)


def combine(nc, k, g_final, y_rows, out_tiles):
    with ExitStack() as c:
        sb = lambda n, s, d=F32: c.enter_context(nc.sbuf_tensor(n, s, d))
        sem = lambda n: c.enter_context(nc.semaphore(n))
        RING = 6
        X = k["x2"]
        Y = [sb(f"Y{i}", [P, K_, D]) for i in range(RING)]
        junk, g_row = sb("junk3", [P, D]), sb("g_row3", [P, D])
        ms, rms, rstd = sb("ms3", [P, TT]), sb("rms3", [P, TT]), sb("rstd3", [P, TT])
        g_in, out_done = sem("g_in3"), sem("out_done")
        y_in = [sem(f"y_in{i}") for i in range(RING)]
        y_used, acc, x_ok, ms_ok, ms2_ok, rms_ok, rstd_ok, out_ok = (
            sem(n) for n in ("y_used", "acc3", "x_ok3", "ms_ok3", "ms2_ok3", "rms_ok3", "rstd_ok3", "out_ok3"))

        with nc.Block() as block:

            @block.sync
            def _(sp):
                sp.dma_start(g_row[:], g_final.rearrange("(a d) -> a d", a=1).to_broadcast([P, D])).then_inc(g_in, 16)
                for t in range(TT):
                    sp.wait_ge(out_ok, t + 1)
                    sp.dma_start(out_tiles[:, t, :], X[:, t, :]).then_inc(out_done, 16)
                sp.wait_ge(out_done, 16 * TT)

            @block.gpsimd
            def _(pool):
                for t in range(TT):
                    if t >= RING:
                        pool.wait_ge(y_used, t - RING + 1)
                    for i in range(K_):
                        nc.gpsimd.indirect_dma_start(
                            out=Y[t % RING][:, i, :], out_offset=None, in_=y_rows[0:T * K_, :],
                            in_offset=bass.IndirectOffsetOnAxis(ap=k["dest"][:, t, i:i + 1], axis=0)).then_inc(y_in[t % RING], 16)

            @block.scalar
            def _(act):
                for t in range(TT):
                    act.wait_ge(x_ok, t + 1)
                    if t:
                        act.wait_ge(ms_ok, t)
                    nc.scalar.activation(junk[:], X[:, t, :], ACT.Square, scale=D ** -0.5,
                                         accum_out=ms[:, t:t + 1]).then_inc(ms_ok, 1)
                    act.wait_ge(ms2_ok, t + 1)
                    nc.scalar.activation(rms[:, t:t + 1], ms[:, t:t + 1], ACT.Sqrt).then_inc(rms_ok, 1)

            @block.vector
            def _(dve):
                def gated_sum(t):
                    dve.wait_ge(y_in[t % RING], 16 * K_ * (t // RING + 1))
                    for i in range(K_):
                        ins = nc.vector.scalar_tensor_tensor(X[:, t, :], Y[t % RING][:, i, :], k["gates"][:, t, i:i + 1],
                                                             X[:, t, :], ALU.mult, ALU.add)
                        if i < K_ - 1:
                            ins.then_inc(acc, 1)
                            dve.wait_ge(acc, (K_ - 1) * t + i + 1)
                    ins.then_inc(x_ok, 1)
                    if t + RING < TT:
                        dve.wait_ge(x_ok, t + 1)
                        dve.sem_inc(y_used, 1)

                def normalize(t):
                    dve.wait_ge(ms_ok, t + 1)
                    nc.vector.tensor_scalar(ms[:, t:t + 1], ms[:, t:t + 1], EPS, None, ALU.add).then_inc(ms2_ok, 1)
                    dve.wait_ge(rms_ok, t + 1)
                    nc.vector.reciprocal(rstd[:, t:t + 1], rms[:, t:t + 1]).then_inc(rstd_ok, 1)
                    dve.wait_ge(rstd_ok, t + 1)
                    nc.vector.scalar_tensor_tensor(X[:, t, :], X[:, t, :], rstd[:, t:t + 1], g_row[:], ALU.mult,
                                                   ALU.mult).then_inc(out_ok, 1)

                dve.wait_ge(g_in, 16)
                gated_sum(0)
                for t in range(1, TT):
                    gated_sum(t)
                    normalize(t - 1)
                normalize(TT - 1)


_INS = ["x", "g_mix", "w_in", "pool_w", "pool_scale", "w_out", "g_moe", "w_router", "b_router",
        "w_gate_up", "b_gate_up", "w_down", "b_down", "g_final"]


def kernel(**inputs):
    import numpy as np
    import concourse.bacc as bacc
    from concourse.bass_utils import run_bass_kernel_spmd

    nc = bacc.Bacc("TRN2", target_bir_lowering=False, num_devices=1)
    arrays, args = {}, []
    for name in _INS:
        a = np.ascontiguousarray(inputs[name])
        arrays[f"in_{name}"] = a
        args.append(nc.dram_tensor(f"in_{name}", a.shape, mybir.dt.from_np(a.dtype), kind="ExternalInput").ap())
    out = nc.dram_tensor("out_0", (1, T, D), F32, kind="ExternalOutput").ap()
    hybrid_moe_kernel(nc, *args, out)
    r = run_bass_kernel_spmd(nc, [arrays], core_ids=[0])
    return r.results[0]["out_0"]
```

```python
from contextlib import ExitStack

import concourse.bass as bass
from concourse import mybir

F32 = mybir.dt.float32
F32R = mybir.dt.float32r
BF16 = mybir.dt.bfloat16
I32 = mybir.dt.int32
U32 = mybir.dt.uint32
ALU = mybir.AluOpType
ACT = mybir.ActivationFunctionType
AX = mybir.AxisListType

P = 128
D = 1024
T = 1024
KO = D // P
TT = T // P
HALF = 512
HEADS, HD = 8, 64
PAIRS = HEADS // 2
QKV = HEADS * HD
WINDOWS = (2, 4, 8, 16)
PAD = max(WINDOWS)
EPS = 1e-5
E_, K_ = 32, 4
LIMIT, ALPHA = 7.0, 1.702

SLOTS = 160
SEG = (128, SLOTS - 128)
WIDTHS = (128, 144, SLOTS)
MAX_BLOCKS_PER_EXPERT = -(-T // SLOTS)
MAX_BLOCKS = E_ + T * K_ // SLOTS
TABLE = 64
assert MAX_BLOCKS + 1 < TABLE

CC = 256
MC = CC // P
PAIR_CHUNKS = D // CC
CHUNKS = 3 * PAIR_CHUNKS
RAW = 6
SPLIT = 4
BANKS = 4
XG = (3, 3, 2)


def hybrid_moe_kernel(nc, x, g_mix, w_in, pool_w, pool_scale, w_out, g_moe, w_router, b_router,
                      w_gate_up, b_gate_up, w_down, b_down, g_final, out):
    h_rows = nc.dram_tensor("h_rows", [T, D], F32, kind="Internal").ap()
    y_rows = nc.dram_tensor("y_rows", [T * K_ + SLOTS, D], F32, kind="Internal").ap()
    x_tiles = x.rearrange("a (t p) d -> p (a t) d", p=P)
    out_tiles = out.rearrange("a (t p) d -> p (a t) d", p=P)

    with ExitStack() as keep:
        sb = lambda n, s, d=F32: keep.enter_context(nc.sbuf_tensor(n, s, d))
        k = {}
        k["ident"] = sb("ident", [P, P])
        k["logits"] = sb("logits", [P, TT, E_])
        k["bias_gu"] = sb("bias_gu", [P, 2 * D // P, E_])
        k["bias_dn"] = sb("bias_dn", [P, D // P, E_])
        k["ranks"] = sb("ranks", [P, TT, E_])
        k["gates"] = sb("gates", [P, TT, K_])
        k["dest"] = sb("dest", [P, TT, K_], I32)
        k["block_expert"] = sb("block_expert", [P, TABLE], I32)
        k["block_first"] = sb("block_first", [P, TABLE])
        k["block_row"] = sb("block_row", [P, TABLE], I32)
        k["block_tokens"] = sb("block_tokens", [P, TABLE], I32)
        k["last_block"] = sb("last_block", [P, 1], I32)
        k["token_of"] = sb("token_of", [P, TT, 2], BF16)
        with ExitStack() as mix:
            pool_T = mix.enter_context(nc.sbuf_tensor("pool_T", [P, KO // 2, T], F32))
            attn = mix.enter_context(nc.sbuf_tensor("attn", [P, TT, QKV], F32))
            with ExitStack() as at:
                h_hi = at.enter_context(nc.sbuf_tensor("h_hi", [P, KO, T], F32R))
                h_lo = at.enter_context(nc.sbuf_tensor("h_lo", [P, KO, T], F32R))
                v_all = at.enter_context(nc.sbuf_tensor("v_all", [P, TT, QKV], F32))
                project(nc, k, x_tiles, g_mix, w_in, pool_w, pool_scale, h_hi, h_lo, v_all, pool_T, attn)
                attend(nc, k, w_in, h_hi, h_lo, v_all, attn)
            k["x2"] = keep.enter_context(nc.sbuf_tensor("x2", [P, TT, D], F32, side="right"))
            project_out(nc, k, x_tiles, g_moe, w_out, w_router, b_router, attn, pool_T, h_rows)
        with ExitStack() as moe:
            raw = [moe.enter_context(nc.sbuf_tensor(f"raw{i}", [P, KO, CC], F32)) for i in range(RAW)]
            raw_in = [moe.enter_context(nc.semaphore(f"raw_in{i}")) for i in range(RAW)]
            route(nc, k, w_gate_up, w_down, b_gate_up, b_down, raw, raw_in)
            experts(nc, k, w_gate_up, w_down, h_rows, y_rows, raw, raw_in)
        combine(nc, k, g_final, y_rows, out_tiles)


def three_passes(nc, out, still, moving, first, last):
    nc.tensor.matmul(out, still[0], moving[0], start=first, stop=False)
    nc.tensor.matmul(out, still[0], moving[1], start=False, stop=False)
    return nc.tensor.matmul(out, still[1], moving[0], start=False, stop=last)


def project(nc, k, x_tiles, g_mix, w_in, pool_w, pool_scale, h_hi, h_lo, v_all, pool_T, spare):
    with ExitStack() as c:
        sb = lambda n, s, d=F32: c.enter_context(nc.sbuf_tensor(n, s, d))
        ps = lambda n, s: c.enter_context(nc.psum_tensor(n, s, F32))
        sem = lambda n: c.enter_context(nc.semaphore(n))
        X = sb("X", [P, TT, D])
        spare = spare[:].rearrange("p t d -> p (t d)")
        square = spare[:, 0:D]
        w_u = spare[:, D:D + KO * P].rearrange("p (k n) -> p k n", k=KO)
        pw = spare[:, D + KO * P:D + (KO + len(WINDOWS)) * P].rearrange("p (k n) -> p k n", k=len(WINDOWS))
        mean_sq, rms, rstd = sb("mean_sq", [P, TT]), sb("rms", [P, TT]), sb("rstd", [P, TT])
        g_col = sb("g_col", [P, KO])
        scale_col = sb("scale_col", [P, len(WINDOWS)])
        w_v, wv_hi, wv_lo = sb("w_v", [P, KO, QKV]), sb("wv_hi", [P, KO, QKV], F32R), sb("wv_lo", [P, KO, QKV], F32R)
        wu_hi, wu_lo = sb("wu_hi", [P, KO, P], F32R), sb("wu_lo", [P, KO, P], F32R)
        count, inv = sb("count", [P, PAD]), sb("inv", [P, len(WINDOWS), PAD])
        iota1 = sb("iota1", [P, PAD])
        X_flat = X[:].rearrange("p t d -> p (t d)")
        u, *sums = (X_flat[:, i * (PAD + T):(i + 1) * (PAD + T)] for i in range(3))
        pooled = X_flat[:, 3 * (PAD + T):3 * (PAD + T) + T]
        bank = [ps(f"pj{i}", [P, HALF]) for i in range(8)]
        x_in = [sem(f"x_in{i}") for i in range(TT)]
        cols_in, wv_in, wu_in, pw_in = (sem(n) for n in ("cols_in", "wv_in", "wu_in", "pw_in"))
        ident_ok, iota_ok, pad_ok = sem("ident_ok"), sem("iota_ok"), sem("pad_ok")
        sq_done, mean_ok, rms_ok, rstd_ok, x_scaled = (sem(n) for n in ("sq_done", "mean_ok", "rms_ok", "rstd_ok", "x_scaled"))
        pe_bank, act_read, dve_read = sem("pe_bank"), sem("act_read"), sem("dve_read")
        wv_hi_ok, wv_lo_ok, wu_hi_ok, wu_lo_ok = (sem(n) for n in ("wv_hi_ok", "wv_lo_ok", "wu_hi_ok", "wu_lo_ok"))
        inv_ok, sum_ok, pooled_ok = sem("inv_ok"), sem("sum_ok"), sem("pooled_ok")
        NW, TH = len(WINDOWS), TT // 2

        uses = [("h", n) for n in range(2 * KO)]
        for g in range(NW):
            uses += [("u", 2 * g), ("u", 2 * g + 1), ("v", 2 * g), ("v", 2 * g + 1), ("mix", 2 * g), ("mix", 2 * g + 1)]
        at = {use: n for n, use in enumerate(uses)}

        with nc.Block() as block:

            @block.sync
            def _(sp):
                for t in range(TT):
                    sp.dma_start(X[:, t, :], x_tiles[:, t, :]).then_inc(x_in[t], 16)
                with nc.allow_non_contiguous_dma(reason="columns of a small vector"):
                    sp.dma_start(g_col[:], g_mix.rearrange("a (k p) -> p (a k)", p=P)).then_inc(cols_in, 16)
                    sp.dma_start(scale_col[:], pool_scale.rearrange("a (k p) -> p (a k)", p=P)).then_inc(cols_in, 16)
                for g in range(NW):
                    if g:
                        sp.wait_ge(wu_lo_ok, g)
                    sp.dma_start(w_u, w_in[0, :, 3 * QKV + g * P:3 * QKV + (g + 1) * P]
                                 .rearrange("(k p) n -> p k n", p=P)).then_inc(wu_in, 16)
                    if g == 0:
                        sp.dma_start(w_v[:], w_in[0, :, 2 * QKV:3 * QKV].rearrange("(k p) n -> p k n", p=P)).then_inc(wv_in, 16)
                        sp.dma_start(pw, pool_w[0].rearrange("g c d -> c g d")).then_inc(pw_in, 16)

            @block.gpsimd
            def _(pool):
                nc.gpsimd.memset(k["ident"][:], 0.0).then_inc(ident_ok, 1)
                pool.wait_ge(ident_ok, 1)
                nc.gpsimd.affine_select(out=k["ident"][:], in_=k["ident"][:], compare_op=ALU.not_equal, fill=1.0,
                                        base=0, pattern=[[-1, P]], channel_multiplier=1).then_inc(ident_ok, 1)
                nc.gpsimd.iota(iota1[:], [[1, PAD]], base=1, channel_multiplier=0,
                               allow_small_or_imprecise_dtypes=True).then_inc(iota_ok, 1)
                pool.wait_ge(pe_bank, 2 * KO)
                for buf in (u, *sums):
                    last = nc.gpsimd.memset(buf[:, 0:PAD], 0.0)
                last.then_inc(pad_ok, 1)

            @block.scalar
            def _(act):
                def split_u(g):
                    act.wait_ge(wu_in, 16 * (g + 1))
                    if g:
                        act.wait_ge(pe_bank, at[("u", 2 * g - 1)] + 1)
                    nc.scalar.activation(wu_hi[:], w_u, ACT.Copy).then_inc(wu_hi_ok, 1)

                for t in range(TT):
                    act.wait_ge(x_in[t], 16)
                    if t:
                        act.wait_ge(sq_done, t)
                    nc.scalar.activation(square, X[:, t, :], ACT.Square, scale=D ** -0.5,
                                         accum_out=mean_sq[:, t:t + 1]).then_inc(sq_done, 1)
                    if t % TH == TH - 1:
                        cols = slice(t + 1 - TH, t + 1)
                        act.wait_ge(mean_ok, t // TH + 1)
                        nc.scalar.activation(rms[:, cols], mean_sq[:, cols], ACT.Sqrt).then_inc(rms_ok, 1)
                act.wait_ge(cols_in, 32)
                for n, (kind, i) in enumerate(uses):
                    if (kind, i) == ("h", KO):
                        split_u(0)
                    if (kind, i) == ("u", 0):
                        act.wait_ge(wv_in, 16)
                        nc.scalar.activation(wv_hi[:], w_v[:], ACT.Copy).then_inc(wv_hi_ok, 1)
                    act.wait_ge(pe_bank, n + 1)
                    src = bank[n % 8]
                    if kind == "h":
                        half, ko = divmod(i, KO)
                        ins = nc.scalar.activation(h_hi[:, ko, half * HALF:(half + 1) * HALF], src[:], ACT.Copy,
                                                   scale=g_col[:, ko:ko + 1])
                    elif kind == "v":
                        ins = nc.scalar.activation(v_all[:, i, :], src[:], ACT.Copy)
                    elif kind == "u":
                        g, half = divmod(i, 2)
                        if half == 0:
                            if g == 0:
                                act.wait_ge(pad_ok, 1)
                            else:
                                act.wait_ge(pooled_ok, g)
                        ins = nc.scalar.activation(u[:, PAD + half * HALF:PAD + (half + 1) * HALF], src[:], ACT.Copy)
                    else:
                        g, half = divmod(i, 2)
                        ins = nc.scalar.activation(pool_T[:, g, half * HALF:(half + 1) * HALF], src[:],
                                                   ACT.Copy, scale=scale_col[:, g:g + 1])
                    ins.then_inc(act_read, 1)
                    if kind == "u" and i % 2 == 1 and i // 2 + 1 < NW:
                        split_u(i // 2 + 1)

            @block.vector
            def _(dve):
                def split_u(g):
                    dve.wait_ge(wu_hi_ok, g + 1)
                    nc.vector.tensor_tensor(wu_lo[:], w_u, wu_hi[:].bitcast(F32), ALU.subtract).then_inc(wu_lo_ok, 1)

                for n in range(2):
                    cols = slice(n * TH, (n + 1) * TH)
                    dve.wait_ge(sq_done, (n + 1) * TH)
                    nc.vector.tensor_scalar(mean_sq[:, cols], mean_sq[:, cols], EPS, None, ALU.add).then_inc(mean_ok, 1)
                    dve.wait_ge(rms_ok, n + 1)
                    nc.vector.reciprocal(rstd[:, cols], rms[:, cols]).then_inc(rstd_ok, 1)
                    dve.wait_ge(rstd_ok, n + 1)
                    for t in range(n * TH, (n + 1) * TH):
                        nc.vector.tensor_scalar(X[:, t, :], X[:, t, :], rstd[:, t:t + 1], None, ALU.mult).then_inc(x_scaled, 1)
                for n in range(2 * KO):
                    half, ko = divmod(n, KO)
                    at_ = (slice(None), ko, slice(half * HALF, (half + 1) * HALF))
                    dve.wait_ge(act_read, n + 1)
                    nc.vector.scalar_tensor_tensor(h_lo[at_], bank[n % 8][:], g_col[:, ko:ko + 1], h_hi[at_].bitcast(F32),
                                                   ALU.mult, ALU.subtract).then_inc(dve_read, 1)
                    if n == KO:
                        split_u(0)
                dve.wait_ge(wv_hi_ok, 1)
                nc.vector.tensor_tensor(wv_lo[:], w_v[:], wv_hi[:].bitcast(F32), ALU.subtract).then_inc(wv_lo_ok, 1)
                dve.wait_ge(iota_ok, 1)
                for g, w in enumerate(WINDOWS):
                    if g:
                        dve.wait_ge(inv_ok, 2 * g)
                    nc.vector.tensor_scalar(count[:], iota1[:], float(w), None, ALU.min).then_inc(inv_ok, 1)
                    dve.wait_ge(inv_ok, 2 * g + 1)
                    nc.vector.reciprocal(inv[:, g, :], count[:]).then_inc(inv_ok, 1)
                dve.wait_ge(inv_ok, 2 * NW)
                dve.wait_ge(pad_ok, 1)
                done = 0
                for g, w in enumerate(WINDOWS):
                    dve.wait_ge(act_read, at[("u", 2 * g + 1)] + 1)
                    if g + 1 < NW:
                        split_u(g + 1)
                    src = u
                    for s in range(g + 1):
                        dst = sums[s % 2]
                        nc.vector.tensor_tensor(dst[:, PAD:], src[:, PAD:], src[:, PAD - 2 ** s:PAD + T - 2 ** s],
                                                ALU.add).then_inc(sum_ok, 1)
                        done += 1
                        dve.wait_ge(sum_ok, done)
                        src = dst
                    if g:
                        dve.wait_ge(pe_bank, at[("mix", 2 * g - 1)] + 1)
                    nc.vector.scalar_tensor_tensor(pooled, src[:, PAD:], 1.0 / w, u[:, PAD:], ALU.mult,
                                                   ALU.subtract).then_inc(sum_ok, 1)
                    dve.wait_ge(sum_ok, done + 1)
                    nc.vector.tensor_tensor(src[:, PAD:2 * PAD], src[:, PAD:2 * PAD], inv[:, g, :], ALU.mult).then_inc(sum_ok, 1)
                    done += 2
                    dve.wait_ge(sum_ok, done)
                    nc.vector.tensor_tensor(pooled[:, 0:PAD], src[:, PAD:2 * PAD], u[:, PAD:2 * PAD],
                                            ALU.subtract).then_inc(pooled_ok, 1)
                    dve.wait_ge(pooled_ok, g + 1)

            @block.tensor
            def _(pe):
                pe.wait_ge(ident_ok, 2)
                for n, (kind, i) in enumerate(uses):
                    dst = bank[n % 8]
                    if n >= 8:
                        if n - 8 < 2 * KO:
                            pe.wait_ge(dve_read, n - 7)
                        else:
                            pe.wait_ge(act_read, n - 7)
                    if kind == "h":
                        half, ko = divmod(i, KO)
                        pe.wait_ge(x_scaled, 4 * (half + 1))
                        for t in range(4):
                            ins = nc.tensor.transpose(dst[:, t * P:(t + 1) * P],
                                                      X[:, 4 * half + t, ko * P:(ko + 1) * P], k["ident"][:])
                    elif kind == "v":
                        if i == 0:
                            pe.wait_ge(wv_lo_ok, 1)
                        tile = (slice(None), slice(i * P, (i + 1) * P))
                        for ko in range(KO):
                            ins = three_passes(nc, dst[:], [h[:, ko, tile[1]] for h in (h_hi, h_lo)],
                                               [w[:, ko, :] for w in (wv_hi, wv_lo)], ko == 0, ko == KO - 1)
                    elif kind == "u":
                        g, half = divmod(i, 2)
                        if g == 0:
                            pe.wait_ge(dve_read, (half + 1) * KO)
                        pe.wait_ge(wu_lo_ok, g + 1)
                        for ko in range(KO):
                            ins = three_passes(nc, dst[:], [w[:, ko, :] for w in (wu_hi, wu_lo)],
                                               [h[:, ko, half * HALF:(half + 1) * HALF] for h in (h_hi, h_lo)],
                                               ko == 0, ko == KO - 1)
                    else:
                        g, half = divmod(i, 2)
                        pe.wait_ge(pw_in, 16)
                        pe.wait_ge(pooled_ok, g + 1)
                        ins = nc.tensor.matmul(dst[:], pw[:, g, :], pooled[:, half * HALF:(half + 1) * HALF],
                                               start=True, stop=True)
                    ins.then_inc(pe_bank, 1)


def attend(nc, k, w_in, h_hi, h_lo, v_all, attn):
    UNITS = 2 * TT
    USES = 2 + UNITS
    groups = [(u, g) for u in range(UNITS) for g in range((u // 2) // 4 + 1)]
    first_group = {u: next(n for n, (v, _) in enumerate(groups) if v == u) for u in range(UNITS)}
    n_groups = {u: (u // 2) // 4 + 1 for u in range(UNITS)}
    G = len(groups)
    WT = 4
    BETA = 4
    TP_AHEAD = G
    PIECES, FIRST_PIECE = 4, 4
    w_piece = lambda n: (slice(None), n // 2, slice(n % 2 * KO // 2, (n % 2 + 1) * KO // 2))
    AV_AHEAD = WT
    assert USES % 2 == 0 and G % WT == 0 and UNITS % BETA == 0
    with ExitStack() as c:
        sb = lambda n, s, d=F32: c.enter_context(nc.sbuf_tensor(n, s, d))
        ps = lambda n, s: c.enter_context(nc.psum_tensor(n, s, F32))
        sem = lambda n: c.enter_context(nc.semaphore(n))
        w_qk = sb("w_qk", [P, 2, KO, P])
        wq_hi, wq_lo = sb("wq_hi", [P, 2, KO, P], F32R), sb("wq_lo", [P, 2, KO, P], F32R)
        q_hi, q_lo, k_hi, k_lo = (sb(n, [P, T], F32R) for n in ("q_hi", "q_lo", "k_hi", "k_lo"))
        v_pair = sb("v_pair", [P, TT, 2, 2, HD], F32R)
        beta = [sb(f"beta{i}", [P, T]) for i in range(BETA)]
        stay = [sb(f"stay{i}", [P, T + 1]) for i in range(2)]
        wT = [sb(f"wT{i}", [P, 4, 2, P], F32R) for i in range(WT)]
        fold = sb("fold", [P, HD])
        acc = [k["logits"][:].rearrange("p t e -> p (t e)")[:, i * P:(i + 1) * P] for i in range(2)]
        wide = [ps(f"wide{i}", [P, T]) for i in range(2)]
        tp = [ps(f"tp{i}", [P, HALF]) for i in range(2)]
        av = [ps(f"av{i}", [P, HALF]) for i in range(2)]
        w_qk_in, wq_hi_ok, wq_lo_ok = sem("w_qk_in"), sem("wq_hi_ok"), sem("wq_lo_ok")
        wide_full, wide_free = sem("wide_full"), sem("wide_free")
        one_ok, mask_ok, scan_ok, weight_ok = (sem(n) for n in ("one_ok", "mask_ok", "scan_ok", "weight_ok"))
        qk_hi_ok, v_hi_ok, v_lo_ok, wt_hi_ok = (sem(n) for n in ("qk_hi_ok", "v_hi_ok", "v_lo_ok", "wt_hi_ok"))
        fold_ok, half_sum, acc_ok, fold_full = (
            sem(n) for n in ("fold_ok", "half_sum", "acc_ok", "fold_full"))
        tp_full, tp_read, av_group, av_read = (sem(n) for n in ("tp_full", "tp_read", "av_group", "av_read"))
        pool_turn = sem("pool_turn")

        with nc.Block() as block:

            @block.sync
            def _(sp):
                def load(hp):
                    for i in range(2):
                        sp.dma_start(w_qk[:, i], w_in[0, :, bass.ds(i * QKV + hp * P, P)]
                                     .rearrange("(k p) n -> p k n", p=P)).then_inc(w_qk_in, 16)
                load(0)
                with sp.Fori(0, PAIRS - 1) as hp:
                    sp.wait_ge(wq_lo_ok, PIECES * hp + PIECES)
                    load(hp + 1)

            @block.scalar
            def _(act):
                act.sem_inc(wide_free, 2)

                def split(hp, piece):
                    if piece == 0:
                        act.wait_ge(w_qk_in, 32 * hp + 32)
                    part = w_piece(piece)
                    nc.scalar.activation(wq_hi[part], w_qk[part], ACT.Copy).then_inc(wq_hi_ok, 1)

                def qk_high(hp, i):
                    act.wait_ge(wide_full, USES * hp + i + 1)
                    nc.scalar.activation((q_hi, k_hi)[i][:], wide[i][:], ACT.Copy,
                                         scale=HD ** -0.5 if i == 0 else 1.0).then_inc(qk_hi_ok, 1)

                for piece in range(PIECES):
                    split(0, piece)
                qk_high(0, 0)
                qk_high(0, 1)

                def body(hp, last):
                    act.wait_ge(av_group, G * hp + AV_AHEAD)
                    nc.scalar.activation(v_pair[:, :, :, 0, :],
                                         v_all[:, :, bass.ds(hp * P, P)].rearrange("p t (h d) -> p t h d", h=2),
                                         ACT.Copy).then_inc(v_hi_ok, 1)

                    def sigmoids(u):
                        w = (u // 2 + 1) * P
                        v = u - BETA
                        ahead = first_group[v % UNITS] + n_groups[v % UNITS] - (0 if v >= 0 else G)
                        act.wait_ge(tp_full, G * hp + TP_AHEAD + ahead)
                        act.wait_ge(wide_full, USES * hp + 2 + u + 1)
                        if u >= 2:
                            act.wait_ge(weight_ok, UNITS * hp + u - 1)
                        nc.scalar.activation(stay[u % 2][:, T - w:T], wide[u % 2][:, 0:w], ACT.Sigmoid, scale=-1.0)
                        nc.scalar.activation(beta[u % BETA][:, 0:w], wide[u % 2][:, 0:w], ACT.Sigmoid).then_inc(wide_free, 1)

                    def copies(u):
                        for g in range(n_groups[u]):
                            n = first_group[u] + g
                            wk = min(4, u // 2 + 1 - 4 * g) * P
                            act.wait_ge(tp_full, G * hp + TP_AHEAD + n + 1)
                            act.wait_ge(av_group, G * hp + AV_AHEAD + n - WT + 1)
                            nc.scalar.activation(wT[n % WT][:, 0:wk // P, 0, :],
                                                 tp[n % 2][:, 0:wk].rearrange("p (b t) -> p b t", t=P),
                                                 ACT.Copy).then_inc(wt_hi_ok, 1)

                    sigmoids(0)
                    sigmoids(1)
                    for u in range(UNITS):
                        if FIRST_PIECE <= u < FIRST_PIECE + PIECES and not last:
                            split(hp + 1, u - FIRST_PIECE)
                        if u == UNITS - 2 and not last:
                            qk_high(hp + 1, 0)
                        copies(u)
                        if u + 2 < UNITS:
                            sigmoids(u + 2)
                    if not last:
                        qk_high(hp + 1, 1)

                with act.Fori(0, PAIRS - 1) as hp:
                    body(hp, False)
                body(PAIRS - 1, True)

            @block.gpsimd
            def _(pool):
                for i in range(2):
                    last = nc.gpsimd.memset(stay[i][:, T:T + 1], 1.0)
                last.then_inc(one_ok, 1)

                def split(hp, piece):
                    pool.wait_ge(wq_hi_ok, PIECES * hp + piece + 1)
                    pool.sem_inc(pool_turn, 1)
                    part = w_piece(piece)
                    nc.gpsimd.tensor_tensor(wq_lo[part], w_qk[part], wq_hi[part].bitcast(F32),
                                            ALU.subtract).then_inc(wq_lo_ok, 1)

                def body(hp, last):
                    for u in range(UNITS):
                        i = u // 2
                        pool.wait_ge(wide_free, USES * hp + 2 + 2 + u + 1)
                        pool.sem_inc(pool_turn, 1)
                        for tile, fill in ((stay[u % 2][:, T - P:T], 1.0),
                                           (beta[u % BETA][:, i * P:(i + 1) * P], 0.0)):
                            nc.gpsimd.affine_select(out=tile, in_=tile, compare_op=ALU.is_gt, fill=fill, base=0,
                                                    pattern=[[-1, P]], channel_multiplier=1).then_inc(mask_ok, 1)
                        if FIRST_PIECE <= u < FIRST_PIECE + PIECES and not last:
                            split(hp + 1, u - FIRST_PIECE)

                for piece in range(PIECES):
                    split(0, piece)
                with pool.Fori(0, PAIRS - 1) as hp:
                    body(hp, False)
                body(PAIRS - 1, True)

            @block.vector
            def _(dve):
                dve.wait_ge(one_ok, 1)
                nc.vector.tensor_tensor(fold[:], k["ident"][:, 0:HD], k["ident"][:, HD:P], ALU.add).then_inc(fold_ok, 1)

                def qk_low(hp, i):
                    hi, lo = ((q_hi, q_lo), (k_hi, k_lo))[i]
                    dve.wait_ge(qk_hi_ok, 2 * hp + i + 1)
                    nc.vector.scalar_tensor_tensor(lo[:], wide[i][:], HD ** -0.5 if i == 0 else 1.0,
                                                   hi[:].bitcast(F32), ALU.mult, ALU.subtract).then_inc(wide_free, 1)

                qk_low(0, 0)
                qk_low(0, 1)

                def body(hp, last):
                    dve.wait_ge(v_hi_ok, hp + 1)
                    nc.vector.tensor_tensor(v_pair[:, :, :, 1, :],
                                            v_all[:, :, bass.ds(hp * P, P)].rearrange("p t (h d) -> p t h d", h=2),
                                            v_pair[:, :, :, 0, :].bitcast(F32), ALU.subtract).then_inc(v_lo_ok, 1)

                    def lows(u):
                        for g in range(n_groups[u]):
                            n = first_group[u] + g
                            nk = min(4, u // 2 + 1 - 4 * g)
                            dve.wait_ge(wt_hi_ok, G * hp + n + 1)
                            nc.vector.tensor_tensor(wT[n % WT][:, 0:nk, 1, :],
                                                    tp[n % 2][:, 0:nk * P].rearrange("p (b t) -> p b t", t=P),
                                                    wT[n % WT][:, 0:nk, 0, :].bitcast(F32), ALU.subtract).then_inc(tp_read, 1)

                    def sum_parts(u):
                        dve.wait_ge(av_group, G * hp + AV_AHEAD + first_group[u] + n_groups[u])
                        if u >= 2:
                            dve.wait_ge(fold_full, UNITS * hp + u - 1)
                        nc.vector.tensor_copy(acc[u % 2], av[u % 2][:, 0:P]).then_inc(half_sum, 1)
                        dve.wait_ge(half_sum, UNITS * hp + u + 1)
                        nc.vector.tensor_tensor(acc[u % 2], av[u % 2][:, P:2 * P], acc[u % 2], ALU.add).then_inc(acc_ok, 1)

                    def take(u):
                        dve.wait_ge(fold_full, UNITS * hp + u + 1)
                        nc.vector.tensor_copy(attn[:, u // 2, bass.ds(hp * P + (u % 2) * HD, HD)],
                                              av[u % 2][:, 2 * P:2 * P + HD]).then_inc(av_read, 1)

                    for u in range(UNITS):
                        w = (u // 2 + 1) * P
                        chain = stay[u % 2][:, T - w:T][:, ::-1]
                        dve.wait_ge(mask_ok, 2 * UNITS * hp + 2 * u + 1)
                        nc.vector.tensor_tensor_scan(chain, chain, chain, 1.0, ALU.mult, ALU.bypass).then_inc(scan_ok, 1)
                        dve.wait_ge(scan_ok, UNITS * hp + u + 1)
                        dve.wait_ge(mask_ok, 2 * UNITS * hp + 2 * u + 2)
                        nc.vector.tensor_tensor(beta[u % BETA][:, 0:w], beta[u % BETA][:, 0:w],
                                                stay[u % 2][:, T - w + 1:T + 1], ALU.mult).then_inc(weight_ok, 1)
                        if u >= 1:
                            lows(u - 1)
                        if u >= 2:
                            sum_parts(u - 2)
                        if u >= 3:
                            take(u - 3)
                        if u == UNITS - 1 and not last:
                            qk_low(hp + 1, 0)
                    lows(UNITS - 1)
                    sum_parts(UNITS - 2)
                    take(UNITS - 3)
                    if not last:
                        qk_low(hp + 1, 1)
                    sum_parts(UNITS - 1)
                    take(UNITS - 2)
                    take(UNITS - 1)

                with dve.Fori(0, PAIRS - 1) as hp:
                    body(hp, False)
                body(PAIRS - 1, True)

            @block.tensor
            def _(pe):
                pe.sem_inc(tp_full, TP_AHEAD)
                pe.sem_inc(av_group, AV_AHEAD)
                pe.wait_ge(fold_ok, 1)

                def projection(hp, i):
                    pe.wait_ge(wq_lo_ok, PIECES * hp + PIECES // 2 * (i + 1))
                    pe.wait_ge(wide_free, USES * hp + i + 1)
                    for half in range(2):
                        cols = slice(half * HALF, (half + 1) * HALF)
                        for ko in range(KO):
                            ins = three_passes(nc, wide[i][:, cols], [w[:, i, ko, :] for w in (wq_hi, wq_lo)],
                                               [h[:, ko, cols] for h in (h_hi, h_lo)], ko == 0, ko == KO - 1)
                    ins.then_inc(wide_full, 1)

                projection(0, 0)
                projection(0, 1)

                def body(hp, last):
                    pe.wait_ge(wide_free, USES * hp + 2 + 2)

                    def scores(u):
                        i, h = divmod(u, 2)
                        w = (i + 1) * P
                        pe.wait_ge(wide_free, USES * hp + 2 + u + 1)
                        for a in range(0, w, HALF):
                            b = min(w, a + HALF)
                            rows = slice(h * HD, (h + 1) * HD)
                            ins = three_passes(nc, wide[u % 2][:, a:b], [q[rows, i * P:(i + 1) * P] for q in (q_hi, q_lo)],
                                               [kk[rows, a:b] for kk in (k_hi, k_lo)], True, True)
                        ins.then_inc(wide_full, 1)

                    def transposes(u):
                        pe.wait_ge(weight_ok, UNITS * hp + u + 1)
                        for g in range(n_groups[u]):
                            n = first_group[u] + g
                            if n >= 2:
                                pe.wait_ge(tp_read, G * hp + n - 1)
                            for kb in range(4 * g, min(4 * g + 4, u // 2 + 1)):
                                ins = nc.tensor.transpose(tp[n % 2][:, (kb % 4) * P:(kb % 4 + 1) * P],
                                                          beta[u % BETA][:, kb * P:(kb + 1) * P], k["ident"][:])
                            ins.then_inc(tp_full, 1)

                    def values(u):
                        i, h = divmod(u, 2)
                        if u >= 2:
                            pe.wait_ge(av_read, UNITS * hp + u - 1)
                        if u == 0:
                            pe.wait_ge(v_lo_ok, hp + 1)
                        for g in range(n_groups[u]):
                            n = first_group[u] + g
                            pe.wait_ge(tp_read, G * hp + n + 1)
                            for kb in range(4 * g, min(4 * g + 4, i + 1)):
                                ins = nc.tensor.matmul(av[u % 2][:, 0:2 * P], v_pair[:, kb, h].rearrange("p a d -> p (a d)"),
                                                       wT[n % WT][:, kb % 4].rearrange("p a t -> p (a t)"),
                                                       start=kb == 0, stop=kb == i)
                            ins.then_inc(av_group, 1)

                    def fold_values(u):
                        pe.wait_ge(acc_ok, UNITS * hp + u + 1)
                        nc.tensor.matmul(av[u % 2][:, 2 * P:2 * P + HD], acc[u % 2], fold[:],
                                         start=True, stop=True).then_inc(fold_full, 1)

                    scores(0)
                    scores(1)
                    for u in range(UNITS):
                        if u + 2 < UNITS:
                            scores(u + 2)
                        if u == UNITS - 2 and not last:
                            projection(hp + 1, 0)
                        transposes(u)
                        if u >= 2:
                            fold_values(u - 2)
                        if u:
                            values(u - 1)
                    if not last:
                        projection(hp + 1, 1)
                    fold_values(UNITS - 2)
                    values(UNITS - 1)
                    fold_values(UNITS - 1)
                    pe.wait_ge(av_read, UNITS * hp + UNITS)

                with pe.Fori(0, PAIRS - 1) as hp:
                    body(hp, False)
                body(PAIRS - 1, True)


def project_out(nc, k, x_tiles, g_moe, w_out, w_router, b_router, attn, pool_T, h_rows):
    with ExitStack() as c:
        sb = lambda n, s, d=F32: c.enter_context(nc.sbuf_tensor(n, s, d))
        ps = lambda n, s: c.enter_context(nc.psum_tensor(n, s, F32))
        sem = lambda n: c.enter_context(nc.semaphore(n))
        RAW_W = 4
        KH = KO // 2
        w_raw = [sb(f"w_raw{i}", [P, D]) for i in range(RAW_W)]
        wo_hi, wo_lo = sb("wo_hi", [P, KO, D], F32R), sb("wo_lo", [P, KO, D], F32R)
        m_hi = [sb(f"m_hi{i}", [P, KO, P], F32R) for i in range(2)]
        m_lo = [sb(f"m_lo{i}", [P, KO, P], F32R) for i in range(2)]
        X = k["x2"]
        H = [sb(f"H{i}", [P, D]) for i in range(2)]
        hT2 = [sb(f"hT2{i}", [P, KO, P]) for i in range(2)]
        junk = sb("junk", [P, D])
        g_row = sb("g_row", [P, D])
        w_r, b_r = sb("w_r", [P, KO, E_]), sb("b_r", [P, E_])
        ms, rms, rstd = sb("ms", [P, TT]), sb("rms2", [P, TT]), sb("rstd2", [P, TT])
        op = [[ps(f"op{i}{j}", [P, HALF]) for j in range(2)] for i in range(2)]
        xp = [ps(f"xp{i}", [P, HALF]) for i in range(2)]
        mt = ps("mt", [P, HALF])
        lp = ps("lp", [P, TT, E_])
        x_in, row_in = [sem(f"x_in2{i}") for i in range(TT)], sem("row_in")
        w_in_ = [sem(f"wo_in{i}") for i in range(RAW_W)]
        wo_hi_ok, wo_lo_ok = sem("wo_hi_ok"), sem("wo_lo_ok")
        mt_full, m_hi_ok, m_lo_ok = sem("mt_full"), sem("m_hi_ok"), sem("m_lo_ok")
        proj_ok, res_ok, ms_ok, ms2_ok, rms_ok, rstd_ok, h_ok = (
            sem(n) for n in ("proj_ok", "res_ok", "ms_ok", "ms2_ok", "rms_ok2", "rstd_ok2", "h_ok"))
        h_out = [sem("h_out0"), sem("h_out1")]
        xp_full, xp_read, lg_full, lg_ok = sem("xp_full"), sem("xp_read"), sem("lg_full"), sem("lg_ok")

        with nc.Block() as block:

            @block.sync
            def _(sp):
                for ko in range(KO):
                    if ko >= RAW_W:
                        sp.wait_ge(wo_lo_ok, ko - RAW_W + 1)
                    sp.dma_start(w_raw[ko % RAW_W][:], w_out[0, ko * P:(ko + 1) * P, :]).then_inc(w_in_[ko % RAW_W], 16)
                for t in range(TT):
                    sp.dma_start(X[:, t, :], x_tiles[:, t, :]).then_inc(x_in[t], 16)
                sp.dma_start(g_row[:], g_moe.to_broadcast([P, D])).then_inc(row_in, 16)
                sp.dma_start(b_r[:], b_router.to_broadcast([P, E_])).then_inc(row_in, 16)
                sp.dma_start(w_r[:], w_router[0].rearrange("(k p) e -> p k e", p=P)).then_inc(row_in, 16)
                for t in range(TT):
                    sp.wait_ge(h_ok, t + 1)
                    sp.dma_start(h_rows[t * P:(t + 1) * P, :], H[t % 2][:]).then_inc(h_out[t % 2], 16)
                for stored in h_out:
                    sp.wait_ge(stored, 16 * TT // 2)

            @block.scalar
            def _(act):
                def mixed_high(t):
                    act.wait_ge(mt_full, t + 1)
                    if t >= 2:
                        act.wait_ge(proj_ok, t - 1)
                    nc.scalar.activation(m_hi[t % 2][:, 0:KH, :], mt[:].rearrange("p (k t) -> p k t", t=P), ACT.Copy)
                    nc.scalar.activation(m_hi[t % 2][:, KH:KO, :], pool_T[:, :, t * P:(t + 1) * P],
                                         ACT.Copy).then_inc(m_hi_ok, 1)

                mixed_high(0)
                for ko in range(KO):
                    act.wait_ge(w_in_[ko % RAW_W], 16 * (ko // RAW_W + 1))
                    nc.scalar.activation(wo_hi[:, ko, :], w_raw[ko % RAW_W][:], ACT.Copy).then_inc(wo_hi_ok, 1)
                mixed_high(1)
                for t in range(TT):
                    if t + 2 < TT:
                        mixed_high(t + 2)
                    act.wait_ge(ms2_ok, t + 1)
                    nc.scalar.activation(rms[:, t:t + 1], ms[:, t:t + 1], ACT.Sqrt).then_inc(rms_ok, 1)
                    for g in range(2):
                        act.wait_ge(xp_full, 2 * t + g + 1)
                        if t >= 2:
                            act.wait_ge(lg_full, t - 1)
                        nc.scalar.activation(hT2[t % 2][:, 4 * g:4 * g + 4, :].rearrange("p k t -> p (k t)"), xp[g][:],
                                             ACT.Copy).then_inc(xp_read, 1)

            @block.tensor
            def _(pe):
                def mixed_transposes(t):
                    if t:
                        pe.wait_ge(m_lo_ok, t)
                    for ko in range(KH):
                        ins = nc.tensor.transpose(mt[:, ko * P:(ko + 1) * P], attn[:, t, ko * P:(ko + 1) * P], k["ident"][:])
                    ins.then_inc(mt_full, 1)

                def products(t):
                    pe.wait_ge(m_lo_ok, t + 1)
                    if t >= 2:
                        pe.wait_ge(res_ok, 2 * t - 2)
                    for half in range(2):
                        for ko in range(KO):
                            if t == 0 and half == 0:
                                pe.wait_ge(wo_lo_ok, ko + 1)
                            ins = three_passes(nc, op[t % 2][half][:], [m[t % 2][:, ko, :] for m in (m_hi, m_lo)],
                                               [w[:, ko, half * HALF:(half + 1) * HALF] for w in (wo_hi, wo_lo)],
                                               ko == 0, ko == KO - 1)
                    ins.then_inc(proj_ok, 1)

                def router(t):
                    pe.wait_ge(xp_read, 2 * t + 2)
                    if t == 0:
                        pe.wait_ge(row_in, 48)
                    for ko in range(KO):
                        ins = nc.tensor.matmul(lp[:, t, :], hT2[t % 2][:, ko, :], w_r[:, ko, :],
                                               start=ko == 0, stop=ko == KO - 1)
                    ins.then_inc(lg_full, 1)

                mixed_transposes(0)
                mixed_transposes(1)
                products(0)
                for t in range(TT):
                    if t + 2 < TT:
                        mixed_transposes(t + 2)
                    if t + 1 < TT:
                        products(t + 1)
                    if t:
                        router(t - 1)
                    pe.wait_ge(h_ok, t + 1)
                    for g in range(2):
                        if t:
                            pe.wait_ge(xp_read, 2 * t + g - 1)
                        for i in range(4):
                            ins = nc.tensor.transpose(xp[g][:, i * P:(i + 1) * P],
                                                      H[t % 2][:, (4 * g + i) * P:(4 * g + i + 1) * P], k["ident"][:])
                        ins.then_inc(xp_full, 1)
                router(TT - 1)

            @block.vector
            def _(dve):
                def mixed_low(t):
                    dve.wait_ge(m_hi_ok, t + 1)
                    nc.vector.tensor_tensor(m_lo[t % 2][:, 0:KH, :], mt[:].rearrange("p (k t) -> p k t", t=P),
                                            m_hi[t % 2][:, 0:KH, :].bitcast(F32), ALU.subtract)
                    nc.vector.tensor_tensor(m_lo[t % 2][:, KH:KO, :], pool_T[:, :, t * P:(t + 1) * P],
                                            m_hi[t % 2][:, KH:KO, :].bitcast(F32), ALU.subtract).then_inc(m_lo_ok, 1)

                mixed_low(0)
                for ko in range(KO):
                    dve.wait_ge(wo_hi_ok, ko + 1)
                    nc.vector.tensor_tensor(wo_lo[:, ko, :], w_raw[ko % RAW_W][:], wo_hi[:, ko, :].bitcast(F32),
                                            ALU.subtract).then_inc(wo_lo_ok, 1)
                mixed_low(1)
                for t in range(TT):
                    x2 = X[:, t, :]
                    dve.wait_ge(proj_ok, t + 1)
                    dve.wait_ge(x_in[t], 16)
                    if t == 0:
                        dve.wait_ge(row_in, 48)
                    for half in range(2):
                        tile = x2[:, half * HALF:(half + 1) * HALF]
                        nc.vector.tensor_tensor(tile, op[t % 2][half][:], tile, ALU.add).then_inc(res_ok, 1)
                    dve.wait_ge(res_ok, 2 * t + 2)
                    if t:
                        dve.wait_ge(ms_ok, t)
                    nc.vector.scalar_tensor_tensor(junk[:], x2, 1.0 / D, x2, ALU.mult, ALU.mult,
                                                   accum_out=ms[:, t:t + 1]).then_inc(ms_ok, 1)
                    dve.wait_ge(ms_ok, t + 1)
                    nc.vector.tensor_scalar(ms[:, t:t + 1], ms[:, t:t + 1], EPS, None, ALU.add).then_inc(ms2_ok, 1)
                    if t + 2 < TT:
                        mixed_low(t + 2)
                    dve.wait_ge(rms_ok, t + 1)
                    nc.vector.reciprocal(rstd[:, t:t + 1], rms[:, t:t + 1]).then_inc(rstd_ok, 1)
                    dve.wait_ge(rstd_ok, t + 1)
                    if t >= 2:
                        dve.wait_ge(xp_full, 2 * (t - 1))
                        dve.wait_ge(h_out[t % 2], 16 * (t // 2))
                    nc.vector.scalar_tensor_tensor(H[t % 2][:], x2, rstd[:, t:t + 1], g_row[:], ALU.mult,
                                                   ALU.mult).then_inc(h_ok, 1)
                dve.wait_ge(lg_full, TT)
                nc.vector.tensor_tensor(k["logits"][:], lp[:], b_r[:, None, :].to_broadcast([P, TT, E_]), ALU.add).then_inc(lg_ok, 1)


def route(nc, k, w_gate_up, w_down, b_gate_up, b_down, raw, raw_in):
    with ExitStack() as c:
        sb = lambda n, s, d=F32: c.enter_context(nc.sbuf_tensor(n, s, d))
        ps = lambda n, s: c.enter_context(nc.psum_tensor(n, s, F32))
        sem = lambda n: c.enter_context(nc.semaphore(n))
        bias_rows = sb("bias_rows", [E_, 3 * D])
        logits = k["logits"]
        top, top_i = sb("top", [P, TT, 8]), sb("top_i", [P, TT, 8], U32)
        top_f = sb("top_f", [P, TT, K_])
        ex, den, rden = sb("ex", [P, TT, K_]), sb("den", [P, TT]), sb("rden", [P, TT])
        iota_e = sb("iota_e", [P, E_])
        block_no = sb("block_no", [P, 1])
        hot = sb("hot", [P, TT, K_, E_])
        mask = sb("mask", [P, TT, E_])
        mask_b = sb("mask_b", [P, TT, E_], BF16)
        before, ones = sb("before", [P, P], BF16), sb("ones", [P, P], BF16)
        steps = sb("steps", [P, MAX_BLOCKS_PER_EXPERT])
        over = sb("over", [P, E_, MAX_BLOCKS_PER_EXPERT])
        cnt, nb, nb_end, base = (sb(n, [P, E_]) for n in ("cnt", "nb", "nb_end", "base"))
        rank, where = sb("rank", [P, TT, E_]), sb("where", [P, TT, E_])
        picked = sb("picked", [P, TT, K_, E_])
        dest_f = sb("dest_f", [P, TT, K_])
        le, le_nb, le_cnt = sb("le", [P, E_]), sb("le_nb", [P, E_]), sb("le_cnt", [P, E_])
        be_c, done_c, row_c = sb("be_c", [P, 1]), sb("done_c", [P, 1]), sb("row_c", [P, 1])
        ones_f, diag, first_row = sb("ones_f", [P, P]), sb("diag", [P, 3, TABLE]), sb("first_row", [P, TABLE])
        rp = ps("rp", [P, TT + 1, E_])
        bp = [ps(f"bp{i}", [P, HALF]) for i in range(2)]
        tp = ps("table", [P, 3, TABLE])
        diag_ok, table_full = sem("diag_ok"), sem("table_full")
        const_ok, b_in, bias_full, bias_ok = sem("const_ok"), sem("b_in"), sem("bias_full"), sem("bias_ok")
        mask_ok, rank_full, ex_in, ex_ok, step = (sem(n) for n in ("mask_ok2", "rank_full", "ex_in", "ex_ok", "step"))

        with nc.Block() as block:

            @block.sync
            def _(sp):
                sp.dma_start(bias_rows[:, 0:2 * D], b_gate_up[0]).then_inc(b_in, 16)
                sp.dma_start(bias_rows[:, 2 * D:3 * D], b_down[0]).then_inc(b_in, 16)
                for c_ in range(RAW):
                    sp.dma_start(raw[c_][:], chunk_source(w_gate_up, w_down, c_, 0)).then_inc(raw_in[c_], 16)
                sp.wait_ge(b_in, 32)

            @block.gpsimd
            def _(pool):
                iota = lambda o, pattern, base, cm: nc.gpsimd.iota(o, pattern, base=base, channel_multiplier=cm,
                                                                   allow_small_or_imprecise_dtypes=True)
                iota(iota_e[:], [[1, E_]], 0, 0)
                iota(block_no[:], [[0, 1]], 0, 1)
                nc.gpsimd.memset(ones_f[:], 1.0)
                iota(steps[:], [[SLOTS, MAX_BLOCKS_PER_EXPERT]], 0, 0)
                iota(k["token_of"][:, :, 0], [[P, TT]], 0, 0)
                iota(k["token_of"][:, :, 1], [[0, TT]], 0, 1)
                nc.gpsimd.memset(ones[:], 1.0)
                nc.gpsimd.memset(before[:], 1.0).then_inc(const_ok, 1)
                pool.wait_ge(const_ok, 1)
                nc.gpsimd.memset(steps[:, 0:1], -1.0)
                nc.gpsimd.affine_select(out=before[:], in_=before[:], compare_op=ALU.is_gt, fill=0.0, base=0,
                                        pattern=[[1, P]], channel_multiplier=-1).then_inc(const_ok, 1)

            @block.scalar
            def _(act):
                act.wait_ge(ex_in, 1)
                nc.scalar.activation(ex[:], ex[:], ACT.Exp).then_inc(ex_ok, 1)
                act.wait_ge(bias_full, 1)
                nc.scalar.activation(k["bias_gu"][:].rearrange("p m e -> p (m e)"), bp[0][:], ACT.Copy)
                nc.scalar.activation(k["bias_dn"][:].rearrange("p m e -> p (m e)"), bp[1][:, 0:E_ * D // P],
                                     ACT.Copy).then_inc(bias_ok, 1)

            @block.tensor
            def _(pe):
                pe.wait_ge(mask_ok, 1)
                pe.wait_ge(const_ok, 2)
                for t in range(TT + 1):
                    for j in range(min(t + 1, TT)):
                        ins = nc.tensor.matmul(rp[:, t, :], before[:] if j == t else ones[:], mask_b[:, j, :],
                                               start=j == 0, stop=j == min(t, TT - 1))
                ins.then_inc(rank_full, 1)
                pe.wait_ge(b_in, 32)
                for m in range(3 * D // P):
                    ins = nc.tensor.transpose(bp[m // 16][:, (m % 16) * E_:(m % 16 + 1) * E_],
                                              bias_rows[:, m * P:(m + 1) * P], k["ident"][0:E_, 0:E_])
                ins.then_inc(bias_full, 1)
                pe.wait_ge(diag_ok, 1)
                nc.tensor.matmul(tp[:], ones_f[0:TABLE, :], diag[0:TABLE], start=True, stop=True).then_inc(table_full, 1)

            @block.vector
            def _(dve):
                count = [0]

                def mark(ins):
                    count[0] += 1
                    ins.then_inc(step, 1)

                def done(ins):
                    mark(ins)
                    dve.wait_ge(step, count[0])

                dve.wait_ge(const_ok, 2)
                for t in range(TT):
                    mark(nc.vector.max(top[:, t, :], logits[:, t, :]))
                dve.wait_ge(step, count[0])
                for t in range(TT):
                    mark(nc.vector.max_index(top_i[:, t, :], top[:, t, :], logits[:, t, :]))
                nc.vector.tensor_tensor(ex[:], top[:, :, 0:K_], top[:, :, 0:1].to_broadcast([P, TT, K_]),
                                        ALU.subtract).then_inc(ex_in, 1)
                dve.wait_ge(step, count[0])
                done(nc.vector.tensor_copy(top_f[:], top_i[:, :, 0:K_]))
                done(nc.vector.tensor_tensor(hot[:].rearrange("p t k e -> p (t k) e"),
                                             iota_e[:, None, :].to_broadcast([P, TT * K_, E_]),
                                             top_f[:].rearrange("p t k -> p (t k)")[:, :, None].to_broadcast([P, TT * K_, E_]),
                                             ALU.is_equal))
                done(nc.vector.tensor_reduce(mask[:], hot[:].rearrange("p t k e -> p t e k"), AX.X, ALU.add))
                nc.vector.tensor_copy(mask_b[:], mask[:]).then_inc(mask_ok, 1)
                dve.wait_ge(rank_full, 1)
                mark(nc.vector.tensor_copy(rank[:], rp[:, 0:TT, :]))
                done(nc.vector.tensor_copy(cnt[:], rp[:, TT, :]))
                mark(nc.vector.tensor_tensor_scan(base[:], cnt[:], cnt[:], 0.0, ALU.add, ALU.bypass))
                done(nc.vector.tensor_tensor(over[:], cnt[:, :, None].to_broadcast([P, E_, MAX_BLOCKS_PER_EXPERT]),
                                             steps[:, None, :].to_broadcast([P, E_, MAX_BLOCKS_PER_EXPERT]), ALU.is_gt))
                done(nc.vector.tensor_reduce(nb[:], over[:], AX.X, ALU.add))
                mark(nc.vector.tensor_tensor_scan(nb_end[:], nb[:], nb[:], 0.0, ALU.add, ALU.bypass))
                done(nc.vector.scalar_tensor_tensor(where[:], rank[:], 1.0, mask[:], ALU.add, ALU.mult))
                mark(nc.vector.tensor_scalar(k["ranks"][:], where[:], -1.0, None, ALU.add))
                mark(nc.vector.tensor_scalar(k["last_block"][:], nb_end[:, E_ - 1:E_], -1.0, None, ALU.add))
                mark(nc.vector.tensor_tensor(base[:], base[:], cnt[:], ALU.subtract))
                done(nc.vector.tensor_scalar(le[:], nb_end[:], block_no[:], None, ALU.is_le))
                mark(nc.vector.tensor_tensor(le_nb[:], le[:], nb[:], ALU.mult))
                mark(nc.vector.tensor_tensor(le_cnt[:], le[:], cnt[:], ALU.mult))
                done(nc.vector.tensor_reduce(be_c[:], le[:], AX.X, ALU.add))
                mark(nc.vector.tensor_reduce(done_c[:], le_nb[:], AX.X, ALU.add))
                mark(nc.vector.tensor_reduce(row_c[:], le_cnt[:], AX.X, ALU.add))
                done(nc.vector.tensor_scalar(be_c[:], be_c[:], float(E_ - 1), None, ALU.min))
                done(nc.vector.tensor_tensor(done_c[:], block_no[:], done_c[:], ALU.subtract))
                done(nc.vector.tensor_scalar(done_c[:], done_c[:], float(SLOTS), None, ALU.mult))
                mark(nc.vector.tensor_scalar(diag[:, 0, :], k["ident"][:, 0:TABLE], be_c[:], None, ALU.mult))
                done(nc.vector.tensor_tensor(row_c[:], row_c[:], done_c[:], ALU.add))
                mark(nc.vector.tensor_scalar(diag[:, 1, :], k["ident"][:, 0:TABLE], done_c[:], None, ALU.mult))
                nc.vector.tensor_scalar(diag[:, 2, :], k["ident"][:, 0:TABLE], row_c[:], None, ALU.mult).then_inc(diag_ok, 1)
                done(nc.vector.tensor_tensor(where[:], rank[:], base[:, None, :].to_broadcast([P, TT, E_]), ALU.add))
                for t in range(TT):
                    mark(nc.vector.tensor_tensor(picked[:, t], hot[:, t], where[:, t, None, :].to_broadcast([P, K_, E_]), ALU.mult))
                dve.wait_ge(table_full, 1)
                mark(nc.vector.tensor_copy(k["block_expert"][:], tp[:, 0, :]))
                mark(nc.vector.tensor_copy(k["block_first"][:], tp[:, 1, :]))
                done(nc.vector.tensor_copy(first_row[:], tp[:, 2, :]))
                mark(nc.vector.tensor_copy(k["block_row"][:], first_row[:]))
                mark(nc.vector.tensor_tensor(k["block_tokens"][:, 0:TABLE - 1], first_row[:, 1:TABLE],
                                             first_row[:, 0:TABLE - 1], ALU.subtract))
                done(nc.vector.tensor_reduce(dest_f[:], picked[:], AX.X, ALU.add))
                done(nc.vector.tensor_copy(k["dest"][:], dest_f[:]))
                dve.wait_ge(ex_ok, 1)
                done(nc.vector.tensor_reduce(den[:], ex[:], AX.X, ALU.add))
                done(nc.vector.reciprocal(rden[:], den[:]))
                done(nc.vector.tensor_tensor(k["gates"][:], ex[:], rden[:, :, None].to_broadcast([P, TT, K_]), ALU.mult))


def chunk_source(w_gate_up, w_down, c_, e):
    if c_ < 2 * PAIR_CHUNKS:
        col = (c_ % 2) * D + (c_ // 2) * CC
        src = w_gate_up[0, bass.ds(e, 1), :, col:col + CC]
    else:
        src = w_down[0, bass.ds(e, 1), :, (c_ - 2 * PAIR_CHUNKS) * CC:(c_ - 2 * PAIR_CHUNKS + 1) * CC]
    return src.rearrange("a (k p) n -> p (a k) n", p=P)


def experts(nc, k, w_gate_up, w_down, h_rows, y_rows, raw, raw_in):
    with ExitStack() as c:
        sb = lambda n, s, d=F32: c.enter_context(nc.sbuf_tensor(n, s, d))
        ps = lambda n, s: c.enter_context(nc.psum_tensor(n, s, F32))
        sem = lambda n: c.enter_context(nc.semaphore(n))
        w_hi = [sb(f"w_hi{i}", [P, KO, CC], F32R) for i in range(SPLIT)]
        w_lo = [sb(f"w_lo{i}", [P, KO, CC], F32R) for i in range(SPLIT)]
        rows = [sb(f"rows{i}", [n, D]) for i, n in enumerate(SEG)]
        x_s = sb("x_s", [P, KO, 2, SLOTS], F32R)
        a_s = sb("a_s", [P, KO, 2, SLOTS], F32R)
        half = [sb(f"half{i}", [P, SLOTS]) for i in range(BANKS)]
        gate = [sb(f"gate{i}", [P, MC, SLOTS]) for i in range(2)]
        sig = [sb(f"sig{i}", [P, MC, SLOTS]) for i in range(2)]
        up = [sb(f"up{i}", [P, MC, SLOTS]) for i in range(2)]
        glu = [sb(f"glu{i}", [P, MC, SLOTS]) for i in range(2)]
        y_col = [sb(f"y_col{i}", [P, MC, SLOTS]) for i in range(2)]
        y_st = [sb(f"y_st{i}", [n, D]) for i, n in enumerate(SEG)]
        rank_cur = sb("rank_cur", [P, TT], BF16)
        slot_no = sb("slot_no", [P, SLOTS], BF16)
        hot = sb("hot_slot", [P, TT, SLOTS], BF16)
        idx = sb("idx", [P, 2], I32)
        b_gu, b_dn = sb("b_gu", [P, 2 * D // P]), sb("b_dn", [P, D // P])
        mm = [ps(f"mm{i}", [P, 2, SLOTS]) for i in range(BANKS)]
        xt = [ps(f"xt{i}", [P, HALF]) for i in range(3)]
        yt = ps("yt", [P, 2, CC])
        LIST = HALF - 8

        hi_done, lo_done, mm_done = sem("hi_done"), sem("lo_done"), sem("mm_done")
        half_ok, sum_ok = sem("half_ok"), sem("sum_ok3")
        gate_ok, up_ok, sig_ok, pre_ok, glu_ok, a_hi_ok, a_lo_ok = (
            sem(n) for n in ("gate_ok", "up_ok", "sig_ok2", "pre_ok", "glu_ok", "a_hi_ok", "a_lo_ok"))
        slot_ok, rank_ok, hot_ok, list_full, idx_ok, rows_in = (
            sem(n) for n in ("slot_ok", "rank_ok", "hot_ok", "list_full", "idx_ok", "rows_in"))
        xt_full, x_hi_ok, x_lo_ok = sem("xt_full"), sem("x_hi_ok"), sem("x_lo_ok")
        b_gu_ok, b_dn_ok = sem("b_gu_ok"), sem("b_dn_ok")
        yt_full, yt_read, y_out, y_free = (sem(n) for n in ("yt_full", "yt_read", "y_out", "y_free"))
        pool_turn, mm_clear = sem("pool_turn2"), sem("mm_clear")
        AHEAD = SPLIT - 1
        PC = PAIR_CHUNKS
        TILES = CHUNKS * MC
        MM_AHEAD = SPLIT * MC
        SUM_AHEAD = BANKS
        YT_AHEAD = 3

        def last_block(eng):
            return eng.value_load(k["last_block"][0:1, 0:1], min_val=E_ - 1, max_val=MAX_BLOCKS - 1)

        with nc.Block() as block:

            @block.sync
            def _(sp):
                final = last_block(sp)

                def load(c_, e, turn):
                    sp.wait_ge(hi_done, turn)
                    sp.wait_ge(lo_done, turn)
                    sp.dma_start(raw[c_ % RAW][:], chunk_source(w_gate_up, w_down, c_, e)).then_inc(raw_in[c_ % RAW], 16)

                def expert_of(b):
                    return sp.value_load(k["block_expert"][0:1, bass.ds(b, 1)], min_val=0, max_val=E_ - 1)

                with sp.Fori(0, final) as b:
                    e = expert_of(b)
                    for c_ in range(RAW, CHUNKS):
                        load(c_, e, CHUNKS * b + c_ - RAW + 1)
                    e = expert_of(b + 1)
                    for c_ in range(RAW):
                        load(c_, e, CHUNKS * b + CHUNKS + c_ - RAW + 1)
                e = expert_of(final)
                for c_ in range(RAW, CHUNKS):
                    load(c_, e, CHUNKS * final + c_ - RAW + 1)

            @block.gpsimd
            def _(pool):
                final = last_block(pool)

                def until(semaphore, value):
                    pool.wait_ge(semaphore, value)
                    pool.sem_inc(pool_turn, 1)

                def expert_of(b):
                    return pool.value_load(k["block_expert"][0:1, bass.ds(b, 1)], min_val=0, max_val=E_ - 1)

                def ranks(e, b):
                    nc.gpsimd.tensor_tensor(rank_cur[:], k["ranks"][:, :, bass.ds(e, 1)].rearrange("p t a -> p (t a)"),
                                            k["block_first"][:, bass.ds(b, 1)].to_broadcast([P, TT]),
                                            ALU.subtract).then_inc(rank_ok, 1)

                def gather(turn):
                    until(idx_ok, turn)
                    for s, n in enumerate(SEG):
                        nc.gpsimd.indirect_dma_start(
                            out=rows[s][:], out_offset=None, in_=h_rows,
                            in_offset=bass.IndirectOffsetOnAxis(ap=idx[0:n, s:s + 1], axis=0)).then_inc(rows_in, 16)

                def bias_gu(e):
                    nc.gpsimd.tensor_copy(b_gu[:], k["bias_gu"][:, :, bass.ds(e, 1)].rearrange("p m a -> p (m a)")).then_inc(b_gu_ok, 1)

                nc.gpsimd.iota(slot_no[:], [[1, SLOTS]], base=0, channel_multiplier=0,
                               allow_small_or_imprecise_dtypes=True).then_inc(slot_ok, 1)
                pool.sem_inc(y_free, 1)
                e = expert_of(0)
                ranks(e, 0)
                bias_gu(e)
                gather(1)
                ranks(expert_of(1), 1)

                def product(b, j):
                    until(sig_ok, PC * b + j + 1)
                    nc.gpsimd.tensor_tensor(sig[j % 2][:], gate[j % 2][:], sig[j % 2][:], ALU.mult).then_inc(pre_ok, 1)

                def head(b):
                    e = expert_of(b)
                    until(sum_ok, SUM_AHEAD + TILES * b)
                    nc.gpsimd.tensor_copy(b_dn[:], k["bias_dn"][:, :, bass.ds(e, 1)].rearrange("p m a -> p (m a)")).then_inc(b_dn_ok, 1)
                    product(b, 0)

                def body(b, last):
                    for j in range(1, PC):
                        product(b, j)
                        if j == 1 and not last:
                            gather(b + 2)
                            until(hot_ok, b + 2)
                            ranks(expert_of(b + 2), b + 2)
                    if not last:
                        until(sum_ok, SUM_AHEAD + TILES * b + 2 * PC * MC)
                        bias_gu(expert_of(b + 1))
                    row = pool.value_load(k["block_row"][0:1, bass.ds(b, 1)], min_val=0, max_val=T * K_)
                    until(yt_read, PC * b + PC)
                    for s, n in enumerate(SEG):
                        pool.dma_start(y_rows[bass.ds(row + s * P, n), :], y_st[s][:]).then_inc(y_out, 16)
                    if not last:
                        head(b + 1)
                    until(y_out, 32 * b + 32)
                    pool.sem_inc(y_free, 1)

                head(0)
                with pool.Fori(0, final) as b:
                    body(b, False)
                body(final, True)

            @block.scalar
            def _(act):
                final = last_block(act)

                def hi(b, c_, first=False):
                    act.wait_ge(raw_in[c_ % RAW], 16 * (CHUNKS // RAW * b + c_ // RAW + 1))
                    if not first:
                        act.wait_ge(mm_done, TILES * b + MC * c_ + MM_AHEAD - (SPLIT - 1) * MC)
                    nc.scalar.activation(w_hi[c_ % SPLIT][:], raw[c_ % RAW][:], ACT.Copy).then_inc(hi_done, 1)

                def x_high(turn):
                    ko = 0
                    for g, n in enumerate(XG):
                        act.wait_ge(xt_full, len(XG) * turn + g + 1)
                        nc.scalar.activation(x_s[:, ko:ko + n, 0, :], xt[g][:, 0:n * SLOTS].rearrange("p (k t) -> p k t", k=n),
                                             ACT.Copy).then_inc(x_hi_ok, 1)
                        ko += n

                def a_high(b, j):
                    act.wait_ge(glu_ok, PC * b + j + 1)
                    nc.scalar.activation(a_s[:, MC * j:MC * j + MC, 0, :], glu[j % 2][:], ACT.Copy).then_inc(a_hi_ok, 1)

                def halves(b, c_):
                    if c_ == 0:
                        act.wait_ge(b_gu_ok, b + 1)
                    if c_ == 2 * PC:
                        act.wait_ge(b_dn_ok, b + 1)
                    for m in range(MC):
                        if c_ < 2 * PC:
                            col = (c_ % 2) * (D // P) + MC * (c_ // 2) + m
                            bias = b_gu[:, col:col + 1]
                        else:
                            col = MC * (c_ - 2 * PC) + m
                            bias = b_dn[:, col:col + 1]
                        t = MC * c_ + m
                        act.wait_ge(mm_done, TILES * b + MM_AHEAD + t + 1)
                        act.wait_ge(sum_ok, TILES * b + SUM_AHEAD + t - BANKS + 1)
                        nc.scalar.activation(half[t % BANKS][:], mm[t % BANKS][:, 1, :], ACT.Identity,
                                             bias=bias).then_inc(half_ok, 1)

                def y_rows_out(b, q):
                    act.wait_ge(yt_full, YT_AHEAD + PC * b + q + 1)
                    if q == 0:
                        act.wait_ge(y_free, b + 1)
                    for s, n in enumerate(SEG):
                        ins = nc.scalar.activation(y_st[s][:, q * CC:(q + 1) * CC], yt[0:n, s, :], ACT.Copy)
                    ins.then_inc(yt_read, 1)

                hi(0, 0, True)
                hi(0, 1, True)
                x_high(0)
                for c_ in range(2, SPLIT):
                    hi(0, c_, True)
                halves(0, 0)

                def body(b, last):
                    for c_ in range(1, CHUNKS + 1):
                        nb, nc_ = (b + 1, c_ - CHUNKS) if c_ == CHUNKS else (b, c_)
                        if c_ + AHEAD < CHUNKS:
                            hi(b, c_ + AHEAD)
                        elif not last:
                            hi(b + 1, c_ + AHEAD - CHUNKS)
                        j = c_ // 2
                        if c_ < 2 * PC and c_ % 2 == 1:
                            act.wait_ge(gate_ok, PC * b + j + 1)
                            nc.scalar.activation(sig[j % 2][:], gate[j % 2][:], ACT.Sigmoid, scale=ALPHA).then_inc(sig_ok, 1)
                            if j:
                                a_high(b, j - 1)
                        if c_ > 2 * PC + 1:
                            y_rows_out(b, c_ - 2 * PC - 2)
                        if c_ < CHUNKS or not last:
                            halves(nb, nc_)
                        if c_ == 2 * PC - 1:
                            a_high(b, PC - 1)
                        if c_ == 2 * PC + 1 and not last:
                            x_high(b + 1)
                    y_rows_out(b, PC - 1)

                with act.Fori(0, final) as b:
                    body(b, False)
                body(final, True)

            @block.vector
            def _(dve):
                final = last_block(dve)
                dve.sem_inc(sum_ok, SUM_AHEAD)

                def lo(b, c_, first=False):
                    dve.wait_ge(hi_done, CHUNKS * b + c_ + 1)
                    if not first:
                        dve.wait_ge(mm_done, TILES * b + MC * c_ + MM_AHEAD - (SPLIT - 1) * MC)
                    nc.vector.tensor_tensor(w_lo[c_ % SPLIT][:], raw[c_ % RAW][:], w_hi[c_ % SPLIT][:].bitcast(F32),
                                            ALU.subtract).then_inc(lo_done, 1)

                def one_hot(turn):
                    dve.wait_ge(rank_ok, turn)
                    nc.vector.tensor_tensor(hot[:], slot_no[:, None, :].to_broadcast([P, TT, SLOTS]),
                                            rank_cur[:, :, None].to_broadcast([P, TT, SLOTS]), ALU.is_equal).then_inc(hot_ok, 1)

                def indices(turn):
                    dve.wait_ge(list_full, turn)
                    with nc.allow_low_precision(reason="whole numbers below 1024"):
                        for s, n in enumerate(SEG):
                            ins = nc.vector.tensor_reduce(idx[0:n, s:s + 1], xt[2][0:n, LIST + 2 * s:LIST + 2 * s + 2],
                                                          AX.X, ALU.add)
                    ins.then_inc(idx_ok, 1)

                def x_low(turn):
                    ko = 0
                    for g, n in enumerate(XG):
                        dve.wait_ge(x_hi_ok, len(XG) * turn + g + 1)
                        nc.vector.tensor_tensor(x_s[:, ko:ko + n, 1, :], xt[g][:, 0:n * SLOTS].rearrange("p (k t) -> p k t", k=n),
                                                x_s[:, ko:ko + n, 0, :].bitcast(F32), ALU.subtract).then_inc(x_lo_ok, 1)
                        ko += n

                def swiglu(b, j):
                    dve.wait_ge(up_ok, PC * b + j + 1)
                    dve.wait_ge(pre_ok, PC * b + j + 1)
                    nc.vector.scalar_tensor_tensor(glu[j % 2][:], up[j % 2][:], 1.0, sig[j % 2][:], ALU.add,
                                                   ALU.mult).then_inc(glu_ok, 1)

                def a_low(b, j):
                    dve.wait_ge(a_hi_ok, PC * b + j + 1)
                    nc.vector.tensor_tensor(a_s[:, MC * j:MC * j + MC, 1, :], glu[j % 2][:],
                                            a_s[:, MC * j:MC * j + MC, 0, :].bitcast(F32), ALU.subtract).then_inc(a_lo_ok, 1)

                def sums(b, c_):
                    j = c_ // 2
                    down = c_ >= 2 * PC
                    dst = y_col[c_ % 2] if down else (gate, up)[c_ % 2][j % 2]
                    if down:
                        dve.wait_ge(yt_full, YT_AHEAD + PC * b + c_ - 2 * PC - 1)
                    for m in range(MC):
                        t = MC * c_ + m
                        dve.wait_ge(half_ok, TILES * b + t + 1)
                        nc.vector.tensor_tensor(dst[:, m, :], mm[t % BANKS][:, 0, :], half[t % BANKS][:],
                                                ALU.add).then_inc(sum_ok, 1)
                    if not down:
                        dve.wait_ge(sum_ok, TILES * b + SUM_AHEAD + MC * (c_ + 1))
                        if c_ % 2 == 0:
                            nc.vector.tensor_scalar(dst[:], dst[:], LIMIT, None, ALU.min).then_inc(gate_ok, 1)
                        else:
                            nc.vector.tensor_scalar(dst[:], dst[:], LIMIT, -LIMIT, ALU.min, ALU.max).then_inc(up_ok, 1)

                dve.wait_ge(slot_ok, 1)
                one_hot(1)
                indices(1)
                for i in range(BANKS):
                    ins = nc.vector.memset(mm[i][:], 0.0)
                ins.then_inc(mm_clear, 1)
                lo(0, 0, True)
                lo(0, 1, True)
                x_low(0)
                one_hot(2)
                for c_ in range(2, SPLIT):
                    lo(0, c_, True)
                sums(0, 0)

                def body(b, last):
                    for c_ in range(1, CHUNKS + 1):
                        if c_ + AHEAD < CHUNKS:
                            lo(b, c_ + AHEAD)
                        elif not last:
                            lo(b + 1, c_ + AHEAD - CHUNKS)
                        j = c_ // 2
                        if c_ < 2 * PC and c_ % 2 == 1 and j:
                            a_low(b, j - 1)
                        if c_ < CHUNKS:
                            sums(b, c_)
                        elif not last:
                            sums(b + 1, 0)
                        if c_ < 2 * PC and c_ % 2 == 0:
                            swiglu(b, j - 1)
                        if c_ == 2 * PC - 1:
                            swiglu(b, PC - 1)
                            a_low(b, PC - 1)
                        if c_ == 2 * PC + 1 and not last:
                            x_low(b + 1)
                        if not last:
                            if c_ == 3:
                                indices(b + 2)
                            if c_ == 2 * PC + 3:
                                one_hot(b + 3)

                with dve.Fori(0, final) as b:
                    body(b, False)
                body(final, True)

            @block.tensor
            def _(pe):
                final = last_block(pe)
                pe.sem_inc(mm_done, MM_AHEAD)
                pe.sem_inc(yt_full, YT_AHEAD)

                def token_list(turn):
                    pe.wait_ge(hot_ok, turn)
                    for s, n in enumerate(SEG):
                        for t in range(TT):
                            ins = nc.tensor.matmul(xt[2][0:n, LIST + 2 * s:LIST + 2 * s + 2], hot[:, t, s * P:s * P + n],
                                                   k["token_of"][:, t, :], start=t == 0, stop=t == TT - 1)
                    ins.then_inc(list_full, 1)

                def x_transposes(turn):
                    pe.wait_ge(rows_in, 32 * turn + 32)
                    ko = 0
                    for g, n in enumerate(XG):
                        for i in range(n):
                            for s, rows_n in enumerate(SEG):
                                ins = nc.tensor.transpose(xt[g][:, i * SLOTS + s * P:i * SLOTS + s * P + rows_n],
                                                          rows[s][:, (ko + i) * P:(ko + i + 1) * P],
                                                          k["ident"][0:rows_n, 0:rows_n])
                        ins.then_inc(xt_full, 1)
                        ko += n

                def y_transposes(b, q):
                    pe.wait_ge(sum_ok, TILES * b + SUM_AHEAD + MC * (2 * PC + q + 1))
                    if q:
                        pe.wait_ge(yt_read, PC * b + q)
                    for s, n in enumerate(SEG):
                        for m in range(MC):
                            ins = nc.tensor.transpose(yt[0:n, s, m * P:(m + 1) * P], y_col[q % 2][:, m, s * P:s * P + n],
                                                      k["ident"][:])
                    ins.then_inc(yt_full, 1)

                def tiles(b, c_, part, width):
                    in_s = a_s if c_ >= 2 * PC else x_s
                    hi_, lo_ = w_hi[c_ % SPLIT], w_lo[c_ % SPLIT]
                    if part[0] == 0:
                        pe.wait_ge(lo_done, CHUNKS * b + c_ + 1)
                    for m in range(MC):
                        t = MC * c_ + m
                        if part[0] == 0:
                            pe.wait_ge(sum_ok, TILES * b + SUM_AHEAD + t - BANKS + 1)
                        for ko in part:
                            nc.tensor.matmul(mm[t % BANKS][:, :, 0:width], hi_[:, ko, m * P:(m + 1) * P],
                                             in_s[:, ko, :, 0:width], start=ko == 0, stop=False)
                            ins = nc.tensor.matmul(mm[t % BANKS][:, 0, 0:width], lo_[:, ko, m * P:(m + 1) * P],
                                                   in_s[:, ko, 0, 0:width], start=False, stop=ko == KO - 1)
                        if part[-1] == KO - 1:
                            ins.then_inc(mm_done, 1)

                def chunk(b, c_, width=SLOTS):
                    tiles(b, c_, range(KO), width)

                def first_down_chunks(b, width):
                    early, late, newest = range(KO - 2 * MC), range(KO - 2 * MC, KO - MC), range(KO - MC, KO)
                    for c_, part in ((2 * PC, early), (2 * PC, late), (2 * PC + 1, range(KO - MC)),
                                     (2 * PC, newest), (2 * PC + 1, newest)):
                        pe.wait_ge(a_lo_ok, PC * b + part[-1] // MC + 1)
                        tiles(b, c_, part, width)

                token_list(1)
                x_transposes(0)
                pe.wait_ge(mm_clear, 1)
                pe.wait_ge(x_lo_ok, len(XG))
                chunk(0, 0)

                def chunks(b, last, width):
                    for c_ in range(1, CHUNKS):
                        if c_ == 2 * PC:
                            first_down_chunks(b, width)
                        elif c_ != 2 * PC + 1:
                            chunk(b, c_, width)
                        if c_ == 2 and not last:
                            token_list(b + 2)
                        if c_ == 2 * PC + 1 and not last:
                            x_transposes(b + 1)
                        if c_ > 2 * PC:
                            y_transposes(b, c_ - 2 * PC - 1)

                def body(b, last):
                    tokens = pe.value_load(k["block_tokens"][0:1, bass.ds(b, 1)], min_val=0, max_val=SLOTS)
                    with pe.If(tokens > WIDTHS[1]):
                        chunks(b, last, WIDTHS[2])
                    with pe.Else():
                        with pe.If(tokens > WIDTHS[0]):
                            chunks(b, last, WIDTHS[1])
                        with pe.Else():
                            chunks(b, last, WIDTHS[0])
                    if not last:
                        pe.wait_ge(x_lo_ok, len(XG) * b + 2 * len(XG))
                        chunk(b + 1, 0)
                    y_transposes(b, PC - 1)

                with pe.Fori(0, final) as b:
                    body(b, False)
                body(final, True)


def combine(nc, k, g_final, y_rows, out_tiles):
    with ExitStack() as c:
        sb = lambda n, s, d=F32: c.enter_context(nc.sbuf_tensor(n, s, d))
        sem = lambda n: c.enter_context(nc.semaphore(n))
        RING = 6
        EARLY = TT - 2
        X = k["x2"]
        Y = [sb(f"Y{i}", [P, K_, D]) for i in range(RING)]
        junk, g_row = sb("junk3", [P, D]), sb("g_row3", [P, D])
        ms, rms, rstd = sb("ms3", [P, TT]), sb("rms3", [P, TT]), sb("rstd3", [P, TT])
        g_in, out_done = sem("g_in3"), sem("out_done")
        y_in = [sem(f"y_in{i}") for i in range(RING)]
        x_scaled = sem("x_scaled3")
        y_used, acc, x_ok, ms_ok, ms2_ok, rms_ok, rstd_ok, out_ok = (
            sem(n) for n in ("y_used", "acc3", "x_ok3", "ms_ok3", "ms2_ok3", "rms_ok3", "rstd_ok3", "out_ok3"))

        with nc.Block() as block:

            @block.sync
            def _(sp):
                sp.dma_start(g_row[:], g_final.rearrange("(a d) -> a d", a=1).to_broadcast([P, D])).then_inc(g_in, 16)
                for t in range(TT):
                    sp.wait_ge(out_ok, t + 1)
                    sp.dma_start(out_tiles[:, t, :], X[:, t, :]).then_inc(out_done, 16)
                sp.wait_ge(out_done, 16 * TT)

            @block.gpsimd
            def _(pool):
                def gains(t):
                    pool.wait_ge(x_scaled, t + 1)
                    nc.gpsimd.tensor_tensor(X[:, t, :], X[:, t, :], g_row[:], ALU.mult).then_inc(out_ok, 1)

                for t in range(TT):
                    if t == RING:
                        pool.wait_ge(g_in, 16)
                    if t >= RING:
                        pool.wait_ge(y_used, t - RING + 1)
                    for i in range(K_):
                        nc.gpsimd.indirect_dma_start(
                            out=Y[t % RING][:, i, :], out_offset=None, in_=y_rows[0:T * K_, :],
                            in_offset=bass.IndirectOffsetOnAxis(ap=k["dest"][:, t, i:i + 1], axis=0)).then_inc(y_in[t % RING], 16)
                for t in range(EARLY):
                    gains(t)

            @block.scalar
            def _(act):
                for t in range(TT):
                    act.wait_ge(x_ok, t + 1)
                    if t:
                        act.wait_ge(ms_ok, t)
                    nc.scalar.activation(junk[:], X[:, t, :], ACT.Square, scale=D ** -0.5,
                                         accum_out=ms[:, t:t + 1]).then_inc(ms_ok, 1)
                    act.wait_ge(ms2_ok, t + 1)
                    nc.scalar.activation(rms[:, t:t + 1], ms[:, t:t + 1], ACT.Sqrt).then_inc(rms_ok, 1)
                    if t < EARLY:
                        act.wait_ge(rstd_ok, t + 1)
                        nc.scalar.activation(X[:, t, :], X[:, t, :], ACT.Copy, scale=rstd[:, t:t + 1]).then_inc(x_scaled, 1)

            @block.vector
            def _(dve):
                def gated_sum(t):
                    dve.wait_ge(y_in[t % RING], 16 * K_ * (t // RING + 1))
                    for i in range(K_):
                        ins = nc.vector.scalar_tensor_tensor(X[:, t, :], Y[t % RING][:, i, :], k["gates"][:, t, i:i + 1],
                                                             X[:, t, :], ALU.mult, ALU.add)
                        if i < K_ - 1:
                            ins.then_inc(acc, 1)
                            dve.wait_ge(acc, (K_ - 1) * t + i + 1)
                    ins.then_inc(x_ok, 1)
                    if t + RING < TT:
                        dve.wait_ge(x_ok, t + 1)
                        dve.sem_inc(y_used, 1)

                def normalize(t):
                    dve.wait_ge(ms_ok, t + 1)
                    nc.vector.tensor_scalar(ms[:, t:t + 1], ms[:, t:t + 1], EPS, None, ALU.add).then_inc(ms2_ok, 1)
                    dve.wait_ge(rms_ok, t + 1)
                    nc.vector.reciprocal(rstd[:, t:t + 1], rms[:, t:t + 1]).then_inc(rstd_ok, 1)
                    if t >= EARLY:
                        dve.wait_ge(rstd_ok, t + 1)
                        if t == EARLY:
                            dve.wait_ge(out_ok, EARLY)
                        nc.vector.scalar_tensor_tensor(X[:, t, :], X[:, t, :], rstd[:, t:t + 1], g_row[:], ALU.mult,
                                                       ALU.mult).then_inc(out_ok, 1)

                dve.wait_ge(g_in, 16)
                gated_sum(0)
                for t in range(1, TT):
                    gated_sum(t)
                    normalize(t - 1)
                normalize(TT - 1)


_INS = ["x", "g_mix", "w_in", "pool_w", "pool_scale", "w_out", "g_moe", "w_router", "b_router",
        "w_gate_up", "b_gate_up", "w_down", "b_down", "g_final"]


def kernel(**inputs):
    import numpy as np
    import concourse.bacc as bacc
    from concourse.bass_utils import run_bass_kernel_spmd

    nc = bacc.Bacc("TRN2", target_bir_lowering=False, num_devices=1)
    arrays, args = {}, []
    for name in _INS:
        a = np.ascontiguousarray(inputs[name])
        arrays[f"in_{name}"] = a
        args.append(nc.dram_tensor(f"in_{name}", a.shape, mybir.dt.from_np(a.dtype), kind="ExternalInput").ap())
    out = nc.dram_tensor("out_0", (1, T, D), F32, kind="ExternalOutput").ap()
    hybrid_moe_kernel(nc, *args, out)
    r = run_bass_kernel_spmd(nc, [arrays], core_ids=[0])
    return r.results[0]["out_0"]
```
